# Optimizing a Trainium2 kernel written in Bass

```python
import jax
import jax.numpy as jnp
from jax import lax
import numpy as np

D_MODEL = 2048
BATCH = 1
SEQ = 512
DEPTH = 1

CHUNK = 64
WINDOW = 128
WIN_CHUNKS = WINDOW // CHUNK
HEAD_DIM = 64
ATTN_WIDTH = D_MODEL // 2
N_Q_HEADS = ATTN_WIDTH // HEAD_DIM
N_KV_HEADS = 2
Q_PER_KV = N_Q_HEADS // N_KV_HEADS
KV_WIDTH = N_KV_HEADS * HEAD_DIM
POOL_WIDTH = D_MODEL - ATTN_WIDTH
POOL_WINDOWS = (2, 4, 8, 16)
N_POOL_GROUPS = len(POOL_WINDOWS)
POOL_GROUP = POOL_WIDTH // N_POOL_GROUPS
MIX_WIDTH = ATTN_WIDTH + POOL_WIDTH
MIX_IN = ATTN_WIDTH + 2 * KV_WIDTH + POOL_WIDTH
N_MEM = 256
X_HEADS = 4
X_HEAD_DIM = 128
X_WIDTH = X_HEADS * X_HEAD_DIM
N_GROUPS = 4
EXPERTS_PER_GROUP = 8
N_EXPERTS = N_GROUPS * EXPERTS_PER_GROUP
TOP_K = 2
D_FF_EXPERT = D_MODEL // 4
MOE_BLOCK = 128
EPS = 1e-6
NEG_INF = -1e30

kernel_name = "hybrid_swa_pool_memxattn_hmoe"

def rmsnorm(x, g):
    x32 = x.astype(jnp.float32)
    y = x32 * lax.rsqrt(jnp.mean(x32 * x32, axis=-1, keepdims=True) + EPS)
    return (y * g.astype(jnp.float32)).astype(x.dtype)

def alibi_slopes(n):
    return 2.0 ** (-8.0 * jnp.arange(1, n + 1, dtype=jnp.float32) / n)

def chunk_shift(t, n):
    if n == 0:
        return t
    pad = [(0, 0)] * t.ndim
    pad[1] = (n, 0)
    return jnp.pad(t, pad)[:, : t.shape[1]]

def sliding_window_attention(q, k, v, q_g, k_g, sinks):
    B, S, _ = q.shape
    nc = S // CHUNK
    q = rmsnorm(q.reshape(B, S, N_Q_HEADS, HEAD_DIM), q_g)
    k = rmsnorm(k.reshape(B, S, N_KV_HEADS, HEAD_DIM), k_g)
    v = v.reshape(B, S, N_KV_HEADS, HEAD_DIM)
    qc = q.reshape(B, nc, CHUNK, N_KV_HEADS, Q_PER_KV, HEAD_DIM)
    kc = k.reshape(B, nc, CHUNK, N_KV_HEADS, HEAD_DIM)
    vc = v.reshape(B, nc, CHUNK, N_KV_HEADS, HEAD_DIM)
    kb = jnp.concatenate([chunk_shift(kc, n) for n in range(WIN_CHUNKS - 1, -1, -1)], axis=2)
    vb = jnp.concatenate([chunk_shift(vc, n) for n in range(WIN_CHUNKS - 1, -1, -1)], axis=2)
    scores = jnp.einsum('bcqkgd,bcskd->bkgcqs', qc, kb,
                        preferred_element_type=jnp.float32) * (HEAD_DIM ** -0.5)
    i = jnp.arange(CHUNK)[:, None]
    slot = jnp.arange(WINDOW)[None, :]
    dist = jnp.abs(i + (WINDOW - CHUNK) - slot).astype(jnp.float32)
    slopes = alibi_slopes(N_Q_HEADS).reshape(N_KV_HEADS, Q_PER_KV)
    bias = -slopes[:, :, None, None] * dist
    src_chunk = jnp.arange(nc)[:, None] - (WIN_CHUNKS - 1) + slot // CHUNK
    valid = (src_chunk >= 0)[None, None, None, :, None, :]
    scores = jnp.where(valid, scores + bias[None, :, :, None], NEG_INF)
    sink = sinks.astype(jnp.float32).reshape(N_KV_HEADS, Q_PER_KV)[None, :, :, None, None, None]
    sink = jnp.broadcast_to(sink, scores.shape[:-1] + (1,))
    probs = jax.nn.softmax(jnp.concatenate([scores, sink], axis=-1), axis=-1)[..., :WINDOW]
    out = jnp.einsum('bkgcqs,bcskd->bcqkgd', probs.astype(vb.dtype), vb)
    return out.reshape(B, S, ATTN_WIDTH)

def multiscale_pool(u, pool_w, pool_scale):
    B, S, _ = u.shape
    ug = u.reshape(B, S, N_POOL_GROUPS, POOL_GROUP).astype(jnp.float32)
    cs = jnp.cumsum(ug, axis=1)
    count = jnp.arange(1, S + 1, dtype=jnp.float32)
    outs = []
    for gi, w in enumerate(POOL_WINDOWS):
        c = cs[:, :, gi]
        lag = jnp.pad(c[:, : S - w], ((0, 0), (w, 0), (0, 0)))
        mean = (c - lag) / jnp.minimum(count, float(w))[None, :, None]
        outs.append(mean - ug[:, :, gi])
    d = jnp.stack(outs, axis=2).astype(u.dtype)
    y = jnp.einsum('bsgc,gce->bsge', d, pool_w)
    return y.reshape(B, S, POOL_WIDTH) * pool_scale

def memory_cross_attention(h, mem_n, xq_w, xkv_w, xq_g, xk_g, xo_w):
    B, S, _ = h.shape
    M = mem_n.shape[1]
    q = rmsnorm((h @ xq_w).reshape(B, S, X_HEADS, X_HEAD_DIM), xq_g)
    k, v = jnp.split(mem_n @ xkv_w, 2, axis=-1)
    k = rmsnorm(k.reshape(B, M, X_HEADS, X_HEAD_DIM), xk_g)
    v = v.reshape(B, M, X_HEADS, X_HEAD_DIM)
    s = jnp.einsum('bqhd,bmhd->bhqm', q, k, preferred_element_type=jnp.float32) * (X_HEAD_DIM ** -0.5)
    p = jax.nn.softmax(s, axis=-1).astype(v.dtype)
    o = jnp.einsum('bhqm,bmhd->bqhd', p, v).reshape(B, S, X_WIDTH)
    return o @ xo_w

def hierarchical_moe(h, rg_w, rg_b, re_w, re_b, w_gate, w_up, w_down):
    B, S, D = h.shape
    T = B * S
    ht = h.reshape(T, D)
    g_logits = (ht @ rg_w).astype(jnp.float32) + rg_b.astype(jnp.float32)
    g_prob = jax.nn.softmax(g_logits, axis=-1)
    g_sel = jnp.argmax(g_logits, axis=-1)
    g_gate = jnp.take_along_axis(g_prob, g_sel[:, None], axis=-1)
    e_all = jnp.einsum('td,gde->tge', ht, re_w).astype(jnp.float32) + re_b.astype(jnp.float32)
    e_logits = jnp.take_along_axis(e_all, g_sel[:, None, None], axis=1)[:, 0]
    top_v, top_i = lax.top_k(e_logits, TOP_K)
    gate = g_gate * jax.nn.softmax(top_v, axis=-1)
    eid = g_sel[:, None] * EXPERTS_PER_GROUP + top_i
    A = T * TOP_K
    eid_f = eid.reshape(A).astype(jnp.int32)
    tok_f = jnp.repeat(jnp.arange(T, dtype=jnp.int32), TOP_K)
    gate_f = gate.reshape(A)
    order = jnp.argsort(eid_f)
    eid_s, tok_s, gate_s = eid_f[order], tok_f[order], gate_f[order]
    counts = jnp.bincount(eid_f, length=N_EXPERTS).astype(jnp.int32)
    start = jnp.cumsum(counts) - counts
    padded = (counts + MOE_BLOCK - 1) // MOE_BLOCK * MOE_BLOCK
    pad_end = jnp.cumsum(padded)
    pad_start = pad_end - padded
    dest = pad_start[eid_s] + (jnp.arange(A, dtype=jnp.int32) - start[eid_s])
    P = A + N_EXPERTS * MOE_BLOCK
    n_blocks = P // MOE_BLOCK
    slot_tok = jnp.zeros((P,), jnp.int32).at[dest].set(tok_s)
    slot_gate = jnp.zeros((P,), gate_s.dtype).at[dest].set(gate_s)
    blk_start = jnp.arange(n_blocks, dtype=jnp.int32) * MOE_BLOCK
    blk_expert = jnp.minimum(jnp.searchsorted(pad_end, blk_start, side='right'), N_EXPERTS - 1)
    xs = ht[slot_tok].reshape(n_blocks, MOE_BLOCK, D)

    def expert_block(args):
        xb, e = args
        return (jax.nn.silu(xb @ w_gate[e]) * (xb @ w_up[e])) @ w_down[e]

    ys = lax.map(expert_block, (xs, blk_expert)).reshape(P, D)
    ys = ys * slot_gate[:, None].astype(ys.dtype)
    out = jax.ops.segment_sum(ys, slot_tok, num_segments=T)
    return out.reshape(B, S, D)

def setup_inputs(seed: int = 0) -> dict:
    key = jax.random.key(seed)
    ks = jax.random.split(key, 25)
    f32 = jnp.float32
    nrm = lambda k, shape, scale: jax.random.normal(k, shape, f32) * scale
    gain = lambda k, shape: 1.0 + 0.02 * jax.random.normal(k, shape, f32)
    L = DEPTH
    return {
        "x": nrm(ks[0], (BATCH, SEQ, D_MODEL), 1.0),
        "mem": nrm(ks[1], (BATCH, N_MEM, D_MODEL), 1.0),
        "mix_norm_g": gain(ks[2], (L, D_MODEL)),
        "w_in": nrm(ks[3], (L, D_MODEL, MIX_IN), D_MODEL ** -0.5),
        "q_norm_g": gain(ks[4], (L, HEAD_DIM)),
        "k_norm_g": gain(ks[5], (L, HEAD_DIM)),
        "sink_logits": nrm(ks[6], (L, N_Q_HEADS), 0.5),
        "pool_w": nrm(ks[7], (L, N_POOL_GROUPS, POOL_GROUP, POOL_GROUP), POOL_GROUP ** -0.5),
        "pool_scale": gain(ks[8], (L, POOL_WIDTH)),
        "w_out": nrm(ks[9], (L, MIX_WIDTH, D_MODEL), MIX_WIDTH ** -0.5),
        "xattn_norm_g": gain(ks[10], (L, D_MODEL)),
        "mem_norm_g": gain(ks[11], (L, D_MODEL)),
        "xq_w": nrm(ks[12], (L, D_MODEL, X_WIDTH), D_MODEL ** -0.5),
        "xkv_w": nrm(ks[13], (L, D_MODEL, 2 * X_WIDTH), D_MODEL ** -0.5),
        "xq_norm_g": gain(ks[14], (L, X_HEAD_DIM)),
        "xk_norm_g": gain(ks[15], (L, X_HEAD_DIM)),
        "xo_w": nrm(ks[16], (L, X_WIDTH, D_MODEL), X_WIDTH ** -0.5),
        "ffn_norm_g": gain(ks[17], (L, D_MODEL)),
        "router_group_w": nrm(ks[18], (L, D_MODEL, N_GROUPS), D_MODEL ** -0.5),
        "router_group_b": nrm(ks[19], (L, N_GROUPS), 0.01),
        "router_expert_w": nrm(ks[20], (L, N_GROUPS, D_MODEL, EXPERTS_PER_GROUP), D_MODEL ** -0.5),
        "router_expert_b": nrm(ks[21], (L, N_GROUPS, EXPERTS_PER_GROUP), 0.01),
        "expert_w_gate": nrm(ks[22], (L, N_EXPERTS, D_MODEL, D_FF_EXPERT), D_MODEL ** -0.5),
        "expert_w_up": nrm(ks[23], (L, N_EXPERTS, D_MODEL, D_FF_EXPERT), D_MODEL ** -0.5),
        "expert_w_down": nrm(ks[24], (L, N_EXPERTS, D_FF_EXPERT, D_MODEL), D_FF_EXPERT ** -0.5),
    }

def reference(x, mem, mix_norm_g, w_in, q_norm_g, k_norm_g, sink_logits, pool_w, pool_scale,
              w_out, xattn_norm_g, mem_norm_g, xq_w, xkv_w, xq_norm_g, xk_norm_g, xo_w,
              ffn_norm_g, router_group_w, router_group_b, router_expert_w, router_expert_b,
              expert_w_gate, expert_w_up, expert_w_down):
    for l in range(DEPTH):
        h = rmsnorm(x, mix_norm_g[l])
        proj = h @ w_in[l]
        q, k, v, u = jnp.split(proj, [ATTN_WIDTH, ATTN_WIDTH + KV_WIDTH,
                                      ATTN_WIDTH + 2 * KV_WIDTH], axis=-1)
        a = sliding_window_attention(q, k, v, q_norm_g[l], k_norm_g[l], sink_logits[l])
        p = multiscale_pool(u, pool_w[l], pool_scale[l])
        x = x + jnp.concatenate([a, p], axis=-1) @ w_out[l]
        h = rmsnorm(x, xattn_norm_g[l])
        x = x + memory_cross_attention(h, rmsnorm(mem, mem_norm_g[l]), xq_w[l], xkv_w[l],
                                       xq_norm_g[l], xk_norm_g[l], xo_w[l])
        h = rmsnorm(x, ffn_norm_g[l])
        x = x + hierarchical_moe(h, router_group_w[l], router_group_b[l], router_expert_w[l],
                                 router_expert_b[l], expert_w_gate[l], expert_w_up[l],
                                 expert_w_down[l])
    return x


_drawn_inputs = setup_inputs


def setup_inputs(seed=0):
    import zlib

    import numpy as np

    out = dict(_drawn_inputs(seed))
    spreads = {}
    factors = {'mix_norm_g': 2.712,
     'q_norm_g': 6.319,
     'k_norm_g': 8.0,
     'sink_logits': 3.421,
     'xattn_norm_g': 8.0,
     'mem_norm_g': 5.878,
     'xq_norm_g': 5.533,
     'xk_norm_g': 8.0,
     'router_group_b': 32.384,
     'router_expert_b': 47.192,
     'ffn_norm_g': 8.0}
    for name, (base, spread) in spreads.items():
        noise = np.random.default_rng([zlib.crc32(name.encode()), seed]).standard_normal(out[name].shape)
        drawn = base * np.exp(spread * noise) if base else spread * noise
        out[name] = jnp.asarray(drawn.astype(out[name].dtype))
    for name, factor in factors.items():
        out[name] = (out[name] * factor).astype(out[name].dtype)
    return out
```

```python
from contextlib import ExitStack

import concourse.bass as bass
from concourse import mybir

P = 128
F32 = mybir.dt.float32
I32 = mybir.dt.int32
U32 = mybir.dt.uint32
ALU = mybir.AluOpType
ACT = mybir.ActivationFunctionType
AX = mybir.AxisListType.X
ds = bass.ds

D = 2048
S = 512
NT = S // P
KD = D // P
HD = 64
NH = 16
CHUNK = 64
WIN = 3 * CHUNK
QKV = 1280
NCT = 18
NM = 256
XW = 512
XH = 4
XD = 128
POOLT = 8
NG, EPG = 4, 8
NE = NG * EPG
FF = 512
KF = FF // P
EPS = 1e-6
NEG = -1e30

SLOTS = 64
MORE = -(-S // SLOTS) - 1
NOVER = 2 * ((2 * S // (SLOTS + 1) + 1) // 2)
NBLK = NE + NOVER
TCOL = NBLK + 2
EMPTY = 8192
CHK = 2048
NSLOT = 12
NA = 4
NCOL = NG + NE


def hybrid_block(nc, x, mem, mix_norm_g, w_in, q_norm_g, k_norm_g, sink_logits, pool_w, pool_scale,
                 w_out, xattn_norm_g, mem_norm_g, xq_w, xkv_w, xq_norm_g, xk_norm_g, xo_w, ffn_norm_g,
                 router_group_w, router_group_b, router_expert_w, router_expert_b,
                 expert_w_gate, expert_w_up, expert_w_down, out):
    hn_dram = nc.dram_tensor("normed_rows", (S, D), F32, kind="Internal").ap()
    y_dram = nc.dram_tensor("expert_rows", (2 * S, D), F32, kind="Internal").ap()

    with ExitStack() as ctx:
        def sb(name, shape, dt=F32):
            return ctx.enter_context(nc.sbuf_tensor(name, shape, dt))

        def sem(name):
            return ctx.enter_context(nc.semaphore(name))

        ring = sb("weight_ring", [P, NSLOT * CHK])
        X = sb("residual", [P, NT, D])
        H = sb("transposed_acts", [P, KD, S])
        PB = sb("proj_buffer", [P, NCT * S])
        kx = sb("memory_keys_T", [P, XH, NM])
        vx = sb("memory_values", [P, NM // P, XW])
        ident = sb("identity", [P, P])
        ones = sb("ones", [P, P])
        blk = sb("head_blocks", [P, P])
        NGR = 4 * KD + POOLT + 4
        gT = sb("gains_T", [P, NGR])
        stat = sb("norm_stats", [P, 3, 14])
        eps = sb("eps", [P, 1])
        sink = sb("sink", [P, NH])
        rbias = sb("router_bias", [P, NCOL])
        sm = sb("softmax_stats", [P, 6, 8])
        cols = sb("slot_columns", [SLOTS, 4], I32)
        io = sb("ramp64", [P, 64])
        tok = sb("token_ids", [P, NT])
        ps = ctx.enter_context(nc.psum_tensor("ps", [P, 8, 512], F32))

        def slot(s):
            return ring[:, s * CHK:(s + 1) * CHK]

        hs = PB[:, 0:2 * D].rearrange("p (b d) -> p b d", b=2)
        proj = PB[:, :].rearrange("p (c s) -> p c s", s=S)
        qx = PB[:, 4096:6144].rearrange("p (h s) -> p h s", s=S)
        SX = PB[:, 6144:8192].rearrange("p (b n) -> p b n", b=2)
        sqx = PB[:, 6144:7168].rearrange("p (b n) -> p b n", b=2)
        rtx = PB[:, 7168:8192].rearrange("p (b n) -> p b n", b=2)
        wr = PB[:, 8192:8192 + KD * NCOL].rearrange("p (k c) -> p k c", c=NCOL)
        tri = PB[:, 8768:8896]
        tidx = PB[0:SLOTS, 8896:8896 + TCOL].bitcast(I32)
        yidx = PB[0:SLOTS, 8960:8960 + TCOL].bitcast(I32)
        gate = PB[0:SLOTS, 9024:9024 + TCOL]
        meta = PB[0:1, 9088:9088 + NOVER + 1].bitcast(I32)
        y = PB[:, 4096:8192].rearrange("p (b d) -> p b d", b=2)
        y4 = PB[:, 4096:8192].rearrange("p (b n c) -> p b n c", b=2, c=512)
        guT = ps[:, 1, :].rearrange("p (f n) -> p f n", n=P)
        Hf = H[:, :, :].rearrange("p k s -> p (k s)")
        PTX = Hf[:, 4 * S:4 * S + 1024]
        xsT = Hf[:, 0:2 * KD * SLOTS].rearrange("p (b k n) -> p b k n", b=2, n=SLOTS)
        act_t = Hf[:, 2048:2048 + KF * SLOTS]
        sil = Hf[:, 2304:2304 + KF * SLOTS]
        gu = Hf[:, 2560:2560 + FF]
        scr = ring[:, NA * CHK:NSLOT * CHK]
        memx = scr[:, 0:4096].rearrange("p (t d) -> p t d", t=2)
        memT = scr[:, 4096:8192].rearrange("p (k m) -> p k m", m=NM)
        sqm = scr[:, 8192:9216]
        rtm = scr[:, 9216:10240]
        bias = scr[:, 0:3072].rearrange("p (h n) -> p h n", n=WIN)
        Ssb = scr[:, 3072:4608].rearrange("p (h n) -> p h n", n=WIN)
        Spair = scr[:, 3072:4608].rearrange("p (j n) -> p j n", n=2 * WIN)
        PT = scr[:, 4608:6144].rearrange("p (j n) -> p j n", n=384)
        a_rows = scr[:, 6144:10240].rearrange("p (t c) -> p t c", t=NT)
        kdup = scr[:, 10240:11392].rearrange("p (g n) -> p g n", g=2)
        vA = scr[:, 11392:11904].rearrange("p (t c) -> p t c", t=NT)
        sq = scr[:, 12416:13440].rearrange("p (b n) -> p b n", b=2)
        rt = scr[:, 13440:14464].rearrange("p (b n) -> p b n", b=2)
        vB = scr[:, 13440:14464].rearrange("p (e t c) -> p e t c", e=2, t=NT)
        wsum = scr[:, 14464:15520].rearrange("p (b n) -> p b n", b=2)
        vTp = scr[:, 15520:16096]
        ramp = scr[:, 16096:16160].rearrange("p (g n) -> p g n", g=4)
        cnt16 = scr[:, 16160:16176]
        dist = sq[:, 0, 0:WIN]
        mask = sq[:, 1, 0:WIN]

        G_MIX, G_XAT, G_MEM, G_FFN = 0, KD, 2 * KD, 3 * KD
        G_POOL = 4 * KD
        G_Q, G_K, G_XQ, G_XK = (G_POOL + POOLT + j for j in range(4))

        landed = [sem(f"landed{s}") for s in range(NSLOT)]
        used = sem("chunks_used")
        mem_in = [sem("mem_in0"), sem("mem_in1")]
        x_in = sem("x_in")
        gain_in = sem("gain_in")
        small_in = sem("small_in")
        consts = sem("consts")
        eps_set = sem("eps_set")
        gain_turned = sem("gain_turned")
        gains = sem("gains")
        ssq_done = sem("ssq_done")
        root_done = sem("root_done")
        rstd_done = sem("rstd_done")
        h_ready = sem("h_ready")
        h_turned = sem("h_turned")
        hT_ready = sem("hT_ready")
        hn_stored = [sem("hn_stored0"), sem("hn_stored1")]
        xk_sq = sem("xk_sq")
        xk_ss = sem("xk_ss")
        xk_root = sem("xk_root")
        kx_ready = sem("kx_ready")
        vx_ready = sem("vx_ready")
        q_sq = sem("q_sq")
        q_ss = sem("q_ss")
        q_root = sem("q_root")
        q_ready = sem("q_ready")
        q_recip = sem("q_recip")
        k_padded = sem("k_padded")
        k_ready = sem("k_ready")
        v_copied = sem("v_copied")
        v_turned = sem("v_turned")
        v_ready = sem("v_ready")
        bias_built = sem("bias_built")
        bias_reset = sem("bias_reset")
        pool_chain = sem("pool_chain")
        ramp_in = sem("ramp_in")
        ramp_ready = sem("ramp_ready")
        scores_done = sem("scores_done")
        scores_read = sem("scores_read")
        max_done = sem("max_done")
        exp_done = sem("exp_done")
        pt_turned = sem("pt_turned")
        pt_dve = sem("pt_dve")
        pt_act = sem("pt_act")
        pv_done = sem("pv_done")
        a_ready = sem("a_ready")
        u_ready = sem("u_ready")
        d_ready = sem("d_ready")
        a_turned = sem("a_turned")
        aT_act = sem("aT_act")
        aT_dve = sem("aT_dve")
        pool_done = sem("pool_done")
        pT_ready = sem("pT_ready")
        o_done = sem("out_product_done")
        x_added = sem("x_added")
        router_in = sem("router_in")
        tri_ready = sem("tri_ready")
        xq_done = sem("xq_done")
        xq_sq = sem("xq_sq")
        xq_ss = sem("xq_ss")
        xq_root = sem("xq_root")
        qx_ready = sem("qx_ready")
        xs_done = sem("xscores_done")
        xmax_done = sem("xmax_done")
        xexp_done = sem("xexp_done")
        xp_ready = sem("xprobs_ready")
        xp_turned = sem("xprobs_turned")
        xpt_dve = sem("xpt_dve")
        xpt_act = sem("xpt_act")
        xo_part = sem("xo_part")
        oT_ready = sem("oT_ready")
        logits_done = sem("logits_done")
        gmax_done = sem("gmax_done")
        gexp_done = sem("gexp_done")
        top_done = sem("top_done")
        texp_done = sem("texp_done")
        picks = sem("picks")
        ranks = sem("ranks")
        onehots = sem("onehots")
        table_done = sem("table_done")
        table_ready = sem("table_ready")
        xs_clear = sem("xs_clear")
        idx_copied = sem("idx_copied")
        gathered = [sem("gathered0"), sem("gathered1")]
        xs_turned = sem("xs_turned")
        xsT_ready = sem("xsT_ready")
        gu_copied = sem("gu_copied")
        gu_turned = sem("gu_turned")
        sil_ready = sem("sil_ready")
        act_ready = sem("act_ready")
        y_act = sem("y_act")
        y_dve = sem("y_dve")
        scattered = [sem("scattered0"), sem("scattered1")]
        all_scattered = sem("all_scattered")
        y_in = [sem(f"y_in{t}") for t in range(NT)]
        sum_ready = sem("sum_ready")
        stored = sem("stored")
        act_link = sem("act_link")
        dve_link = sem("dve_link")
        pool_link = sem("pool_link")

        xkv_v = xkv_w[0].rearrange("(k p) n -> p k n", p=P)
        w_in_v = w_in[0].rearrange("(k p) n -> p k n", p=P)
        w_out_v = w_out[0].rearrange("(k p) n -> p k n", p=P)
        xq_v = xq_w[0].rearrange("(k p) n -> p k n", p=P)
        xo_v = xo_w[0].rearrange("(k p) n -> p k n", p=P)
        pool_v = pool_w[0].rearrange("g (k p) n -> p (g k) n", p=P)
        early = []
        for half in range(2):
            for c in range(4):
                early.append((c, xkv_v[:, 4 * c:4 * c + 4, half * XW:(half + 1) * XW], XW))
        SEQ_Q = len(early)
        for ct in range(NCT):
            early.append((ct % 4 if ct < 8 else [0, 1][ct - 8] if ct < 10 else 2 + ct % 2,
                          w_in_v[:, :, ct * P:(ct + 1) * P], P))
        SEQ_K = SEQ_Q + 8
        SEQ_U = SEQ_K + 2
        SEQ_POOL = len(early)
        early.append((0, pool_v, 256))
        SEQ_OUT = len(early)
        for n in range(4):
            for c in range(4):
                early.append((c, w_out_v[:, 4 * c:4 * c + 4, n * 512:(n + 1) * 512], 512))
        SEQ_XQ = len(early)
        for c in range(4):
            early.append((c, xq_v[:, 4 * c:4 * c + 4, :], XW))
        SEQ_XO = len(early)
        for c in range(4):
            early.append((c, xo_v[:, c:c + 1, :], D))
        UE = SEQ_XO
        loads_before = []
        for n, (s, _, _) in enumerate(early):
            loads_before.append(sum(1 for m in range(n) if early[m][0] == s))
        early_loads = [sum(1 for e in early if e[0] == s) for s in range(NSLOT)]

        def wait_past(eng, semaphore, value):
            if not isinstance(value, int) or value > 0:
                eng.wait_ge(semaphore, value)

        def chunk(n, width):
            return slot(early[n][0]).rearrange("p (k n) -> p k n", n=width)

        def chunk_landed(eng, n):
            eng.wait_ge(landed[early[n][0]], 16 * (loads_before[n] + 1))

        rq = {}

        def carve(spec):
            at = 4096
            for name, shape in spec:
                n = 1
                for v in shape:
                    n *= v
                v = PB[:, at:at + n]
                if len(shape) == 2:
                    v = v.rearrange("p (a b) -> p a b", b=shape[1])
                elif len(shape) == 3:
                    v = v.rearrange("p (a b c) -> p a b c", b=shape[1], c=shape[2])
                rq[name] = v
                at += n
            assert at <= 8192, at

        carve([("L", (NT, NCOL)), ("gm", (NT,)), ("gs", (NT, NG)), ("eg", (NT, NG)), ("gsum", (NT,)), ("gg", (NT,)),
               ("gh", (NT, NG)), ("ti", (NT,)), ("t8", (NT, EPG)), ("es", (NT, EPG)),
               ("m1", (NT,)), ("m2", (NT,)), ("h1", (NT, EPG)), ("h2", (NT, EPG)), ("dt", (NT,)), ("et", (NT,)),
               ("w1", (NT,)), ("w2", (NT,)), ("tg", (NT, NG, EPG)), ("M1", (NT, NE)), ("M2", (NT, NE)),
               ("M", (NT, NE)), ("R", (NT + 1, NE)), ("over", (NE,)), ("cmp", (NE, MORE)), ("ca", (16 + NE,)),
               ("cb", (16 + NE,)), ("base", (NE,)), ("pos", (NT,)), ("ob", (NT,)), ("ek", (NT,)), ("pc", (NT, MORE)),
               ("q", (NT,)), ("z", (NT,)), ("row", (NT,)), ("bk", (NT,)), ("cand", (NT, EPG)),
               ("fin", (2 * TCOL,)), ("tmp", (NT, NE)), ("thr", (MORE,)), ("one", (NT, TCOL)), ("val", (NT,)), ("ec", (NOVER, NE)), ("ev", (NOVER + 1,)),
               ("P1", (NT, SLOTS)), ("P2", (NT, SLOTS)), ("B1", (NT, 2 * TCOL)), ("B2", (NT, 2 * TCOL))])

        def head_at(n):
            return 8 * (n // 8) + 2 * (n % 4) + (n % 8) // 4

        WINDOW = (((0, WIN, 0),), ((0, CHUNK, P), (CHUNK, P, 0)))

        block = ctx.enter_context(nc.Block())

        gate_v = expert_w_gate[0].rearrange("e (k p) n -> e p k n", p=P)
        up_v = expert_w_up[0].rearrange("e (k p) n -> e p k n", p=P)
        down_v = expert_w_down[0].rearrange("e (k p) n -> e p k n", p=P)

        def expert_chunk(e, j):
            if j < 8:
                return (gate_v, up_v)[j % 2][ds(e, 1), :, 4 * (j // 2):4 * (j // 2) + 4, :].rearrange(
                    "e p k n -> p (e k) n")
            return down_v[ds(e, 1), :, j - 8:j - 7, :].rearrange("e p k n -> p (e k) n")

        def expert_slot(j):
            return (j + 4) % NSLOT

        @block.sync
        def _(sp):
            for t in range(2):
                sp.dma_start(memx[:, t, :], mem[0, t * P:(t + 1) * P, :]).then_inc(mem_in[t], 16)
            for n, (s, src, width) in enumerate(early):
                if n == SEQ_OUT + 4:
                    sp.wait_ge(aT_act, 4)
                    sp.wait_ge(aT_dve, 4)
                    sp.wait_ge(used, SEQ_POOL + 1)
                    sp.wait_ge(d_ready, 8)
                    for j in range(8):
                        sp.dma_start(slot(expert_slot(j)).rearrange("p (k n) -> p k n", n=FF),
                                     expert_chunk(0, j)).then_inc(landed[expert_slot(j)], 16)
                last = [m for m in range(n) if early[m][0] == s]
                if last:
                    sp.wait_ge(used, last[-1] + 1)
                sp.dma_start(slot(s).rearrange("p (k n) -> p k n", n=width), src).then_inc(landed[s], 16)
            for j in range(8, 12):
                s = expert_slot(j)
                sp.wait_ge(o_done, 28)
                sp.dma_start(slot(s).rearrange("p (k n) -> p k n", n=D), expert_chunk(0, j)).then_inc(landed[s], 16)

            def load_expert(e, b):
                for j in range(12):
                    s = expert_slot(j)
                    sp.wait_ge(used, b * 12 + (UE - 12 + j + 1))
                    sp.dma_start(slot(s).rearrange("p (k n) -> p k n", n=FF if j < 8 else D),
                                 expert_chunk(e, j)).then_inc(landed[s], 16)

            with sp.Fori(1, NE) as b:
                load_expert(b, b)
            sp.wait_ge(table_ready, 1)
            more = sp.value_load(meta[0:1, NOVER:NOVER + 1], min_val=0, max_val=NOVER)
            with sp.If(more > 0):
                with sp.Fori(0, NOVER) as j:
                    e = sp.value_load(meta[0:1, ds(j, 1)], min_val=0, max_val=NE - 1)
                    load_expert(e, j + NE)
            sp.wait_ge(all_scattered, 1)
            for t in range(NT):
                sp.dma_start(scr[:, t * 2 * D:(t + 1) * 2 * D],
                             y_dram[t * 2 * P:(t + 1) * 2 * P, :].rearrange("(p two) d -> p (two d)", two=2)
                             ).then_inc(y_in[t], 16)
            for t in range(NT):
                sp.wait_ge(sum_ready, t + 1)
                sp.dma_start(out[0, t * P:(t + 1) * P, :], X[:, t, :]).then_inc(stored, 16)
            sp.wait_ge(stored, 16 * NT)

        @block.gpsimd
        def _(pool):
            links = [0]

            def link(ins):
                links[0] += 1
                ins.then_inc(pool_link, 1)
                pool.wait_ge(pool_link, links[0])

            g = nc.gpsimd
            g.memset(ones[:, :], 1.0).then_inc(consts, 1)
            g.memset(eps[:, :], EPS).then_inc(eps_set, 1)
            g.iota(io[:, :], pattern=[[1, 64]], base=0, channel_multiplier=0,
                   allow_small_or_imprecise_dtypes=True).then_inc(consts, 1)
            g.iota(tok[:, :], pattern=[[P, NT]], base=0, channel_multiplier=1,
                   allow_small_or_imprecise_dtypes=True).then_inc(consts, 1)
            link(g.memset(ident[:, :], 0.0))
            g.affine_select(out=ident[:, :], in_=ident[:, :], compare_op=ALU.not_equal, fill=1.0, base=0,
                            pattern=[[-1, P]], channel_multiplier=1).then_inc(consts, 1)
            link(g.memset(blk[:, :], 0.0))
            g.memset(blk[0:HD, 0:HD], 1.0).then_inc(consts, 1)
            g.memset(blk[HD:P, HD:P], 1.0).then_inc(consts, 1)

            pool.wait_ge(kx_ready, 2)
            pool.wait_ge(used, 8)
            g.memset(kdup[:, :, 0:CHUNK], 0.0).then_inc(k_padded, 1)
            g.memset(vTp[:, 0:CHUNK], 0.0).then_inc(k_padded, 1)
            link(g.memset(wsum[:, :, 0:16], 0.0))
            g.iota(cnt16, pattern=[[1, 16]], base=1, channel_multiplier=0,
                   allow_small_or_imprecise_dtypes=True).then_inc(ramp_in, 1)
            link(g.iota(mask, pattern=[[-1, WIN]], base=CHUNK, channel_multiplier=1,
                        allow_small_or_imprecise_dtypes=True))
            link(g.tensor_scalar(dist, mask, -1.0, 0.0, ALU.mult, ALU.max))
            link(g.tensor_scalar(mask, mask, 0.0, None, ALU.max))
            link(g.tensor_tensor(dist, dist, mask, ALU.add))
            link(g.memset(mask, 0.0))
            link(g.memset(mask[0:CHUNK, 2 * CHUNK:3 * CHUNK], NEG))
            link(g.memset(mask[CHUNK:P, 0:CHUNK], NEG))
            for h in range(NH):
                slope = 2.0 ** (-8.0 * (head_at(h) + 1) / NH)
                for at, n, col in WINDOW[h % 2]:
                    part = bias[:, h, at:at + n]
                    link(g.tensor_scalar(part, dist[:, col:col + n], -slope, None, ALU.mult))
                    link(g.tensor_tensor(part, part, mask[:, col:col + n], ALU.add))
            pairs = bias.rearrange("p (j e) n -> p j (e n)", e=2)
            before = [pairs[:, :, 0:CHUNK], pairs[:, :, WIN + CHUNK:WIN + 2 * CHUNK]]
            for part in before:
                g.memset(part, NEG).then_inc(bias_built, 1)
            pool.wait_ge(scores_read, 8)
            for part in before:
                g.memset(part[CHUNK:P], NEG).then_inc(bias_reset, 1)
            for h in range(NH):
                slope = 2.0 ** (-8.0 * (head_at(h) + 1) / NH)
                part = before[h % 2][0:CHUNK, h // 2, :]
                link(g.iota(part, pattern=[[-1, CHUNK]], base=CHUNK, channel_multiplier=1,
                            allow_small_or_imprecise_dtypes=True))
                g.tensor_scalar(part, part, -slope, None, ALU.mult).then_inc(bias_reset, 1)

            pool.wait_ge(ramp_ready, 1)
            for i in range(8):
                lv = i // 2 + 1
                w = 2 ** lv
                u = proj[:, 10 + i, :]
                pool.wait_ge(u_ready, i + 1)
                g.tensor_copy(wsum[:, 0, 16:17], u[:, 0:1])
                link(g.tensor_tensor(wsum[:, 0, 17:528], u[:, 1:512], u[:, 0:511], ALU.add))
                for n in range(1, lv):
                    a, b, sh = (n - 1) % 2, n % 2, 2 ** n
                    link(g.tensor_tensor(wsum[:, b, 16:528], wsum[:, a, 16:528],
                                         wsum[:, a, 16 - sh:528 - sh], ALU.add))
                c = (lv - 1) % 2
                link(g.tensor_tensor(wsum[:, c, 16:32], wsum[:, c, 16:32], ramp[:, lv - 1, :], ALU.mult))
                link(g.tensor_scalar(wsum[:, c, 16:528], wsum[:, c, 16:528], 1.0 / w, None, ALU.mult))
                g.tensor_tensor(u, wsum[:, c, 16:528], u, ALU.subtract).then_inc(d_ready, 1)
                pool.wait_ge(d_ready, i + 1)

            pool.wait_ge(used, SEQ_POOL + 1)
            link(g.memset(tri, 1.0))
            g.affine_select(out=tri, in_=tri, compare_op=ALU.is_gt, fill=0.0, base=0,
                            pattern=[[1, P]], channel_multiplier=-1).then_inc(tri_ready, 1)
            for grp in range(NG):
                pool.dma_start(wr[:, :, NG + grp * EPG:NG + (grp + 1) * EPG],
                               router_expert_w[0, grp].rearrange("(k p) e -> p k e", p=P)).then_inc(router_in, 16)
            pool.dma_start(wr[:, :, 0:NG], router_group_w[0].rearrange("(k p) e -> p k e", p=P)).then_inc(router_in, 16)

            for t in range(NT):
                pool.wait_ge(h_ready, 10 + t + 1)
                pool.dma_start(hn_dram[t * P:(t + 1) * P, :], hs[:, t % 2, :]).then_inc(hn_stored[t % 2], 16)
            for b in range(2):
                pool.wait_ge(hn_stored[b], 32)
            pool.wait_ge(h_turned, 4 * 14)
            g.memset(hs[:, :, :], 0.0).then_inc(xs_clear, 1)
            pool.wait_ge(xs_clear, 1)
            pool.wait_ge(table_ready, 1)
            xs = hs

            def reg(value):
                return value if isinstance(value, int) else pool.to_reg(value)

            def scatter(b, par):
                wait_past(pool, scattered[par], b * 8 - 8 * par)
                g.tensor_copy(cols[:, 2 + par:3 + par], yidx[:, ds(b, 1)]).then_inc(idx_copied, 1)
                copied, done = reg(b * 2 + 3), reg(b + 1)
                pool.wait_ge(table_ready, 1)
                pool.wait_ge(idx_copied, copied)
                pool.wait_ge(y_act, done)
                pool.wait_ge(y_dve, done)
                g.indirect_dma_start(out=y_dram, out_offset=bass.IndirectOffsetOnAxis(ap=cols[:, 2 + par:3 + par], axis=0),
                                     in_=y[0:SLOTS, par, :], in_offset=None,
                                     bounds_check=2 * S - 1, oob_is_err=False).then_inc(scattered[par], 16)

            g.tensor_copy(cols[:, 0:1], tidx[:, 0:1]).then_inc(idx_copied, 1)
            pool.wait_ge(idx_copied, 1)
            g.indirect_dma_start(out=xs[0:SLOTS, 0, :], out_offset=None, in_=hn_dram,
                                 in_offset=bass.IndirectOffsetOnAxis(ap=cols[:, 0:1], axis=0),
                                 bounds_check=S - 1, oob_is_err=False).then_inc(gathered[0], 16)

            def step(b, par):
                wait_past(pool, xs_turned, b * 2)
                g.tensor_copy(cols[:, 1 - par:2 - par], tidx[:, ds(b + 1, 1)]).then_inc(idx_copied, 1)
                copied = reg(b * 2 + 2)
                pool.wait_ge(table_ready, 1)
                pool.wait_ge(idx_copied, copied)
                g.indirect_dma_start(out=xs[0:SLOTS, 1 - par, :], out_offset=None, in_=hn_dram,
                                     in_offset=bass.IndirectOffsetOnAxis(ap=cols[:, 1 - par:2 - par], axis=0),
                                     bounds_check=S - 1, oob_is_err=False).then_inc(gathered[1 - par], 16)
                scatter(b, par)

            step(0, 0)
            step(1, 1)
            with pool.Fori(1, NE // 2) as it:
                b = it * 2
                step(b, 0)
                step(b + 1, 1)
            for par in range(2):
                pool.wait_ge(scattered[par], 16 * NE // 2)
            pool.wait_ge(gathered[0], 16 * (NE // 2 + 1))
            more = pool.value_load(meta[0:1, NOVER:NOVER + 1], min_val=0, max_val=NOVER)
            with pool.If(more > 0):
                with pool.Fori(NE // 2, NBLK // 2) as it:
                    b = it * 2
                    step(b, 0)
                    step(b + 1, 1)
                for par in range(2):
                    pool.wait_ge(scattered[par], 16 * NBLK // 2)
                pool.wait_ge(gathered[0], 16 * (NBLK // 2 + 1))
            g.memset(cols[:, 0:1], 0).then_inc(all_scattered, 1)

        @block.scalar
        def _(act):
            a = nc.scalar
            links = [0]

            def link(ins):
                links[0] += 1
                ins.then_inc(act_link, 1)
                act.wait_ge(act_link, links[0])

            grow = PB[0:NGR, 8192:8192 + P]
            for r0, v in ((G_MIX, mix_norm_g), (G_XAT, xattn_norm_g), (G_MEM, mem_norm_g), (G_FFN, ffn_norm_g),
                          (G_POOL, pool_scale)):
                act.dma_start(grow[r0:r0 + v.shape[1] // P, :], v[0].rearrange("(k p) -> k p", p=P)).then_inc(gain_in, 16)
            for r0, v in ((G_Q, q_norm_g), (G_K, k_norm_g)):
                for c in range(2):
                    act.dma_start(grow[r0:r0 + 1, c * HD:(c + 1) * HD], v[0:1, :]).then_inc(gain_in, 16)
            for r0, v in ((G_XQ, xq_norm_g), (G_XK, xk_norm_g)):
                act.dma_start(grow[r0:r0 + 1, :], v[0:1, :]).then_inc(gain_in, 16)
            act.dma_start(X[:, :, :], x[0].rearrange("(t p) d -> p t d", p=P)).then_inc(x_in, 16)
            act.dma_start(sink[:, :], sink_logits[0:1, :].broadcast_to([P, NH])).then_inc(small_in, 16)
            act.dma_start(rbias[:, 0:NG], router_group_b[0:1, :].broadcast_to([P, NG])).then_inc(small_in, 16)
            act.dma_start(rbias[:, NG:NCOL], router_expert_b.rearrange("l g e -> l (g e)").broadcast_to([P, NE])
                          ).then_inc(small_in, 16)
            act.wait_ge(eps_set, 1)

            def norm_tile(T, par, src, first=False, stored=None):
                if not first:
                    act.wait_ge(h_turned, 4 * T - 4)
                if stored is not None:
                    act.wait_ge(hn_stored[par], stored)
                a.activation(hs[:, par, :], src, ACT.Square, accum_out=stat[:, 0, ds(T, 1)]).then_inc(ssq_done, 1)
                act.wait_ge(ssq_done, T + 1)
                a.activation(stat[:, 1, ds(T, 1)], stat[:, 0, ds(T, 1)], ACT.Sqrt, bias=eps[:, 0:1],
                             scale=1.0 / D).then_inc(root_done, 1)
                act.wait_ge(rstd_done, T + 1)
                a.activation(hs[:, par, :], src, ACT.Copy, scale=stat[:, 2, ds(T, 1)]).then_inc(h_ready, 1)

            for t in range(2):
                act.wait_ge(mem_in[t], 16)
                norm_tile(t, t, memx[:, t, :], first=True)
            act.wait_ge(used, 4)
            for b in range(2):
                a.activation(sqm[:, b * 512:(b + 1) * 512], ps[:, 4 + b, :], ACT.Square).then_inc(xk_sq, 1)
            for b in range(2):
                act.wait_ge(xk_ss, b + 1)
                a.activation(rtm[:, b * 512:(b + 1) * 512], ps[:, b, :], ACT.Sqrt, bias=eps[:, 0:1],
                             scale=1.0 / XD).then_inc(xk_root, 1)
            act.wait_ge(x_in, 16)
            act.wait_ge(xk_ss, 2)
            for t in range(NT):
                norm_tile(2 + t, t % 2, X[:, t, :])
            act.wait_ge(used, 8)
            for m in range(2):
                a.activation(vx[:, m, :], ps[:, 6 + m, :], ACT.Copy).then_inc(vx_ready, 1)

            def squares(n, s, b, first=False):
                act.wait_ge(used, n + (SEQ_Q + 1))
                if not first:
                    act.wait_ge(q_ss, n - 1)
                a.activation(sq[:, b, :], ps[:, 4 + s, :], ACT.Square).then_inc(q_sq, 1)

            def root(n, s, b):
                act.wait_ge(q_ss, n + 1)
                a.activation(rt[:, b, :], ps[:, s, :], ACT.Sqrt, bias=eps[:, 0:1], scale=1.0 / HD).then_inc(q_root, 1)

            act.wait_ge(bias_built, 2)
            act.wait_ge(kx_ready, 2)
            with act.Fori(0, 2) as it:
                n = it * 4
                for s in range(4):
                    squares(n + s, s, s % 2, first=s < 2)
                    if s >= 1:
                        act.wait_ge(q_ready, n + s)
                    root(n + s, s, s % 2)
                act.wait_ge(q_ready, n + 3)
            act.wait_ge(q_ss, 8)
            squares(8, 0, 0)
            act.wait_ge(q_ready, 8)
            root(8, 0, 0)
            act.wait_ge(used, SEQ_K + 2)
            a.activation(vTp[:, CHUNK:CHUNK + S], ps[:, 5, :], ACT.Copy).then_inc(v_copied, 1)
            act.wait_ge(v_turned, 2)
            a.activation(vA[:, :, :], ps[:, 2, :].rearrange("p (t c) -> p t c", t=NT), ACT.Copy).then_inc(v_ready, 1)

            for i in range(8):
                act.wait_ge(max_done, 2 * i + 2)
                for h in range(8):
                    a.activation(Ssb[:, h, :], Ssb[:, h, :], ACT.Exp, bias=sm[:, 1, h:h + 1],
                                 accum_out=sm[:, 2, h:h + 1]).then_inc(exp_done, 1)
                a.activation(sm[:, 4, :], sm[:, 3, :], ACT.Exp).then_inc(exp_done, 1)
                act.wait_ge(used, SEQ_U + i + 1)
                a.activation(proj[:, 10 + i, :], ps[:, 4, :], ACT.Copy).then_inc(u_ready, 1)
                for j in (1, 3):
                    act.wait_ge(pt_turned, 4 * i + j + 1)
                    a.activation(PT[:, j, :], ps[:, j, 0:384], ACT.Copy).then_inc(pt_act, 1)
            for tt in range(NT):
                act.wait_ge(a_turned, 2 * tt + 2)
                b = 2 * (tt % 2) + 1
                a.activation(H[:, 4:8, tt * P:(tt + 1) * P], ps[:, b, :].rearrange("p (k n) -> p k n", n=P),
                             ACT.Copy).then_inc(aT_act, 1)
            for m in range(8):
                act.wait_ge(*((pool_done, m + 1) if m < 7 else (used, SEQ_POOL + 1)))
                a.activation(H[:, 8 + m, :], ps[:, 4 + m % 4, :], ACT.Copy,
                             scale=gT[:, G_POOL + m:G_POOL + m + 1]).then_inc(pT_ready, 1)

            act.wait_ge(x_added, 16)
            with act.Fori(0, NT // 2) as it:
                t = it * 2
                for q in range(2):
                    norm_tile(6 + q + t, q, X[:, ds(t + q, 1), :].rearrange("p a d -> p (a d)"))
            for f in range(XH):
                act.wait_ge(*((xq_done, f + 1) if f < 3 else (used, SEQ_XQ + 4)))
                if f >= 2:
                    act.wait_ge(xq_ss, f - 1)
                a.activation(sqx[:, f % 2, :], ps[:, 4 + f, :], ACT.Square).then_inc(xq_sq, 1)
            for f in range(XH):
                act.wait_ge(xq_ss, f + 1)
                if f >= 2:
                    act.wait_ge(qx_ready, f - 1)
                a.activation(rtx[:, f % 2, :], ps[:, f, :], ACT.Sqrt, bias=eps[:, 0:1], scale=1.0 / XD
                             ).then_inc(xq_root, 1)
            act.wait_ge(qx_ready, XH)

            def xexps(t):
                act.wait_ge(xmax_done, t + 1)
                for h in range(XH):
                    c = (t % 2) * 4 + h
                    a.activation(SX[:, t % 2, h * NM:(h + 1) * NM],
                                 ps[:, 5 * (t % 2) + h // 2, (h % 2) * NM:(h % 2 + 1) * NM], ACT.Exp,
                                 bias=sm[:, 1, c:c + 1], scale=XD ** -0.5,
                                 accum_out=sm[:, 2, c:c + 1]).then_inc(xexp_done, 1)

            xexps(0)
            for t in range(NT):
                if t + 1 < NT:
                    xexps(t + 1)
                act.wait_ge(xp_turned, 2 * t + 1)
                a.activation(PTX[:, 0:512], ps[:, 2, :], ACT.Copy).then_inc(xpt_act, 1)

            act.wait_ge(x_added, 32)
            for t in range(NT):
                norm_tile(10 + t, t % 2, X[:, t, :], stored=16 if t >= 2 else None)

            act.wait_ge(gmax_done, 1)
            a.activation(rq["eg"], rq["gs"], ACT.Exp).then_inc(gexp_done, 1)
            act.wait_ge(top_done, 1)
            a.activation(rq["et"], rq["dt"], ACT.Exp).then_inc(texp_done, 1)

            def block_act(b, par):
                act.wait_ge(used, b * 12 + (UE + 8))
                a.activation(gu, ps[:, 0, :], ACT.Copy).then_inc(gu_copied, 1)
                act.wait_ge(gu_turned, b + 1)
                wait_past(act, act_ready, b)
                a.activation(sil.rearrange("p (f n) -> p f n", n=SLOTS), guT[:, :, 0:SLOTS],
                             ACT.Silu).then_inc(sil_ready, 1)
                act.wait_ge(used, b * 12 + (UE + 12))
                wait_past(act, scattered[par], b * 8 - 8 * par)
                a.activation(y4[0:SLOTS, par, 0:4:2, :], ps[0:SLOTS, 4:8:2, :], ACT.Copy,
                             scale=gate[:, ds(b, 1)]).then_inc(y_act, 1)

            act.wait_ge(table_ready, 1)
            block_act(0, 0)
            block_act(1, 1)
            with act.Fori(1, NE // 2) as it:
                b = it * 2
                block_act(b, 0)
                block_act(b + 1, 1)
            more = act.value_load(meta[0:1, NOVER:NOVER + 1], min_val=0, max_val=NOVER)
            with act.If(more > 0):
                with act.Fori(NE // 2, NBLK // 2) as it:
                    b = it * 2
                    block_act(b, 0)
                    block_act(b + 1, 1)

        @block.vector
        def _(dve):
            v = nc.vector
            links = [0]

            def link(ins):
                links[0] += 1
                ins.then_inc(dve_link, 1)
                dve.wait_ge(dve_link, links[0])

            def wide(ap, *shape):
                return ap.broadcast_to(list(shape))

            def norm_tile(T, dstT, at, gcol):
                dve.wait_ge(root_done, T + 1)
                v.reciprocal(stat[:, 2, ds(T, 1)], stat[:, 1, ds(T, 1)]).then_inc(rstd_done, 1)
                for b in range(4):
                    dve.wait_ge(h_turned, T * 4 + b + 1)
                    v.tensor_tensor(dstT[:, 4 * b:4 * b + 4, ds(at, P)],
                                    ps[:, b, :].rearrange("p (k n) -> p k n", n=P),
                                    wide(gT[:, gcol + 4 * b:gcol + 4 * b + 4].unsqueeze(2), P, 4, P),
                                    ALU.mult).then_inc(hT_ready, 1)

            dve.wait_ge(gain_turned, 1)
            v.tensor_copy(gT[:, :], ps[:, 7, 0:NGR]).then_inc(gains, 1)
            dve.wait_ge(gains, 1)
            for t in range(2):
                norm_tile(t, memT, t * P, G_MEM)
            for b in range(2):
                dve.wait_ge(xk_root, b + 1)
                link(v.reciprocal(rtm[:, b * 512:(b + 1) * 512], rtm[:, b * 512:(b + 1) * 512]))
                v.scalar_tensor_tensor(out=kx[:, 2 * b:2 * b + 2, :].rearrange("p h n -> p (h n)"),
                                       in0=ps[:, 4 + b, :], scalar=gT[:, G_XK:G_XK + 1],
                                       in1=rtm[:, b * 512:(b + 1) * 512],
                                       op0=ALU.mult, op1=ALU.mult).then_inc(kx_ready, 1)
            for t in range(NT):
                norm_tile(2 + t, H, t * P, G_MIX)
            dve.wait_ge(ramp_in, 1)
            for lv in range(4):
                w = float(2 ** (lv + 1))
                link(v.tensor_scalar(ramp[:, lv, :], cnt16, w, None, ALU.min))
                link(v.reciprocal(ramp[:, lv, :], ramp[:, lv, :]))
                r = v.tensor_scalar(ramp[:, lv, :], ramp[:, lv, :], w, None, ALU.mult)
                if lv < 3:
                    link(r)
            r.then_inc(ramp_ready, 1)

            with dve.Fori(0, 2) as it:
                n = it * 4
                for s in range(4):
                    dve.wait_ge(q_root, n + (s + 1))
                    v.reciprocal(rt[:, s % 2, :], rt[:, s % 2, :]).then_inc(q_recip, 1)
                    dve.wait_ge(q_recip, n + (s + 1))
                    v.scalar_tensor_tensor(out=proj[:, ds(n + s, 1), :].rearrange("p a n -> p (a n)"),
                                           in0=ps[:, 4 + s, :], scalar=gT[:, G_Q:G_Q + 1], in1=rt[:, s % 2, :],
                                           op0=ALU.mult, op1=ALU.mult).then_inc(q_ready, 1)
            dve.wait_ge(q_root, 9)
            link(v.reciprocal(rt[:, 0, :], rt[:, 0, :]))
            dve.wait_ge(k_padded, 2)
            for g in range(2):
                half = slice(g * HD, (g + 1) * HD)
                link(v.scalar_tensor_tensor(out=kdup[half, g, CHUNK:CHUNK + S], in0=ps[half, 4, :],
                                            scalar=gT[half, G_K:G_K + 1], in1=rt[half, 0, :],
                                            op0=ALU.mult, op1=ALU.mult))
            for g in range(2):
                v.tensor_copy(kdup[(1 - g) * HD:(2 - g) * HD, g, CHUNK:CHUNK + S],
                              kdup[g * HD:(g + 1) * HD, g, CHUNK:CHUNK + S]).then_inc(k_ready, 1)
            link(v.memset(vB[:, :, :, :], 0.0))
            dve.wait_ge(v_turned, 2)
            for g in range(2):
                v.tensor_copy(vB[g * HD:(g + 1) * HD, g, :, :],
                              ps[0:HD, 3, :].rearrange("p (t c) -> p t c", t=NT)).then_inc(v_ready, 1)

            for i in range(8):
                t, g = i // 2, i % 2
                if i == 0:
                    dve.wait_ge(bias_built, 2)
                    dve.wait_ge(small_in, 48)
                if i == 2:
                    dve.wait_ge(bias_reset, 2 + NH)
                for n, j in enumerate((0, 2, 1, 3)):
                    dve.wait_ge(scores_done, 4 * i + n + 1)
                    v.scalar_tensor_tensor(out=Ssb[:, 2 * j:2 * j + 2, :],
                                           in0=ps[:, j, 0:2 * WIN].rearrange("p (h n) -> p h n", n=WIN),
                                           scalar=HD ** -0.5, in1=bias[:, 8 * g + 2 * j:8 * g + 2 * j + 2, :],
                                           op0=ALU.mult, op1=ALU.add).then_inc(scores_read, 1)
                dve.wait_ge(scores_read, 4 * i + 4)
                link(v.tensor_reduce(sm[:, 0, :], Ssb[:, :, :], AX, ALU.max))
                sinks = sink[:, 8 * g:8 * g + 8].rearrange("p (a b) -> p b a", b=2)
                smv = sm[:, :, :].rearrange("p r (b a) -> p r b a", b=2)
                link(v.tensor_tensor(smv[:, 0], smv[:, 0], sinks, ALU.max))
                v.tensor_scalar(sm[:, 1, :], sm[:, 0, :], -1.0, None, ALU.mult).then_inc(max_done, 1)
                v.tensor_tensor(smv[:, 3], sinks, smv[:, 0], ALU.subtract).then_inc(max_done, 1)
                dve.wait_ge(exp_done, 9 * i + 9)
                link(v.tensor_tensor(sm[:, 5, :], sm[:, 2, :], sm[:, 4, :], ALU.add))
                link(v.reciprocal(sm[:, 5, :], sm[:, 5, :]))
                for j in (0, 2):
                    dve.wait_ge(pt_turned, 4 * i + j + 1)
                    v.tensor_copy(PT[:, j, :], ps[:, j, 0:384]).then_inc(pt_dve, 1)
                dve.wait_ge(pv_done, i + 1)
                v.tensor_tensor(a_rows[:, t, g * 512:(g + 1) * 512].rearrange("p (a b d) -> p b a d", b=2, d=HD),
                                ps[:, 5, :].rearrange("p (b a d) -> p b a d", b=2, d=HD),
                                wide(smv[:, 5].unsqueeze(3), P, 2, 4, HD), ALU.mult).then_inc(a_ready, 1)
            for tt in range(NT):
                dve.wait_ge(a_turned, 2 * tt + 1)
                v.tensor_copy(H[:, 0:4, tt * P:(tt + 1) * P],
                              ps[:, 2 * (tt % 2), :].rearrange("p (k n) -> p k n", n=P)).then_inc(aT_dve, 1)

            def add_out(n, par, cross):
                for t in range(NT):
                    if cross:
                        dve.wait_ge(o_done, n * 4 + (12 + t + 1))
                    elif t < 3:
                        dve.wait_ge(o_done, n * 3 + (t + 1))
                    else:
                        dve.wait_ge(used, n * 4 + (SEQ_OUT + 4))
                    xs_ = X[:, t, ds(n * 512, 512)]
                    v.tensor_tensor(xs_, ps[:, 4 * par + t, :], xs_, ALU.add).then_inc(x_added, 1)

            dve.wait_ge(x_in, 16)
            with dve.Fori(0, 2) as it:
                n = it * 2
                for par in range(2):
                    add_out(n + par, par, False)

            with dve.Fori(0, NT // 2) as it:
                t = it * 2
                for q in range(2):
                    norm_tile(t + (6 + q), H, t * P + q * P, G_XAT)
            for f in range(XH):
                dve.wait_ge(xq_root, f + 1)
                link(v.reciprocal(rtx[:, f % 2, :], rtx[:, f % 2, :]))
                v.scalar_tensor_tensor(out=qx[:, f, :], in0=ps[:, 4 + f, :], scalar=gT[:, G_XQ:G_XQ + 1],
                                       in1=rtx[:, f % 2, :], op0=ALU.mult, op1=ALU.mult).then_inc(qx_ready, 1)

            def xmax(t):
                c = slice(4 * (t % 2), 4 * (t % 2) + 4)
                dve.wait_ge(xs_done, t + 1)
                b0 = 5 * (t % 2)
                link(v.tensor_reduce(sm[:, 0, c], ps[:, b0:b0 + 2, :].rearrange("p b (h n) -> p (b h) n", n=NM),
                                     AX, ALU.max))
                v.tensor_scalar(sm[:, 1, c], sm[:, 0, c], -(XD ** -0.5), None, ALU.mult).then_inc(xmax_done, 1)

            def xnorm(t):
                c = slice(4 * (t % 2), 4 * (t % 2) + 4)
                dve.wait_ge(xexp_done, 4 * t + 4)
                link(v.reciprocal(sm[:, 5, c], sm[:, 2, c]))
                sx = SX[:, t % 2, :].rearrange("p (h n) -> p h n", n=NM)
                v.tensor_tensor(sx, sx, wide(sm[:, 5, c].unsqueeze(2), P, XH, NM), ALU.mult).then_inc(xp_ready, 1)

            xmax(0)
            xnorm(0)
            xmax(1)
            for t in range(NT):
                dve.wait_ge(xp_turned, 2 * t + 2)
                v.tensor_copy(PTX[:, 512:1024], ps[:, 3, :]).then_inc(xpt_dve, 1)
                dve.wait_ge(xo_part, t + 1)
                v.tensor_copy(H[:, 0:XH, t * P:(t + 1) * P],
                              ps[:, 4 + 3 * (t % 2), :].rearrange("p (h n) -> p h n", n=P)).then_inc(oT_ready, 1)
                if t + 1 < NT:
                    xnorm(t + 1)
                if t + 2 < NT:
                    xmax(t + 2)
            with dve.Fori(0, 2) as it:
                n = it * 2
                for par in range(2):
                    add_out(n + par, par, True)
            for t in range(NT):
                norm_tile(10 + t, H, t * P, G_FFN)

            r = rq
            dve.wait_ge(logits_done, 1)
            link(v.tensor_tensor(r["L"], ps[:, 4, 0:NT * NCOL].rearrange("p (t c) -> p t c", c=NCOL),
                                 wide(rbias[:, :].unsqueeze(1), P, NT, NCOL), ALU.add))
            LG = r["L"][:, :, 0:NG]
            LE = r["L"][:, :, NG:NCOL].rearrange("p t (g e) -> p t g e", e=EPG)

            def top(vals, width, best, pick, cand):
                link(v.tensor_reduce(best, vals, AX, ALU.max))
                link(v.tensor_tensor(pick, vals, wide(best.unsqueeze(2), P, NT, width), ALU.is_equal))
                link(v.scalar_tensor_tensor(out=cand, in0=pick, scalar=-64.0,
                                            in1=wide(io[:, 0:width].unsqueeze(1), P, NT, width),
                                            op0=ALU.mult, op1=ALU.add))
                link(v.tensor_reduce(r["ti"], cand, AX, ALU.min))
                link(v.tensor_scalar(r["ti"], r["ti"], 64.0, None, ALU.add))
                link(v.tensor_tensor(pick, wide(io[:, 0:width].unsqueeze(1), P, NT, width),
                                     wide(r["ti"].unsqueeze(2), P, NT, width), ALU.is_equal))

            top(LG, NG, r["gm"], r["gh"], r["cand"][:, :, 0:NG])
            v.tensor_tensor(r["gs"], LG, wide(r["gm"].unsqueeze(2), P, NT, NG), ALU.subtract).then_inc(gmax_done, 1)
            link(v.tensor_tensor(r["tg"], LE, wide(r["gh"].unsqueeze(3), P, NT, NG, EPG), ALU.mult))
            link(v.tensor_reduce(r["es"], r["tg"].rearrange("p t g e -> p t e g"), AX, ALU.add))
            top(r["es"], EPG, r["m1"], r["h1"], r["cand"])
            link(v.scalar_tensor_tensor(out=r["t8"], in0=r["h1"], scalar=NEG, in1=r["es"], op0=ALU.mult, op1=ALU.add))
            top(r["t8"], EPG, r["m2"], r["h2"], r["cand"])
            v.tensor_tensor(r["dt"], r["m2"], r["m1"], ALU.subtract).then_inc(top_done, 1)
            for k, name in enumerate(("M1", "M2")):
                link(v.tensor_tensor(r[name].rearrange("p t (g e) -> p t g e", e=EPG),
                                     wide(r["gh"].unsqueeze(3), P, NT, NG, EPG),
                                     wide(r["h1" if k == 0 else "h2"].unsqueeze(2), P, NT, NG, EPG), ALU.mult))
            v.tensor_tensor(r["M"], r["M1"], r["M2"], ALU.add).then_inc(picks, 1)
            dve.wait_ge(gexp_done, 1)
            link(v.tensor_reduce(r["gsum"], r["eg"], AX, ALU.add))
            link(v.reciprocal(r["gg"], r["gsum"]))
            dve.wait_ge(texp_done, 1)
            link(v.tensor_scalar(r["w2"], r["et"], 1.0, None, ALU.add))
            link(v.reciprocal(r["w2"], r["w2"]))
            link(v.tensor_tensor(r["w1"], r["gg"], r["w2"], ALU.mult))
            link(v.tensor_tensor(r["w2"], r["w1"], r["et"], ALU.mult))
            dve.wait_ge(ranks, 1)
            link(v.tensor_copy(r["R"], ps[:, 5, 0:(NT + 1) * NE].rearrange("p (t e) -> p t e", e=NE)))
            link(v.tensor_scalar(r["thr"], io[:, 1:1 + MORE], float(SLOTS), None, ALU.mult))
            link(v.tensor_tensor(r["cmp"], wide(r["R"][:, NT, :].unsqueeze(2), P, NE, MORE),
                                 wide(r["thr"].unsqueeze(1), P, NE, MORE), ALU.is_gt))
            link(v.tensor_reduce(r["over"], r["cmp"], AX, ALU.add))
            link(v.memset(r["ca"], 0.0))
            link(v.memset(r["cb"], 0.0))
            link(v.tensor_copy(r["ca"][:, 16:16 + NE], r["over"]))
            src, dst = r["ca"], r["cb"]
            for sh in (1, 2, 4, 8, 16):
                link(v.tensor_tensor(dst[:, 16:16 + NE], src[:, 16:16 + NE], src[:, 16 - sh:16 + NE - sh], ALU.add))
                src, dst = dst, src
            upto = src[:, 16:16 + NE]
            link(v.tensor_tensor(r["base"], upto, r["over"], ALU.subtract))
            for k in range(2):
                M = r["M1" if k == 0 else "M2"]

                def of_pick(dst_, table):
                    link(v.tensor_tensor(r["tmp"], table, M, ALU.mult))
                    link(v.tensor_reduce(dst_, r["tmp"], AX, ALU.add))

                of_pick(r["pos"], r["R"][:, 0:NT, :])
                of_pick(r["ob"], wide(r["base"].unsqueeze(1), P, NT, NE))
                of_pick(r["ek"], wide(io[:, 0:NE].unsqueeze(1), P, NT, NE))
                link(v.tensor_tensor(r["pc"], wide(r["pos"].unsqueeze(2), P, NT, MORE),
                                     wide(r["thr"].unsqueeze(1), P, NT, MORE), ALU.is_ge))
                link(v.tensor_reduce(r["q"], r["pc"], AX, ALU.add))
                link(v.scalar_tensor_tensor(out=r["row"], in0=r["q"], scalar=-float(SLOTS), in1=r["pos"],
                                            op0=ALU.mult, op1=ALU.add))
                link(v.tensor_scalar(r["z"], r["q"], 0.0, None, ALU.is_equal))
                link(v.scalar_tensor_tensor(out=r["bk"], in0=r["ob"], scalar=float(NE - 1), in1=r["q"],
                                            op0=ALU.add, op1=ALU.add))
                link(v.tensor_tensor(r["ek"], r["ek"], r["bk"], ALU.subtract))
                link(v.tensor_tensor(r["ek"], r["ek"], r["z"], ALU.mult))
                link(v.tensor_tensor(r["bk"], r["bk"], r["ek"], ALU.add))
                v.tensor_tensor(r["P1" if k == 0 else "P2"], wide(io[:, 0:SLOTS].unsqueeze(1), P, NT, SLOTS),
                                wide(r["row"].unsqueeze(2), P, NT, SLOTS), ALU.is_equal).then_inc(onehots, 1)
                link(v.tensor_tensor(r["one"], wide(io[:, 0:TCOL].unsqueeze(1), P, NT, TCOL),
                                     wide(r["bk"].unsqueeze(2), P, NT, TCOL), ALU.is_equal))
                link(v.tensor_scalar(r["val"], tok[:, :], 2.0, float(k + 1), ALU.mult, ALU.add))
                B = r["B1" if k == 0 else "B2"]
                v.tensor_tensor(B[:, :, 0:TCOL], r["one"], wide(r["val"].unsqueeze(2), P, NT, TCOL),
                                ALU.mult).then_inc(onehots, 1)
                v.tensor_tensor(B[:, :, TCOL:2 * TCOL], r["one"],
                                wide(r["w1" if k == 0 else "w2"].unsqueeze(2), P, NT, TCOL),
                                ALU.mult).then_inc(onehots, 1)
                dve.wait_ge(onehots, 3 * k + 3)
            link(v.tensor_tensor(r["ec"], wide(upto.unsqueeze(1), P, NOVER, NE),
                                 wide(io[:, 0:NOVER].unsqueeze(2), P, NOVER, NE), ALU.is_le))
            link(v.tensor_reduce(r["ev"][:, 0:NOVER], r["ec"], AX, ALU.add))
            link(v.tensor_scalar(r["ev"][:, 0:NOVER], r["ev"][:, 0:NOVER], float(NE - 1), None, ALU.min))
            link(v.tensor_copy(r["ev"][:, NOVER:NOVER + 1], upto[:, NE - 1:NE]))
            link(v.tensor_copy(meta, r["ev"][0:1, :]))
            dve.wait_ge(table_done, 1)
            link(v.tensor_copy(r["fin"][0:SLOTS, :], ps[0:SLOTS, 6, 0:2 * TCOL]))
            V = r["fin"][0:SLOTS, 0:TCOL]
            link(v.tensor_copy(gate, r["fin"][0:SLOTS, TCOL:2 * TCOL]))
            zero = r["one"][0:SLOTS, 0, :]
            link(v.tensor_scalar(zero, V, 0.0, float(EMPTY), ALU.is_equal, ALU.mult))
            link(v.scalar_tensor_tensor(out=V, in0=V, scalar=-1.0, in1=zero, op0=ALU.add, op1=ALU.add))
            link(v.tensor_copy(yidx, V))
            v.tensor_scalar(tidx, yidx, 1, None, ALU.logical_shift_right).then_inc(table_ready, 1)

            def turn_evac(b, par):
                for q in range(2):
                    dve.wait_ge(xs_turned, b * 2 + (q + 1))
                    v.tensor_tensor(xsT[:, par, 8 * q:8 * q + 8, :],
                                    ps[:, 2 + q, 0:8 * SLOTS].rearrange("p (k n) -> p k n", n=SLOTS),
                                    wide(gT[:, G_FFN + 8 * q:G_FFN + 8 * q + 8].unsqueeze(2), P, 8, SLOTS),
                                    ALU.mult).then_inc(xsT_ready, 1)

            def block_dve(b, par):
                dve.wait_ge(sil_ready, b + 1)
                v.tensor_tensor(act_t.rearrange("p (f n) -> p f n", n=SLOTS), sil.rearrange("p (f n) -> p f n", n=SLOTS),
                                guT[:, :, SLOTS:2 * SLOTS], ALU.mult).then_inc(act_ready, 1)
                turn_evac(b + 1, 1 - par)
                dve.wait_ge(used, b * 12 + (UE + 12))
                wait_past(dve, scattered[par], b * 8 - 8 * par)
                v.tensor_scalar(y4[0:SLOTS, par, 1:4:2, :], ps[SLOTS:2 * SLOTS, 5:8:2, :],
                                gate[:, ds(b, 1)], None, ALU.mult).then_inc(y_dve, 1)

            dve.wait_ge(table_ready, 1)
            turn_evac(0, 0)
            block_dve(0, 0)
            block_dve(1, 1)
            with dve.Fori(1, NE // 2) as it:
                b = it * 2
                block_dve(b, 0)
                block_dve(b + 1, 1)
            more = dve.value_load(meta[0:1, NOVER:NOVER + 1], min_val=0, max_val=NOVER)
            with dve.If(more > 0):
                with dve.Fori(NE // 2, NBLK // 2) as it:
                    b = it * 2
                    block_dve(b, 0)
                    block_dve(b + 1, 1)
            for t in range(NT):
                dve.wait_ge(y_in[t], 16)
                link(v.tensor_tensor(X[:, t, :], X[:, t, :], scr[:, t * 2 * D:t * 2 * D + D], ALU.add))
                v.tensor_tensor(X[:, t, :], X[:, t, :], scr[:, t * 2 * D + D:(t + 1) * 2 * D],
                                ALU.add).then_inc(sum_ready, 1)

        @block.tensor
        def _(pe):
            mm, turn = nc.tensor.matmul, nc.tensor.transpose

            pe.wait_ge(consts, 6)
            pe.wait_ge(gain_in, 16 * 11)
            turn(ps[:, 7, 0:NGR], PB[0:NGR, 8192:8192 + P], ident[0:NGR, 0:NGR]).then_inc(gain_turned, 1)

            def norm_tile(T, par, first=False):
                pe.wait_ge(h_ready, T + 1)
                for b in range(4):
                    if not first:
                        pe.wait_ge(hT_ready, T * 4 + (b - 3))
                    for k in range(4 * b, 4 * b + 4):
                        ins = turn(ps[:, b, (k % 4) * P:(k % 4 + 1) * P], hs[:, par, k * P:(k + 1) * P], ident[:, :])
                    ins.then_inc(h_turned, 1)

            norm_tile(0, 0, first=True)
            norm_tile(1, 1)
            pe.wait_ge(hT_ready, 8)
            for c in range(4):
                n = c
                chunk_landed(pe, n)
                w = chunk(n, XW)
                for kk in range(4):
                    k = 4 * c + kk
                    for f in range(XH):
                        ins = mm(ps[:, 4 + f // 2, (f % 2) * NM:(f % 2 + 1) * NM], w[:, kk, f * P:(f + 1) * P],
                                 memT[:, k, :], start=(k == 0 and f % 2 == 0), stop=(k == KD - 1),
                                 skip_group_check=True)
                ins.then_inc(used, 1)
            for c in range(4):
                n = 4 + c
                chunk_landed(pe, n)
                if c == 0:
                    pe.wait_ge(gains, 1)
                w = chunk(n, XW)
                for kk in range(4):
                    k = 4 * c + kk
                    for m in range(2):
                        ins = mm(ps[:, 6 + m, :], memT[:, k, m * P:(m + 1) * P], w[:, kk, :],
                                 start=(k == 0), stop=(k == KD - 1))
                ins.then_inc(used, 1)
                if c == 0:
                    pe.wait_ge(xk_sq, 2)
                    for b in range(2):
                        mm(ps[:, b, :], ones[:, :], sqm[:, b * 512:(b + 1) * 512], start=True, stop=True
                           ).then_inc(xk_ss, 1)
            pe.wait_ge(xk_root, 2)
            for t in range(NT):
                norm_tile(2 + t, t % 2)
            pe.wait_ge(hT_ready, 24)
            pe.wait_ge(kx_ready, 2)
            pe.wait_ge(vx_ready, 2)

            def col_tile(s, bank):
                w = slot(s).rearrange("p (k n) -> p k n", n=P)
                for k in range(KD):
                    ins = mm(ps[:, bank, :], w[:, k, :], H[:, k, :], start=(k == 0), stop=(k == KD - 1))
                ins.then_inc(used, 1)

            def head_sums(n, s):
                pe.wait_ge(q_sq, n + 1)
                mm(ps[:, s, :], blk[:, :], sq[:, s % 2, :], start=True, stop=True).then_inc(q_ss, 1)

            with pe.Fori(0, 2) as it:
                n = it * 4
                for s in range(4):
                    pe.wait_ge(landed[s], n * 4 + 16 * (loads_before[SEQ_Q + s] + 1))
                    if s == 3:
                        pe.wait_ge(q_ready, n + 1)
                    col_tile(s, 4 + s)
                    if s > 0:
                        head_sums(n + (s - 1), s - 1)
                head_sums(n + 3, 3)
                pe.wait_ge(q_ready, n + 3)
            for c in range(2):
                chunk_landed(pe, SEQ_K + c)
                col_tile(early[SEQ_K + c][0], 4 + c)
                if c == 1:
                    head_sums(8, 0)
            pe.wait_ge(v_copied, 1)
            pe.wait_ge(k_padded, 2)
            pe.wait_ge(q_ready, 8)
            for t in range(NT):
                ins = turn(ps[:, 2, t * P:(t + 1) * P], vTp[:, t * P:(t + 1) * P], ident[:, :])
            ins.then_inc(v_turned, 1)
            for t in range(NT):
                ins = turn(ps[0:CHUNK, 3, t * P:(t + 1) * P], vTp[:, t * P + P:t * P + P + CHUNK], ident[:, :])
            ins.then_inc(v_turned, 1)
            pe.wait_ge(k_ready, 2)
            pe.wait_ge(v_ready, 3)

            for i in range(8):
                t, g = i // 2, i % 2
                for m in (0, 4, 1, 5, 2, 6, 3, 7):
                    hp = slice(m // 4 * HD, (m // 4 + 1) * HD)
                    for at, n, col in WINDOW[m % 2]:
                        ins = mm(ps[:, m // 2, (m % 2) * WIN + at:(m % 2) * WIN + at + n],
                                 proj[hp, 4 * g + m % 4, t * P:(t + 1) * P],
                                 kdup[hp, g, t * P + col:t * P + col + n], start=True, stop=True,
                                 skip_group_check=True)
                    if m % 2 == 1:
                        ins.then_inc(scores_done, 1)
                chunk_landed(pe, SEQ_U + i)
                if i > 0:
                    pe.wait_ge(u_ready, i)
                w = chunk(SEQ_U + i, P)
                for k in range(KD):
                    ins = mm(ps[:, 4, :], w[:, k, :], H[:, k, :], start=(k == 0), stop=(k == KD - 1))
                ins.then_inc(used, 1)
                pe.wait_ge(exp_done, 9 * i + 9)
                for j in range(4):
                    for n in range(3):
                        ins = turn(ps[:, j, n * P:(n + 1) * P], Spair[:, j, n * P:(n + 1) * P], ident[:, :])
                    ins.then_inc(pt_turned, 1)
                for j in range(4):
                    pe.wait_ge(pt_dve if j % 2 == 0 else pt_act, 2 * i + j // 2 + 1)
                    if j == 0 and i > 0:
                        pe.wait_ge(a_ready, i)
                    for e in range(2):
                        o = ps[:, 5, (2 * j + e) * HD:(2 * j + e + 1) * HD]
                        mm(o, PT[:, j, 2 * e * P:(2 * e + 1) * P], vA[:, t, g * HD:(g + 1) * HD],
                           start=True, stop=False, skip_group_check=True)
                        ins = mm(o, PT[:, j, P:2 * P], vB[:, e, t, g * HD:(g + 1) * HD],
                                 start=False, stop=True, skip_group_check=True)
                ins.then_inc(pv_done, 1)
            pe.wait_ge(a_ready, 8)
            for t in range(NT):
                if t >= 2:
                    pe.wait_ge(aT_dve, t - 1)
                    pe.wait_ge(aT_act, t - 1)
                for b in range(2):
                    for k in range(4 * b, 4 * b + 4):
                        ins = turn(ps[:, 2 * (t % 2) + b, (k % 4) * P:(k % 4 + 1) * P],
                                   a_rows[:, t, k * P:(k + 1) * P], ident[:, :])
                    ins.then_inc(a_turned, 1)
            chunk_landed(pe, SEQ_POOL)
            pe.wait_ge(u_ready, 8)
            w = chunk(SEQ_POOL, 256)
            for m in range(8):
                g = m // 2
                if m % 2 == 0:
                    pe.wait_ge(d_ready, 2 * g + 2)
                if m >= 4:
                    pe.wait_ge(pT_ready, m - 3)
                for kk in range(2):
                    ins = mm(ps[:, 4 + m % 4, :], w[:, 2 * g + kk, (m % 2) * P:(m % 2 + 1) * P],
                             proj[:, 10 + 2 * g + kk, :], start=(kk == 0), stop=(kk == 1))
                ins.then_inc(pool_done if m < 7 else used, 1)

            pe.wait_ge(aT_dve, 4)
            pe.wait_ge(aT_act, 4)
            pe.wait_ge(pT_ready, 8)
            with pe.Fori(0, 2) as it:
                n = it * 2
                for par in range(2):
                    if par == 1:
                        pe.wait_ge(x_added, n * 4 + 1)
                    for c in range(4):
                        pe.wait_ge(landed[c], n * 16 + 16 * (loads_before[SEQ_OUT + c] + 1 + par))
                        w = slot(c).rearrange("p (k n) -> p k n", n=512)
                        for t in range(NT):
                            for kk in range(4):
                                k = 4 * c + kk
                                ins = mm(ps[:, 4 * par + t, :], H[:, k, t * P:(t + 1) * P], w[:, kk, :],
                                         start=(k == 0), stop=(k == KD - 1))
                            if c == 3 and t < 3:
                                ins.then_inc(o_done, 1)
                        ins.then_inc(used, 1)
                pe.wait_ge(x_added, n * 4 + 4)
            pe.wait_ge(x_added, 16)
            with pe.Fori(0, NT // 2) as it:
                t = it * 2
                for q in range(2):
                    norm_tile(t + (6 + q), q)
            pe.wait_ge(hT_ready, 40)
            for c in range(4):
                chunk_landed(pe, SEQ_XQ + c)
                w = chunk(SEQ_XQ + c, XW)
                for kk in range(4):
                    k = 4 * c + kk
                    for f in range(XH):
                        ins = mm(ps[:, 4 + f, :], w[:, kk, f * P:(f + 1) * P], H[:, k, :],
                                 start=(k == 0), stop=(k == KD - 1))
                        if k == KD - 1 and f < 3:
                            ins.then_inc(xq_done, 1)
                ins.then_inc(used, 1)
            for f in range(XH):
                pe.wait_ge(xq_sq, f + 1)
                mm(ps[:, f, :], ones[:, :], sqx[:, f % 2, :], start=True, stop=True).then_inc(xq_ss, 1)

            def xscores(t):
                if t >= 2:
                    pe.wait_ge(xexp_done, 4 * t - 4)
                for h in range(XH):
                    ins = mm(ps[:, 5 * (t % 2) + h // 2, (h % 2) * NM:(h % 2 + 1) * NM], qx[:, h, t * P:(t + 1) * P],
                             kx[:, h, :], start=True, stop=True, skip_group_check=True)
                ins.then_inc(xs_done, 1)

            def xturn(t):
                pe.wait_ge(xp_ready, t + 1)
                for n in range(8):
                    if n == 0 and t > 0:
                        pe.wait_ge(xpt_act, t)
                    if n == 4 and t > 0:
                        pe.wait_ge(xpt_dve, t)
                    ins = turn(ps[:, 2 + n // 4, (n % 4) * P:(n % 4 + 1) * P],
                               SX[:, t % 2, n * P:(n + 1) * P], ident[:, :])
                    if n % 4 == 3:
                        ins.then_inc(xp_turned, 1)

            def xvalues(t):
                pe.wait_ge(xpt_act, t + 1)
                pe.wait_ge(xpt_dve, t + 1)
                if t >= 2:
                    pe.wait_ge(oT_ready, t - 1)
                for h in range(XH):
                    for m in range(2):
                        ins = mm(ps[:, 4 + 3 * (t % 2), h * P:(h + 1) * P], vx[:, m, h * P:(h + 1) * P],
                                 PTX[:, (2 * h + m) * P:(2 * h + m + 1) * P], start=(m == 0), stop=(m == 1),
                                 skip_group_check=True)
                ins.then_inc(xo_part, 1)

            pe.wait_ge(qx_ready, XH)
            xscores(0)
            xscores(1)
            for t in range(NT):
                xturn(t)
                xvalues(t)
                if t + 2 < NT:
                    xscores(t + 2)
            pe.wait_ge(oT_ready, NT)
            for c in range(4):
                chunk_landed(pe, SEQ_XO + c)
            with pe.Fori(0, 2) as it:
                n = it * 2
                for par in range(2):
                    if par == 1:
                        pe.wait_ge(x_added, n * 4 + 16)
                    for t in range(NT):
                        for c in range(4):
                            ins = mm(ps[:, 4 * par + t, :], H[:, c, t * P:(t + 1) * P],
                                     slot(early[SEQ_XO + c][0])[:, ds(n * 512 + par * 512, 512)],
                                     start=(c == 0), stop=(c == 3))
                        ins.then_inc(o_done, 1)
                pe.wait_ge(x_added, n * 4 + 20)
            pe.wait_ge(x_added, 32)
            for t in range(NT):
                norm_tile(10 + t, t % 2)
            pe.wait_ge(router_in, 16 * (NG + 1))
            for t in range(NT):
                pe.wait_ge(hT_ready, 40 + 4 * t + 4)
                for k in range(KD):
                    ins = mm(ps[:, 4, t * NCOL:(t + 1) * NCOL], H[:, k, t * P:(t + 1) * P], wr[:, k, :],
                             start=(k == 0), stop=(k == KD - 1), skip_group_check=True)
            ins.then_inc(logits_done, 1)
            pe.wait_ge(tri_ready, 1)
            pe.wait_ge(picks, 1)
            for t in range(NT + 1):
                for s in range(min(t + 1, NT)):
                    ins = mm(ps[:, 5, t * NE:(t + 1) * NE], tri if s == t else ones[:, :], rq["M"][:, s, :],
                             start=(s == 0), stop=(s == min(t, NT - 1)), skip_group_check=True)
            ins.then_inc(ranks, 1)
            pe.wait_ge(onehots, 6)
            for n in range(2 * NT):
                k, t = n // NT, n % NT
                ins = mm(ps[0:SLOTS, 6, 0:2 * TCOL], rq["P1" if k == 0 else "P2"][:, t, :],
                         rq["B1" if k == 0 else "B2"][:, t, :], start=(n == 0), stop=(n == 2 * NT - 1))
            ins.then_inc(table_done, 1)

            xs = hs

            def turn_rows(b, par):
                if isinstance(b, int):
                    pe.wait_ge(gathered[par], b * 8 + (16 - 8 * par))
                    wait_past(pe, xsT_ready, b * 2)
                else:
                    rows, copied = pe.to_reg(b * 8 + (16 - 8 * par)), pe.to_reg(b * 2)
                    pe.wait_ge(table_ready, 1)
                    pe.wait_ge(gathered[par], rows)
                    pe.wait_ge(xsT_ready, copied)
                for q in range(2):
                    for k in range(8 * q, 8 * q + 8):
                        ins = turn(ps[:, 2 + q, (k % 8) * SLOTS:(k % 8 + 1) * SLOTS],
                                   xs[0:SLOTS, par, k * P:(k + 1) * P], ident[0:SLOTS, 0:SLOTS])
                    ins.then_inc(xs_turned, 1)

            def expert_landed(b, j):
                s = expert_slot(j)
                pe.wait_ge(landed[s], b * 16 + 16 * (early_loads[s] + 1))

            def block_pe(b, par):
                pe.wait_ge(xsT_ready, b * 2 + 2)
                wait_past(pe, gu_copied, b)
                for c in range(4):
                    for kk in range(4):
                        k = 4 * c + kk
                        for side in range(2):
                            j = 2 * c + side
                            if kk == 0:
                                expert_landed(b, j)
                            w = slot(expert_slot(j)).rearrange("p (k n) -> p k n", n=FF)
                            ins = mm(ps[side * SLOTS:(side + 1) * SLOTS, 0, :], xsT[:, par, k, :], w[:, kk, :],
                                     start=(k == 0), stop=(k == KD - 1), skip_group_check=True)
                            if kk == 3:
                                ins.then_inc(used, 1)
                turn_rows(b + 1, 1 - par)
                pe.wait_ge(gu_copied, b + 1)
                for f in range(KF):
                    ins = turn(guT[:, f, :], gu[:, f * P:(f + 1) * P], ident[:, :])
                ins.then_inc(gu_turned, 1)
                pe.wait_ge(act_ready, b + 1)
                wait_past(pe, y_act, b)
                wait_past(pe, y_dve, b)
                for f in range(KF):
                    expert_landed(b, 8 + f)
                    w = slot(expert_slot(8 + f))
                    for n in range(4):
                        half = slice(n % 2 * SLOTS, (n % 2 + 1) * SLOTS)
                        ins = mm(ps[half, 4 + n, :], act_t[:, f * SLOTS:(f + 1) * SLOTS],
                                 w[:, n * 512:(n + 1) * 512], start=(f == 0), stop=(f == KF - 1))
                    ins.then_inc(used, 1)

            turn_rows(0, 0)
            block_pe(0, 0)
            block_pe(1, 1)
            with pe.Fori(1, NE // 2) as it:
                b = it * 2
                block_pe(b, 0)
                block_pe(b + 1, 1)
            more = pe.value_load(meta[0:1, NOVER:NOVER + 1], min_val=0, max_val=NOVER)
            with pe.If(more > 0):
                with pe.Fori(NE // 2, NBLK // 2) as it:
                    b = it * 2
                    block_pe(b, 0)
                    block_pe(b + 1, 1)


_INS = ['x', 'mem', 'mix_norm_g', 'w_in', 'q_norm_g', 'k_norm_g', 'sink_logits', 'pool_w', 'pool_scale', 'w_out',
        'xattn_norm_g', 'mem_norm_g', 'xq_w', 'xkv_w', 'xq_norm_g', 'xk_norm_g', 'xo_w', 'ffn_norm_g',
        'router_group_w', 'router_group_b', 'router_expert_w', 'router_expert_b', 'expert_w_gate',
        'expert_w_up', 'expert_w_down']
_OUTS = [((1, S, D), 'float32')]


def kernel(**inputs):
    import numpy as _np
    import concourse.bacc as _bacc
    from concourse import mybir as _mybir
    from concourse.bass_utils import run_bass_kernel_spmd as _run

    nc = _bacc.Bacc("TRN2", target_bir_lowering=False, num_devices=1)
    arrays, args = {}, []
    for name in _INS:
        a = _np.ascontiguousarray(inputs[name])
        arrays[f"in_{name}_dram"] = a
        args.append(nc.dram_tensor(f"in_{name}_dram", a.shape, _mybir.dt.from_np(a.dtype), kind="ExternalInput").ap())
    for i, (shape, dtype) in enumerate(_OUTS):
        dt = _mybir.dt.from_np(_np.dtype(dtype))
        args.append(nc.dram_tensor(f"out_{i}_dram", shape, dt, kind="ExternalOutput").ap())
    hybrid_block(nc, *args)
    r = _run(nc, [arrays], core_ids=[0])
    got = tuple(r.results[0][f"out_{i}_dram"] for i in range(len(_OUTS)))
    return got[0]
```

```python
from contextlib import ExitStack

import concourse.bass as bass
from concourse import mybir

P = 128
F32 = mybir.dt.float32
I32 = mybir.dt.int32
U32 = mybir.dt.uint32
ALU = mybir.AluOpType
ACT = mybir.ActivationFunctionType
AX = mybir.AxisListType.X
ds = bass.ds

D = 2048
S = 512
NT = S // P
KD = D // P
HD = 64
NH = 16
CHUNK = 64
WIN = 3 * CHUNK
QKV = 1280
NCT = 18
NM = 256
XW = 512
XH = 4
XD = 128
POOLT = 8
NG, EPG = 4, 8
NE = NG * EPG
FF = 512
KF = FF // P
EPS = 1e-6
NEG = -1e30

SLOTS = 64
MORE = -(-S // SLOTS) - 1
NOVER = 2 * ((2 * S // (SLOTS + 1) + 1) // 2)
NBLK = NE + NOVER
TCOL = NBLK + 2
EMPTY = 8192
CHK = 2048
NSLOT = 12
NA = 4
NCOL = NG + NE


def hybrid_block(nc, x, mem, mix_norm_g, w_in, q_norm_g, k_norm_g, sink_logits, pool_w, pool_scale,
                 w_out, xattn_norm_g, mem_norm_g, xq_w, xkv_w, xq_norm_g, xk_norm_g, xo_w, ffn_norm_g,
                 router_group_w, router_group_b, router_expert_w, router_expert_b,
                 expert_w_gate, expert_w_up, expert_w_down, out):
    hn_dram = nc.dram_tensor("normed_rows", (S, D), F32, kind="Internal").ap()

    with ExitStack() as ctx:
        def sb(name, shape, dt=F32):
            return ctx.enter_context(nc.sbuf_tensor(name, shape, dt))

        def sem(name):
            return ctx.enter_context(nc.semaphore(name))

        ring = sb("weight_ring", [P, NSLOT * CHK])
        X = sb("residual", [P, NT, D])
        H = sb("transposed_acts", [P, KD, S])
        PB = sb("proj_buffer", [P, NCT * S])
        kx = sb("memory_keys_T", [P, XH, NM])
        vx = sb("memory_values", [P, NM // P, XW])
        ident = sb("identity", [P, P])
        ones = sb("ones", [P, P])
        blk = sb("head_blocks", [P, P])
        NGR = 4 * KD + POOLT + 4
        gT = sb("gains_T", [P, NGR])
        stat = sb("norm_stats", [P, 3, 14])
        psq = sb("square_parts", [P, 2, NT, 4])
        eps = sb("eps", [P, 1])
        sink = sb("sink", [P, NH])
        rbias = sb("router_bias", [P, NCOL])
        sm = sb("softmax_stats", [P, 6, 8])
        cols = sb("slot_columns", [SLOTS, 2], I32)
        io = sb("ramp64", [P, 64])
        tok = sb("token_ids", [P, NT])
        ps = ctx.enter_context(nc.psum_tensor("ps", [P, 8, 512], F32))

        def slot(s):
            return ring[:, s * CHK:(s + 1) * CHK]

        hs = PB[:, 0:2 * D].rearrange("p (b d) -> p b d", b=2)
        proj = PB[:, :].rearrange("p (c s) -> p c s", s=S)
        qx = PB[:, 4096:6144].rearrange("p (h s) -> p h s", s=S)
        SX = PB[:, 6144:8192].rearrange("p (b n) -> p b n", b=2)
        sqx = PB[:, 6144:7168].rearrange("p (b n) -> p b n", b=2)
        rtx = PB[:, 7168:8192].rearrange("p (b n) -> p b n", b=2)
        wr = PB[:, 8192:8192 + KD * NCOL].rearrange("p (k c) -> p k c", c=NCOL)
        tri = PB[:, 8768:8896]
        tidx = PB[0:SLOTS, 8896:8896 + TCOL].bitcast(I32)
        tokf = PB[:, 8960:8960 + TCOL]
        gate = PB[:, 9024:9024 + TCOL]
        meta = PB[0:1, 9088:9088 + NOVER + 1].bitcast(I32)
        y = PB[:, 4096:6144].rearrange("p (n c) -> p n c", c=512)
        spread = PB[:, 6144:6656]
        tramp = PB[:, 6656:7168]
        guT = ps[:, 1, :].rearrange("p (f n) -> p f n", n=P)
        dg = PB[:, 7936:8192].rearrange("p (b n) -> p b n", b=2)
        Hf = H[:, :, :].rearrange("p k s -> p (k s)")
        PTX = Hf[:, 4 * S:4 * S + 1024]
        xsT = Hf[:, 0:2 * KD * SLOTS].rearrange("p (b k n) -> p b k n", b=2, n=SLOTS)
        act_t = Hf[:, 2048:2048 + KF * SLOTS]
        sil = Hf[:, 2304:2304 + KF * SLOTS]
        gu = Hf[:, 2560:2560 + FF]
        scr = ring[:, NA * CHK:NSLOT * CHK]
        memx = scr[:, 0:4096].rearrange("p (t d) -> p t d", t=2)
        memT = scr[:, 4096:8192].rearrange("p (k m) -> p k m", m=NM)
        sqm = scr[:, 8192:9216]
        rtm = scr[:, 9216:10240]
        bias = scr[:, 0:3072].rearrange("p (h n) -> p h n", n=WIN)
        Ssb = scr[:, 3072:4608].rearrange("p (h n) -> p h n", n=WIN)
        Spair = scr[:, 3072:4608].rearrange("p (j n) -> p j n", n=2 * WIN)
        PT = scr[:, 4608:6144].rearrange("p (j n) -> p j n", n=384)
        a_rows = scr[:, 6144:10240].rearrange("p (t c) -> p t c", t=NT)
        kdup = scr[:, 10240:11392].rearrange("p (g n) -> p g n", g=2)
        vA = scr[:, 11392:11904].rearrange("p (t c) -> p t c", t=NT)
        sq = scr[:, 12416:13440].rearrange("p (b n) -> p b n", b=2)
        rt = scr[:, 13440:14464].rearrange("p (b n) -> p b n", b=2)
        vB = scr[:, 13440:14464].rearrange("p (e t c) -> p e t c", e=2, t=NT)
        wsum = scr[:, 14464:15520].rearrange("p (b n) -> p b n", b=2)
        vTp = scr[:, 15520:16096]
        ramp = scr[:, 16096:16160].rearrange("p (g n) -> p g n", g=4)
        cnt16 = scr[:, 16160:16176]
        dist = sq[:, 0, 0:WIN]
        mask = sq[:, 1, 0:WIN]

        G_MIX, G_XAT, G_MEM, G_FFN = 0, KD, 2 * KD, 3 * KD
        G_POOL = 4 * KD
        G_Q, G_K, G_XQ, G_XK = (G_POOL + POOLT + j for j in range(4))

        landed = [sem(f"landed{s}") for s in range(NSLOT)]
        used = sem("chunks_used")
        mem_in = [sem("mem_in0"), sem("mem_in1")]
        x_in = [sem(f"x_in{t}") for t in range(NT)]
        gain_in = sem("gain_in")
        small_in = sem("small_in")
        consts = sem("consts")
        eps_set = sem("eps_set")
        gain_turned = sem("gain_turned")
        gains = sem("gains")
        ssq_done = sem("ssq_done")
        root_done = sem("root_done")
        parts_done = sem("square_parts_done")
        rstd_done = sem("rstd_done")
        diag_ready = sem("diag_ready")
        rows_ready = sem("rows_ready")
        h_turned = sem("h_turned")
        hT_ready = sem("hT_ready")
        hn_stored = [sem("hn_stored0"), sem("hn_stored1")]
        xk_sq = sem("xk_sq")
        xk_ss = sem("xk_ss")
        xk_root = sem("xk_root")
        kx_ready = sem("kx_ready")
        vx_ready = sem("vx_ready")
        q_sq = sem("q_sq")
        q_ss = sem("q_ss")
        q_root = sem("q_root")
        q_ready = sem("q_ready")
        q_recip = sem("q_recip")
        k_padded = sem("k_padded")
        k_ready = sem("k_ready")
        v_copied = sem("v_copied")
        v_turned = sem("v_turned")
        v_ready = sem("v_ready")
        bias_built = sem("bias_built")
        bias_reset = sem("bias_reset")
        pool_chain = sem("pool_chain")
        ramp_in = sem("ramp_in")
        ramp_ready = sem("ramp_ready")
        scores_done = sem("scores_done")
        scores_read = sem("scores_read")
        max_done = sem("max_done")
        exp_done = sem("exp_done")
        pt_turned = sem("pt_turned")
        pt_dve = sem("pt_dve")
        pt_act = sem("pt_act")
        pv_done = sem("pv_done")
        a_ready = sem("a_ready")
        u_ready = sem("u_ready")
        d_ready = sem("d_ready")
        a_turned = sem("a_turned")
        aT_act = sem("aT_act")
        aT_dve = sem("aT_dve")
        pool_done = sem("pool_done")
        pT_ready = sem("pT_ready")
        o_done = sem("out_product_done")
        x_added = sem("x_added")
        router_in = sem("router_in")
        tri_ready = sem("tri_ready")
        xq_done = sem("xq_done")
        xq_sq = sem("xq_sq")
        xq_ss = sem("xq_ss")
        xq_root = sem("xq_root")
        qx_ready = sem("qx_ready")
        xs_done = sem("xscores_done")
        xmax_done = sem("xmax_done")
        xexp_done = sem("xexp_done")
        xp_ready = sem("xprobs_ready")
        xp_turned = sem("xprobs_turned")
        xpt_dve = sem("xpt_dve")
        xpt_act = sem("xpt_act")
        xo_part = sem("xo_part")
        oT_ready = sem("oT_ready")
        logits_done = sem("logits_done")
        gmax_done = sem("gmax_done")
        gexp_done = sem("gexp_done")
        top_done = sem("top_done")
        texp_done = sem("texp_done")
        picks = sem("picks")
        ranks = sem("ranks")
        onehots = sem("onehots")
        table_done = sem("table_done")
        table_ready = sem("table_ready")
        xs_clear = sem("xs_clear")
        idx_copied = sem("idx_copied")
        gathered = [sem("gathered0"), sem("gathered1")]
        xs_turned = sem("xs_turned")
        xsT_ready = sem("xsT_ready")
        gu_copied = sem("gu_copied")
        gu_turned = sem("gu_turned")
        sil_ready = sem("sil_ready")
        act_ready = sem("act_ready")
        y_act = sem("y_act")
        y_dve = sem("y_dve")
        tramp_ready = sem("token_ramp_ready")
        spread_ready = sem("spread_ready")
        part_done = sem("part_done")
        part_added = sem("part_added")
        sum_ready = sem("sum_ready")
        stored = sem("stored")
        act_link = sem("act_link")
        dve_link = sem("dve_link")
        pool_link = sem("pool_link")

        xkv_v = xkv_w[0].rearrange("(k p) n -> p k n", p=P)
        w_in_v = w_in[0].rearrange("(k p) n -> p k n", p=P)
        w_out_v = w_out[0].rearrange("(k p) n -> p k n", p=P)
        xq_v = xq_w[0].rearrange("(k p) n -> p k n", p=P)
        xo_v = xo_w[0].rearrange("(k p) n -> p k n", p=P)
        pool_v = pool_w[0].rearrange("g (k p) n -> p (g k) n", p=P)
        early = []
        for half in range(2):
            for c in range(4):
                early.append((c, xkv_v[:, 4 * c:4 * c + 4, half * XW:(half + 1) * XW], XW))
        SEQ_K = len(early)
        SEQ_Q = SEQ_K + 1
        SEQ_V = SEQ_Q + 8
        SEQ_U = SEQ_V + 1
        for ct, s in [(8, 2)] + [(ct, ct % 4) for ct in range(8)] + [(9, 0)] + [(ct, 2 + ct % 2) for ct in range(10, NCT)]:
            early.append((s, w_in_v[:, :, ct * P:(ct + 1) * P], P))
        SEQ_POOL = len(early)
        early.append((1, pool_v, 256))
        SEQ_OUT = len(early)
        for n in range(4):
            for c in range(4):
                early.append((c, w_out_v[:, 4 * c:4 * c + 4, n * 512:(n + 1) * 512], 512))
        SEQ_XQ = len(early)
        for c in range(4):
            early.append((c, xq_v[:, 4 * c:4 * c + 4, :], XW))
        SEQ_XO = len(early)
        for c in range(4):
            early.append((c, xo_v[:, c:c + 1, :], D))
        UE = SEQ_XO
        loads_before = []
        for n, (s, _, _) in enumerate(early):
            loads_before.append(sum(1 for m in range(n) if early[m][0] == s))
        early_loads = [sum(1 for e in early if e[0] == s) for s in range(NSLOT)]

        def wait_past(eng, semaphore, value):
            if not isinstance(value, int) or value > 0:
                eng.wait_ge(semaphore, value)

        def chunk(n, width):
            return slot(early[n][0]).rearrange("p (k n) -> p k n", n=width)

        def chunk_landed(eng, n):
            eng.wait_ge(landed[early[n][0]], 16 * (loads_before[n] + 1))

        rq = {}

        def carve(spec):
            at = 4096
            for name, shape in spec:
                n = 1
                for v in shape:
                    n *= v
                v = PB[:, at:at + n]
                if len(shape) == 2:
                    v = v.rearrange("p (a b) -> p a b", b=shape[1])
                elif len(shape) == 3:
                    v = v.rearrange("p (a b c) -> p a b c", b=shape[1], c=shape[2])
                rq[name] = v
                at += n
            assert at <= 8192, at

        carve([("L", (NT, NCOL)), ("gm", (NT,)), ("gs", (NT, NG)), ("eg", (NT, NG)), ("gsum", (NT,)), ("gg", (NT,)),
               ("gh", (NT, NG)), ("ti", (NT,)), ("t8", (NT, EPG)), ("es", (NT, EPG)),
               ("m1", (NT,)), ("m2", (NT,)), ("h1", (NT, EPG)), ("h2", (NT, EPG)), ("dt", (NT,)), ("et", (NT,)),
               ("w1", (NT,)), ("w2", (NT,)), ("tg", (NT, NG, EPG)), ("M1", (NT, NE)), ("M2", (NT, NE)),
               ("M", (NT, NE)), ("R", (NT + 1, NE)), ("over", (NE,)), ("cmp", (NE, MORE)), ("ca", (16 + NE,)),
               ("cb", (16 + NE,)), ("base", (NE,)), ("pos", (NT,)), ("ob", (NT,)), ("ek", (NT,)), ("pc", (NT, MORE)),
               ("q", (NT,)), ("z", (NT,)), ("row", (NT,)), ("bk", (NT,)), ("cand", (NT, EPG)),
               ("fin", (2 * TCOL,)), ("tmp", (NT, NE)), ("thr", (MORE,)), ("one", (NT, TCOL)), ("val", (NT,)), ("ec", (NOVER, NE)), ("ev", (NOVER + 1,)),
               ("P1", (NT, SLOTS)), ("P2", (NT, SLOTS)), ("B1", (NT, 2 * TCOL)), ("B2", (NT, 2 * TCOL))])

        def head_at(n):
            return 8 * (n // 8) + 2 * (n % 4) + (n % 8) // 4

        WINDOW = (((0, WIN, 0),), ((0, CHUNK, P), (CHUNK, P, 0)))

        block = ctx.enter_context(nc.Block())

        gate_v = expert_w_gate[0].rearrange("e (k p) n -> e p k n", p=P)
        up_v = expert_w_up[0].rearrange("e (k p) n -> e p k n", p=P)
        down_v = expert_w_down[0].rearrange("e (k p) n -> e p k n", p=P)

        def expert_chunk(e, j):
            if j < 8:
                return (gate_v, up_v)[j % 2][ds(e, 1), :, 4 * (j // 2):4 * (j // 2) + 4, :].rearrange(
                    "e p k n -> p (e k) n")
            return down_v[ds(e, 1), :, j - 8:j - 7, :].rearrange("e p k n -> p (e k) n")

        def expert_slot(j):
            return (j + 4) % NSLOT

        @block.sync
        def _(sp):
            for t in range(2):
                sp.dma_start(memx[:, t, :], mem[0, t * P:(t + 1) * P, :]).then_inc(mem_in[t], 16)
            sp.wait_ge(gain_in, 16 * 11)
            for n, (s, src, width) in enumerate(early):
                if n == 4:
                    for t in range(NT):
                        sp.dma_start(X[:, t, :], x[0, t * P:(t + 1) * P, :]).then_inc(x_in[t], 16)
                if n == SEQ_OUT + 4:
                    sp.wait_ge(aT_act, 4)
                    sp.wait_ge(aT_dve, 4)
                    sp.wait_ge(used, SEQ_POOL + 1)
                    sp.wait_ge(d_ready, 8)
                    for j in range(8):
                        sp.dma_start(slot(expert_slot(j)).rearrange("p (k n) -> p k n", n=FF),
                                     expert_chunk(0, j)).then_inc(landed[expert_slot(j)], 16)
                last = [m for m in range(n) if early[m][0] == s]
                if last:
                    sp.wait_ge(used, last[-1] + 1)
                sp.dma_start(slot(s).rearrange("p (k n) -> p k n", n=width), src).then_inc(landed[s], 16)
            for j in range(8, 12):
                s = expert_slot(j)
                sp.wait_ge(o_done, 28)
                sp.dma_start(slot(s).rearrange("p (k n) -> p k n", n=D), expert_chunk(0, j)).then_inc(landed[s], 16)

            def load_expert(e, b):
                for j in range(12):
                    s = expert_slot(j)
                    sp.wait_ge(used, b * 12 + (UE - 12 + j + 1))
                    sp.dma_start(slot(s).rearrange("p (k n) -> p k n", n=FF if j < 8 else D),
                                 expert_chunk(e, j)).then_inc(landed[s], 16)

            with sp.Fori(1, NE) as b:
                load_expert(b, b)
            sp.wait_ge(table_ready, 1)
            more = sp.value_load(meta[0:1, NOVER:NOVER + 1], min_val=0, max_val=NOVER)
            with sp.If(more > 0):
                with sp.Fori(0, NOVER) as j:
                    e = sp.value_load(meta[0:1, ds(j, 1)], min_val=0, max_val=NE - 1)
                    load_expert(e, j + NE)
            for t in range(NT):
                sp.wait_ge(sum_ready, 4 * t + 4)
                sp.dma_start(out[0, t * P:(t + 1) * P, :], X[:, t, :]).then_inc(stored, 16)
            sp.wait_ge(stored, 16 * NT)

        @block.gpsimd
        def _(pool):
            links = [0]

            def link(ins):
                links[0] += 1
                ins.then_inc(pool_link, 1)
                pool.wait_ge(pool_link, links[0])

            g = nc.gpsimd
            g.memset(ones[:, :], 1.0).then_inc(consts, 1)
            g.memset(eps[:, :], EPS).then_inc(eps_set, 1)
            g.iota(io[:, :], pattern=[[1, 64]], base=0, channel_multiplier=0,
                   allow_small_or_imprecise_dtypes=True).then_inc(consts, 1)
            g.iota(tok[:, :], pattern=[[P, NT]], base=0, channel_multiplier=1,
                   allow_small_or_imprecise_dtypes=True).then_inc(consts, 1)
            link(g.memset(ident[:, :], 0.0))
            g.affine_select(out=ident[:, :], in_=ident[:, :], compare_op=ALU.not_equal, fill=1.0, base=0,
                            pattern=[[-1, P]], channel_multiplier=1).then_inc(consts, 1)
            link(g.memset(blk[:, :], 0.0))
            g.memset(blk[0:HD, 0:HD], 1.0).then_inc(consts, 1)
            g.memset(blk[HD:P, HD:P], 1.0).then_inc(consts, 1)

            pool.wait_ge(kx_ready, 2)
            pool.wait_ge(used, 8)
            g.memset(kdup[:, :, 0:CHUNK], 0.0).then_inc(k_padded, 1)
            g.memset(vTp[:, 0:CHUNK], 0.0).then_inc(k_padded, 1)
            link(g.memset(wsum[:, :, 0:16], 0.0))
            g.iota(cnt16, pattern=[[1, 16]], base=1, channel_multiplier=0,
                   allow_small_or_imprecise_dtypes=True).then_inc(ramp_in, 1)
            link(g.iota(mask, pattern=[[-1, WIN]], base=CHUNK, channel_multiplier=1,
                        allow_small_or_imprecise_dtypes=True))
            link(g.tensor_scalar(dist, mask, -1.0, 0.0, ALU.mult, ALU.max))
            link(g.tensor_scalar(mask, mask, 0.0, None, ALU.max))
            link(g.tensor_tensor(dist, dist, mask, ALU.add))
            link(g.memset(mask, 0.0))
            link(g.memset(mask[0:CHUNK, 2 * CHUNK:3 * CHUNK], NEG))
            link(g.memset(mask[CHUNK:P, 0:CHUNK], NEG))
            for h in range(NH):
                slope = 2.0 ** (-8.0 * (head_at(h) + 1) / NH)
                for at, n, col in WINDOW[h % 2]:
                    part = bias[:, h, at:at + n]
                    link(g.tensor_scalar(part, dist[:, col:col + n], -slope, None, ALU.mult))
                    link(g.tensor_tensor(part, part, mask[:, col:col + n], ALU.add))
            pairs = bias.rearrange("p (j e) n -> p j (e n)", e=2)
            before = [pairs[:, :, 0:CHUNK], pairs[:, :, WIN + CHUNK:WIN + 2 * CHUNK]]
            for part in before:
                g.memset(part, NEG).then_inc(bias_built, 1)
            pool.wait_ge(scores_read, 8)
            for part in before:
                g.memset(part[CHUNK:P], NEG).then_inc(bias_reset, 1)
            for h in range(NH):
                slope = 2.0 ** (-8.0 * (head_at(h) + 1) / NH)
                part = before[h % 2][0:CHUNK, h // 2, :]
                link(g.iota(part, pattern=[[-1, CHUNK]], base=CHUNK, channel_multiplier=1,
                            allow_small_or_imprecise_dtypes=True))
                g.tensor_scalar(part, part, -slope, None, ALU.mult).then_inc(bias_reset, 1)

            pool.wait_ge(ramp_ready, 1)
            for i in range(8):
                lv = i // 2 + 1
                w = 2 ** lv
                u = proj[:, 10 + i, :]
                pool.wait_ge(u_ready, i + 1)
                g.tensor_copy(wsum[:, 0, 16:17], u[:, 0:1])
                link(g.tensor_tensor(wsum[:, 0, 17:528], u[:, 1:512], u[:, 0:511], ALU.add))
                for n in range(1, lv):
                    a, b, sh = (n - 1) % 2, n % 2, 2 ** n
                    link(g.tensor_tensor(wsum[:, b, 16:528], wsum[:, a, 16:528],
                                         wsum[:, a, 16 - sh:528 - sh], ALU.add))
                c = (lv - 1) % 2
                link(g.tensor_tensor(wsum[:, c, 16:32], wsum[:, c, 16:32], ramp[:, lv - 1, :], ALU.mult))
                link(g.tensor_scalar(wsum[:, c, 16:528], wsum[:, c, 16:528], 1.0 / w, None, ALU.mult))
                g.tensor_tensor(u, wsum[:, c, 16:528], u, ALU.subtract).then_inc(d_ready, 1)
                pool.wait_ge(d_ready, i + 1)

            pool.wait_ge(used, SEQ_POOL + 1)
            link(g.memset(tri, 1.0))
            g.affine_select(out=tri, in_=tri, compare_op=ALU.is_gt, fill=0.0, base=0,
                            pattern=[[1, P]], channel_multiplier=-1).then_inc(tri_ready, 1)
            for grp in range(NG):
                pool.dma_start(wr[:, :, NG + grp * EPG:NG + (grp + 1) * EPG],
                               router_expert_w[0, grp].rearrange("(k p) e -> p k e", p=P)).then_inc(router_in, 16)
            pool.dma_start(wr[:, :, 0:NG], router_group_w[0].rearrange("(k p) e -> p k e", p=P)).then_inc(router_in, 16)

            for t in range(NT):
                pool.wait_ge(rows_ready, t + 1)
                pool.dma_start(hn_dram[t * P:(t + 1) * P, :], hs[:, t % 2, :]).then_inc(hn_stored[t % 2], 16)
            for b in range(2):
                pool.wait_ge(hn_stored[b], 32)
            pool.wait_ge(h_turned, 4 * 14)
            g.memset(hs[:, :, :], 0.0).then_inc(xs_clear, 1)
            pool.wait_ge(xs_clear, 1)
            pool.wait_ge(table_ready, 1)
            xs = hs

            def reg(value):
                return value if isinstance(value, int) else pool.to_reg(value)

            g.iota(tramp, pattern=[[1, S]], base=0, channel_multiplier=0,
                   allow_small_or_imprecise_dtypes=True).then_inc(tramp_ready, 1)
            g.tensor_copy(cols[:, 0:1], tidx[:, 0:1]).then_inc(idx_copied, 1)
            pool.wait_ge(idx_copied, 1)
            g.indirect_dma_start(out=xs[0:SLOTS, 0, :], out_offset=None, in_=hn_dram,
                                 in_offset=bass.IndirectOffsetOnAxis(ap=cols[:, 0:1], axis=0),
                                 bounds_check=S - 1, oob_is_err=False).then_inc(gathered[0], 16)

            def step(b, par):
                wait_past(pool, xs_turned, b * 2)
                g.tensor_copy(cols[:, 1 - par:2 - par], tidx[:, ds(b + 1, 1)]).then_inc(idx_copied, 1)
                copied = reg(b + 2)
                pool.wait_ge(table_ready, 1)
                pool.wait_ge(idx_copied, copied)
                g.indirect_dma_start(out=xs[0:SLOTS, 1 - par, :], out_offset=None, in_=hn_dram,
                                     in_offset=bass.IndirectOffsetOnAxis(ap=cols[:, 1 - par:2 - par], axis=0),
                                     bounds_check=S - 1, oob_is_err=False).then_inc(gathered[1 - par], 16)

            step(0, 0)
            step(1, 1)
            with pool.Fori(1, NE // 2) as it:
                b = it * 2
                step(b, 0)
                step(b + 1, 1)
            pool.wait_ge(gathered[0], 16 * (NE // 2 + 1))
            more = pool.value_load(meta[0:1, NOVER:NOVER + 1], min_val=0, max_val=NOVER)
            with pool.If(more > 0):
                with pool.Fori(NE // 2, NBLK // 2) as it:
                    b = it * 2
                    step(b, 0)
                    step(b + 1, 1)
                pool.wait_ge(gathered[0], 16 * (NBLK // 2 + 1))

        @block.scalar
        def _(act):
            a = nc.scalar
            links = [0]

            def link(ins):
                links[0] += 1
                ins.then_inc(act_link, 1)
                act.wait_ge(act_link, links[0])

            grow = PB[0:NGR, 8192:8192 + P]
            for r0, v in ((G_MIX, mix_norm_g), (G_XAT, xattn_norm_g), (G_MEM, mem_norm_g), (G_FFN, ffn_norm_g),
                          (G_POOL, pool_scale)):
                act.dma_start(grow[r0:r0 + v.shape[1] // P, :], v[0].rearrange("(k p) -> k p", p=P)).then_inc(gain_in, 16)
            for r0, v in ((G_Q, q_norm_g), (G_K, k_norm_g)):
                for c in range(2):
                    act.dma_start(grow[r0:r0 + 1, c * HD:(c + 1) * HD], v[0:1, :]).then_inc(gain_in, 16)
            for r0, v in ((G_XQ, xq_norm_g), (G_XK, xk_norm_g)):
                act.dma_start(grow[r0:r0 + 1, :], v[0:1, :]).then_inc(gain_in, 16)
            act.dma_start(sink[:, :], sink_logits[0:1, :].broadcast_to([P, NH])).then_inc(small_in, 16)
            act.dma_start(rbias[:, 0:NG], router_group_b[0:1, :].broadcast_to([P, NG])).then_inc(small_in, 16)
            act.dma_start(rbias[:, NG:NCOL], router_expert_b.rearrange("l g e -> l (g e)").broadcast_to([P, NE])
                          ).then_inc(small_in, 16)
            act.wait_ge(eps_set, 1)

            def root_of(T):
                act.wait_ge(ssq_done, T + 1)
                a.activation(stat[:, 1, T:T + 1], stat[:, 0, T:T + 1], ACT.Sqrt, bias=eps[:, 0:1],
                             scale=1.0 / D).then_inc(root_done, 1)

            def square_sum(T, src):
                a.activation(hs[:, T % 2, :], src, ACT.Square, accum_out=stat[:, 0, T:T + 1]).then_inc(ssq_done, 1)

            def square_parts(stage):
                with act.Fori(0, 4) as n:
                    for t in range(NT):
                        act.wait_ge(x_added, n * 4 + (16 * stage + t + 1))
                        a.activation(hs[:, 0, t * 512:(t + 1) * 512], X[:, t, ds(n * 512, 512)], ACT.Square,
                                     accum_out=psq[:, stage, t, ds(n, 1)]).then_inc(parts_done, 1)
                    act.wait_ge(parts_done, n * 4 + (16 * stage + 4))

            for t in range(2):
                act.wait_ge(mem_in[t], 16)
                square_sum(t, memx[:, t, :])
                root_of(t)
            for t in range(NT):
                act.wait_ge(x_in[t], 16)
                square_sum(2 + t, X[:, t, :])
                root_of(2 + t)
            act.wait_ge(used, 4)
            for b in range(2):
                a.activation(sqm[:, b * 512:(b + 1) * 512], ps[:, 4 + b, :], ACT.Square).then_inc(xk_sq, 1)
            for b in range(2):
                act.wait_ge(xk_ss, b + 1)
                a.activation(rtm[:, b * 512:(b + 1) * 512], ps[:, b, :], ACT.Sqrt, bias=eps[:, 0:1],
                             scale=1.0 / XD).then_inc(xk_root, 1)
            act.wait_ge(used, 8)
            for m in range(2):
                a.activation(vx[:, m, :], ps[:, 6 + m, :], ACT.Copy).then_inc(vx_ready, 1)

            def squares(n, bank, b):
                act.wait_ge(used, n + (SEQ_K + 1))
                a.activation(sq[:, b, :], ps[:, bank, :], ACT.Square).then_inc(q_sq, 1)

            def root(n, bank, b):
                act.wait_ge(q_ss, n + 1)
                a.activation(rt[:, b, :], ps[:, bank, :], ACT.Sqrt, bias=eps[:, 0:1], scale=1.0 / HD).then_inc(q_root, 1)

            act.wait_ge(bias_built, 2)
            act.wait_ge(kx_ready, 2)
            squares(0, 7, 0)
            root(0, 3, 0)
            with act.Fori(0, 2) as it:
                n = it * 4
                for s in range(4):
                    act.wait_ge(q_ss, n + (s + 1))
                    squares(n + (s + 1), 4 + s, (s + 1) % 2)
                    act.wait_ge(q_ready, n + (s + 1))
                    root(n + (s + 1), s, (s + 1) % 2)
            act.wait_ge(used, SEQ_V + 1)
            a.activation(vTp[:, CHUNK:CHUNK + S], ps[:, 5, :], ACT.Copy).then_inc(v_copied, 1)
            act.wait_ge(v_turned, 2)
            a.activation(vA[:, :, :], ps[:, 6, :].rearrange("p (t c) -> p t c", t=NT), ACT.Copy).then_inc(v_ready, 1)

            for i in range(8):
                act.wait_ge(max_done, 2 * i + 2)
                for h in range(8):
                    a.activation(Ssb[:, h, :], Ssb[:, h, :], ACT.Exp, bias=sm[:, 1, h:h + 1],
                                 accum_out=sm[:, 2, h:h + 1]).then_inc(exp_done, 1)
                a.activation(sm[:, 4, :], sm[:, 3, :], ACT.Exp).then_inc(exp_done, 1)
                act.wait_ge(used, SEQ_U + i + 1)
                a.activation(proj[:, 10 + i, :], ps[:, 4, :], ACT.Copy).then_inc(u_ready, 1)
                for j in (1, 3):
                    act.wait_ge(pt_turned, 4 * i + j + 1)
                    a.activation(PT[:, j, :], ps[:, j, 0:384], ACT.Copy).then_inc(pt_act, 1)
            for tt in range(NT):
                act.wait_ge(a_turned, 2 * tt + 2)
                b = 2 * (tt % 2) + 1
                a.activation(H[:, 4:8, tt * P:(tt + 1) * P], ps[:, b, :].rearrange("p (k n) -> p k n", n=P),
                             ACT.Copy).then_inc(aT_act, 1)
            for m in range(8):
                act.wait_ge(*((pool_done, m + 1) if m < 7 else (used, SEQ_POOL + 1)))
                a.activation(H[:, 8 + m, :], ps[:, 4 + m % 4, :], ACT.Copy,
                             scale=gT[:, G_POOL + m:G_POOL + m + 1]).then_inc(pT_ready, 1)

            square_parts(0)
            for t in range(NT):
                root_of(6 + t)
            for f in range(XH):
                act.wait_ge(*((xq_done, f + 1) if f < 3 else (used, SEQ_XQ + 4)))
                if f >= 2:
                    act.wait_ge(xq_ss, f - 1)
                a.activation(sqx[:, f % 2, :], ps[:, 4 + f, :], ACT.Square).then_inc(xq_sq, 1)
                act.wait_ge(xq_ss, f + 1)
                if f >= 2:
                    act.wait_ge(qx_ready, f - 1)
                a.activation(rtx[:, f % 2, :], ps[:, f, :], ACT.Sqrt, bias=eps[:, 0:1], scale=1.0 / XD
                             ).then_inc(xq_root, 1)
            act.wait_ge(qx_ready, XH)

            def xexps(t):
                act.wait_ge(xmax_done, t + 1)
                for h in range(XH):
                    c = (t % 2) * 4 + h
                    a.activation(SX[:, t % 2, h * NM:(h + 1) * NM],
                                 ps[:, 5 * (t % 2) + h // 2, (h % 2) * NM:(h % 2 + 1) * NM], ACT.Exp,
                                 bias=sm[:, 1, c:c + 1], scale=XD ** -0.5,
                                 accum_out=sm[:, 2, c:c + 1]).then_inc(xexp_done, 1)

            xexps(0)
            for t in range(NT):
                if t + 1 < NT:
                    xexps(t + 1)
                act.wait_ge(xp_turned, 2 * t + 1)
                a.activation(PTX[:, 0:512], ps[:, 2, :], ACT.Copy).then_inc(xpt_act, 1)

            square_parts(1)
            for t in range(NT):
                root_of(10 + t)
            for t in range(NT):
                act.wait_ge(rstd_done, 10 + t + 1)
                if t >= 2:
                    act.wait_ge(hn_stored[t % 2], 16)
                a.activation(hs[:, t % 2, :], X[:, t, :], ACT.Copy, scale=stat[:, 2, 10 + t:11 + t]).then_inc(rows_ready, 1)

            act.wait_ge(gmax_done, 1)
            a.activation(rq["eg"], rq["gs"], ACT.Exp).then_inc(gexp_done, 1)
            act.wait_ge(top_done, 1)
            a.activation(rq["et"], rq["dt"], ACT.Exp).then_inc(texp_done, 1)

            def block_act(b, par):
                act.wait_ge(used, b * 12 + (UE + 8))
                a.activation(gu, ps[:, 0, :], ACT.Copy).then_inc(gu_copied, 1)
                act.wait_ge(gu_turned, b + 1)
                wait_past(act, act_ready, b)
                a.activation(sil.rearrange("p (f n) -> p f n", n=SLOTS), guT[:, :, 0:SLOTS],
                             ACT.Silu).then_inc(sil_ready, 1)
                act.wait_ge(used, b * 12 + (UE + 12))
                a.activation(y[par * SLOTS:(par + 1) * SLOTS, 0:4:2, :], ps[0:SLOTS, 4:6, :], ACT.Copy).then_inc(y_act, 1)

            act.wait_ge(table_ready, 1)
            block_act(0, 0)
            block_act(1, 1)
            with act.Fori(1, NE // 2) as it:
                b = it * 2
                block_act(b, 0)
                block_act(b + 1, 1)
            more = act.value_load(meta[0:1, NOVER:NOVER + 1], min_val=0, max_val=NOVER)
            with act.If(more > 0):
                with act.Fori(NE // 2, NBLK // 2) as it:
                    b = it * 2
                    block_act(b, 0)
                    block_act(b + 1, 1)

        @block.vector
        def _(dve):
            v = nc.vector
            links = [0]

            def link(ins):
                links[0] += 1
                ins.then_inc(dve_link, 1)
                dve.wait_ge(dve_link, links[0])

            def wide(ap, *shape):
                return ap.broadcast_to(list(shape))

            def scale_of(T):
                dve.wait_ge(root_done, T + 1)
                v.reciprocal(stat[:, 2, T:T + 1], stat[:, 1, T:T + 1]).then_inc(rstd_done, 1)
                dve.wait_ge(rstd_done, T + 1)
                if T >= 2:
                    dve.wait_ge(h_turned, 4 * T - 4)
                v.tensor_scalar(dg[:, T % 2, :], ident[:, :], stat[:, 2, T:T + 1], None, ALU.mult).then_inc(diag_ready, 1)

            def sum_parts(T, stage):
                dve.wait_ge(parts_done, 16 * stage + 12 + (T - 6) % 4 + 1)
                v.tensor_reduce(stat[:, 0, T:T + 1], psq[:, stage, (T - 6) % 4, :], AX, ALU.add).then_inc(ssq_done, 1)

            def turned(T, dstT, at, gcol):
                for b in range(4):
                    dve.wait_ge(h_turned, T * 4 + b + 1)
                    v.tensor_tensor(dstT[:, 4 * b:4 * b + 4, at:at + P],
                                    ps[:, b, :].rearrange("p (k n) -> p k n", n=P),
                                    wide(gT[:, gcol + 4 * b:gcol + 4 * b + 4].unsqueeze(2), P, 4, P),
                                    ALU.mult).then_inc(hT_ready, 1)

            def norm_tiles(T0, count, dstT, gcol):
                for t in range(min(2, count)):
                    scale_of(T0 + t)
                for t in range(count):
                    turned(T0 + t, dstT, t * P, gcol)
                    if t + 2 < count:
                        scale_of(T0 + t + 2)

            dve.wait_ge(gain_turned, 1)
            v.tensor_copy(gT[:, :], ps[:, 7, 0:NGR]).then_inc(gains, 1)
            dve.wait_ge(gains, 1)
            norm_tiles(0, 2, memT, G_MEM)
            for b in range(2):
                dve.wait_ge(xk_root, b + 1)
                link(v.reciprocal(rtm[:, b * 512:(b + 1) * 512], rtm[:, b * 512:(b + 1) * 512]))
                v.scalar_tensor_tensor(out=kx[:, 2 * b:2 * b + 2, :].rearrange("p h n -> p (h n)"),
                                       in0=ps[:, 4 + b, :], scalar=gT[:, G_XK:G_XK + 1],
                                       in1=rtm[:, b * 512:(b + 1) * 512],
                                       op0=ALU.mult, op1=ALU.mult).then_inc(kx_ready, 1)
            norm_tiles(2, NT, H, G_MIX)
            dve.wait_ge(ramp_in, 1)
            for lv in range(4):
                w = float(2 ** (lv + 1))
                link(v.tensor_scalar(ramp[:, lv, :], cnt16, w, None, ALU.min))
                link(v.reciprocal(ramp[:, lv, :], ramp[:, lv, :]))
                r = v.tensor_scalar(ramp[:, lv, :], ramp[:, lv, :], w, None, ALU.mult)
                if lv < 3:
                    link(r)
            r.then_inc(ramp_ready, 1)

            dve.wait_ge(q_root, 1)
            link(v.reciprocal(rt[:, 0, :], rt[:, 0, :]))
            dve.wait_ge(k_padded, 2)
            for g in range(2):
                half = slice(g * HD, (g + 1) * HD)
                ins = v.scalar_tensor_tensor(out=kdup[half, g, CHUNK:CHUNK + S], in0=ps[half, 7, :],
                                             scalar=gT[half, G_K:G_K + 1], in1=rt[half, 0, :],
                                             op0=ALU.mult, op1=ALU.mult)
                if g == 0:
                    link(ins)
            ins.then_inc(q_ready, 1)
            dve.wait_ge(q_ready, 1)
            for g in range(2):
                v.tensor_copy(kdup[(1 - g) * HD:(2 - g) * HD, g, CHUNK:CHUNK + S],
                              kdup[g * HD:(g + 1) * HD, g, CHUNK:CHUNK + S]).then_inc(k_ready, 1)
            with dve.Fori(0, 2) as it:
                n = it * 4
                for s in range(4):
                    b = (s + 1) % 2
                    dve.wait_ge(q_root, n + (s + 2))
                    v.reciprocal(rt[:, b, :], rt[:, b, :]).then_inc(q_recip, 1)
                    dve.wait_ge(q_recip, n + (s + 1))
                    v.scalar_tensor_tensor(out=proj[:, ds(n + s, 1), :].rearrange("p a n -> p (a n)"),
                                           in0=ps[:, 4 + s, :], scalar=gT[:, G_Q:G_Q + 1], in1=rt[:, b, :],
                                           op0=ALU.mult, op1=ALU.mult).then_inc(q_ready, 1)
            dve.wait_ge(q_ready, 9)
            link(v.memset(vB[:, :, :, :], 0.0))

            for i in range(8):
                t, g = i // 2, i % 2
                if i == 0:
                    dve.wait_ge(bias_built, 2)
                    dve.wait_ge(small_in, 48)
                if i == 2:
                    dve.wait_ge(bias_reset, 2 + NH)
                for n, j in enumerate((0, 2, 1, 3)):
                    dve.wait_ge(scores_done, 4 * i + n + 1)
                    v.scalar_tensor_tensor(out=Ssb[:, 2 * j:2 * j + 2, :],
                                           in0=ps[:, j, 0:2 * WIN].rearrange("p (h n) -> p h n", n=WIN),
                                           scalar=HD ** -0.5, in1=bias[:, 8 * g + 2 * j:8 * g + 2 * j + 2, :],
                                           op0=ALU.mult, op1=ALU.add).then_inc(scores_read, 1)
                dve.wait_ge(scores_read, 4 * i + 4)
                link(v.tensor_reduce(sm[:, 0, :], Ssb[:, :, :], AX, ALU.max))
                sinks = sink[:, 8 * g:8 * g + 8].rearrange("p (a b) -> p b a", b=2)
                smv = sm[:, :, :].rearrange("p r (b a) -> p r b a", b=2)
                link(v.tensor_tensor(smv[:, 0], smv[:, 0], sinks, ALU.max))
                v.tensor_scalar(sm[:, 1, :], sm[:, 0, :], -1.0, None, ALU.mult).then_inc(max_done, 1)
                v.tensor_tensor(smv[:, 3], sinks, smv[:, 0], ALU.subtract).then_inc(max_done, 1)
                if i == 0:
                    dve.wait_ge(v_turned, 2)
                    for g_ in range(2):
                        v.tensor_copy(vB[g_ * HD:(g_ + 1) * HD, g_, :, :],
                                      ps[0:HD, 7, :].rearrange("p (t c) -> p t c", t=NT)).then_inc(v_ready, 1)
                dve.wait_ge(exp_done, 9 * i + 9)
                link(v.tensor_tensor(sm[:, 5, :], sm[:, 2, :], sm[:, 4, :], ALU.add))
                link(v.reciprocal(sm[:, 5, :], sm[:, 5, :]))
                for j in (0, 2):
                    dve.wait_ge(pt_turned, 4 * i + j + 1)
                    v.tensor_copy(PT[:, j, :], ps[:, j, 0:384]).then_inc(pt_dve, 1)
                dve.wait_ge(pv_done, i + 1)
                v.tensor_tensor(a_rows[:, t, g * 512:(g + 1) * 512].rearrange("p (a b d) -> p b a d", b=2, d=HD),
                                ps[:, 5, :].rearrange("p (b a d) -> p b a d", b=2, d=HD),
                                wide(smv[:, 5].unsqueeze(3), P, 2, 4, HD), ALU.mult).then_inc(a_ready, 1)
            for tt in range(NT):
                dve.wait_ge(a_turned, 2 * tt + 1)
                v.tensor_copy(H[:, 0:4, tt * P:(tt + 1) * P],
                              ps[:, 2 * (tt % 2), :].rearrange("p (k n) -> p k n", n=P)).then_inc(aT_dve, 1)

            def add_out(n, par, cross):
                for t in range(NT):
                    if cross:
                        dve.wait_ge(o_done, n * 4 + (12 + t + 1))
                    elif t < 3:
                        dve.wait_ge(o_done, n * 3 + (t + 1))
                    else:
                        dve.wait_ge(used, n * 4 + (SEQ_OUT + 4))
                    xs_ = X[:, t, ds(n * 512, 512)]
                    v.tensor_tensor(xs_, ps[:, 4 * par + t, :], xs_, ALU.add).then_inc(x_added, 1)

            for t in range(NT):
                dve.wait_ge(x_in[t], 16)
            with dve.Fori(0, 2) as it:
                n = it * 2
                for par in range(2):
                    add_out(n + par, par, False)

            for t in range(NT):
                sum_parts(6 + t, 0)
            norm_tiles(6, NT, H, G_XAT)
            for f in range(XH):
                dve.wait_ge(xq_root, f + 1)
                link(v.reciprocal(rtx[:, f % 2, :], rtx[:, f % 2, :]))
                v.scalar_tensor_tensor(out=qx[:, f, :], in0=ps[:, 4 + f, :], scalar=gT[:, G_XQ:G_XQ + 1],
                                       in1=rtx[:, f % 2, :], op0=ALU.mult, op1=ALU.mult).then_inc(qx_ready, 1)

            def xmax(t):
                c = slice(4 * (t % 2), 4 * (t % 2) + 4)
                dve.wait_ge(xs_done, t + 1)
                b0 = 5 * (t % 2)
                link(v.tensor_reduce(sm[:, 0, c], ps[:, b0:b0 + 2, :].rearrange("p b (h n) -> p (b h) n", n=NM),
                                     AX, ALU.max))
                v.tensor_scalar(sm[:, 1, c], sm[:, 0, c], -(XD ** -0.5), None, ALU.mult).then_inc(xmax_done, 1)

            def xnorm(t):
                c = slice(4 * (t % 2), 4 * (t % 2) + 4)
                dve.wait_ge(xexp_done, 4 * t + 4)
                link(v.reciprocal(sm[:, 5, c], sm[:, 2, c]))
                sx = SX[:, t % 2, :].rearrange("p (h n) -> p h n", n=NM)
                v.tensor_tensor(sx, sx, wide(sm[:, 5, c].unsqueeze(2), P, XH, NM), ALU.mult).then_inc(xp_ready, 1)

            xmax(0)
            xnorm(0)
            xmax(1)
            for t in range(NT):
                dve.wait_ge(xp_turned, 2 * t + 2)
                v.tensor_copy(PTX[:, 512:1024], ps[:, 3, :]).then_inc(xpt_dve, 1)
                dve.wait_ge(xo_part, t + 1)
                v.tensor_copy(H[:, 0:XH, t * P:(t + 1) * P],
                              ps[:, 4 + 3 * (t % 2), :].rearrange("p (h n) -> p h n", n=P)).then_inc(oT_ready, 1)
                if t + 1 < NT:
                    xnorm(t + 1)
                if t + 2 < NT:
                    xmax(t + 2)
            with dve.Fori(0, 2) as it:
                n = it * 2
                for par in range(2):
                    add_out(n + par, par, True)
            for t in range(NT):
                sum_parts(10 + t, 1)
            norm_tiles(10, NT, H, G_FFN)

            r = rq
            dve.wait_ge(logits_done, 1)
            link(v.tensor_tensor(r["L"], ps[:, 4, 0:NT * NCOL].rearrange("p (t c) -> p t c", c=NCOL),
                                 wide(rbias[:, :].unsqueeze(1), P, NT, NCOL), ALU.add))
            LG = r["L"][:, :, 0:NG]
            LE = r["L"][:, :, NG:NCOL].rearrange("p t (g e) -> p t g e", e=EPG)

            def top(vals, width, best, pick, cand):
                link(v.tensor_reduce(best, vals, AX, ALU.max))
                link(v.tensor_tensor(pick, vals, wide(best.unsqueeze(2), P, NT, width), ALU.is_equal))
                link(v.scalar_tensor_tensor(out=cand, in0=pick, scalar=-64.0,
                                            in1=wide(io[:, 0:width].unsqueeze(1), P, NT, width),
                                            op0=ALU.mult, op1=ALU.add))
                link(v.tensor_reduce(r["ti"], cand, AX, ALU.min))
                link(v.tensor_scalar(r["ti"], r["ti"], 64.0, None, ALU.add))
                link(v.tensor_tensor(pick, wide(io[:, 0:width].unsqueeze(1), P, NT, width),
                                     wide(r["ti"].unsqueeze(2), P, NT, width), ALU.is_equal))

            top(LG, NG, r["gm"], r["gh"], r["cand"][:, :, 0:NG])
            v.tensor_tensor(r["gs"], LG, wide(r["gm"].unsqueeze(2), P, NT, NG), ALU.subtract).then_inc(gmax_done, 1)
            link(v.tensor_tensor(r["tg"], LE, wide(r["gh"].unsqueeze(3), P, NT, NG, EPG), ALU.mult))
            link(v.tensor_reduce(r["es"], r["tg"].rearrange("p t g e -> p t e g"), AX, ALU.add))
            top(r["es"], EPG, r["m1"], r["h1"], r["cand"])
            link(v.scalar_tensor_tensor(out=r["t8"], in0=r["h1"], scalar=NEG, in1=r["es"], op0=ALU.mult, op1=ALU.add))
            top(r["t8"], EPG, r["m2"], r["h2"], r["cand"])
            v.tensor_tensor(r["dt"], r["m2"], r["m1"], ALU.subtract).then_inc(top_done, 1)
            for k, name in enumerate(("M1", "M2")):
                link(v.tensor_tensor(r[name].rearrange("p t (g e) -> p t g e", e=EPG),
                                     wide(r["gh"].unsqueeze(3), P, NT, NG, EPG),
                                     wide(r["h1" if k == 0 else "h2"].unsqueeze(2), P, NT, NG, EPG), ALU.mult))
            v.tensor_tensor(r["M"], r["M1"], r["M2"], ALU.add).then_inc(picks, 1)
            dve.wait_ge(gexp_done, 1)
            link(v.tensor_reduce(r["gsum"], r["eg"], AX, ALU.add))
            link(v.reciprocal(r["gg"], r["gsum"]))
            dve.wait_ge(texp_done, 1)
            link(v.tensor_scalar(r["w2"], r["et"], 1.0, None, ALU.add))
            link(v.reciprocal(r["w2"], r["w2"]))
            link(v.tensor_tensor(r["w1"], r["gg"], r["w2"], ALU.mult))
            link(v.tensor_tensor(r["w2"], r["w1"], r["et"], ALU.mult))
            dve.wait_ge(ranks, 1)
            link(v.tensor_copy(r["R"], ps[:, 5, 0:(NT + 1) * NE].rearrange("p (t e) -> p t e", e=NE)))
            link(v.tensor_scalar(r["thr"], io[:, 1:1 + MORE], float(SLOTS), None, ALU.mult))
            link(v.tensor_tensor(r["cmp"], wide(r["R"][:, NT, :].unsqueeze(2), P, NE, MORE),
                                 wide(r["thr"].unsqueeze(1), P, NE, MORE), ALU.is_gt))
            link(v.tensor_reduce(r["over"], r["cmp"], AX, ALU.add))
            link(v.memset(r["ca"], 0.0))
            link(v.memset(r["cb"], 0.0))
            link(v.tensor_copy(r["ca"][:, 16:16 + NE], r["over"]))
            src, dst = r["ca"], r["cb"]
            for sh in (1, 2, 4, 8, 16):
                link(v.tensor_tensor(dst[:, 16:16 + NE], src[:, 16:16 + NE], src[:, 16 - sh:16 + NE - sh], ALU.add))
                src, dst = dst, src
            upto = src[:, 16:16 + NE]
            link(v.tensor_tensor(r["base"], upto, r["over"], ALU.subtract))
            for k in range(2):
                M = r["M1" if k == 0 else "M2"]

                def of_pick(dst_, table):
                    link(v.tensor_tensor(r["tmp"], table, M, ALU.mult))
                    link(v.tensor_reduce(dst_, r["tmp"], AX, ALU.add))

                of_pick(r["pos"], r["R"][:, 0:NT, :])
                of_pick(r["ob"], wide(r["base"].unsqueeze(1), P, NT, NE))
                of_pick(r["ek"], wide(io[:, 0:NE].unsqueeze(1), P, NT, NE))
                link(v.tensor_tensor(r["pc"], wide(r["pos"].unsqueeze(2), P, NT, MORE),
                                     wide(r["thr"].unsqueeze(1), P, NT, MORE), ALU.is_ge))
                link(v.tensor_reduce(r["q"], r["pc"], AX, ALU.add))
                link(v.scalar_tensor_tensor(out=r["row"], in0=r["q"], scalar=-float(SLOTS), in1=r["pos"],
                                            op0=ALU.mult, op1=ALU.add))
                link(v.tensor_scalar(r["z"], r["q"], 0.0, None, ALU.is_equal))
                link(v.scalar_tensor_tensor(out=r["bk"], in0=r["ob"], scalar=float(NE - 1), in1=r["q"],
                                            op0=ALU.add, op1=ALU.add))
                link(v.tensor_tensor(r["ek"], r["ek"], r["bk"], ALU.subtract))
                link(v.tensor_tensor(r["ek"], r["ek"], r["z"], ALU.mult))
                link(v.tensor_tensor(r["bk"], r["bk"], r["ek"], ALU.add))
                v.tensor_tensor(r["P1" if k == 0 else "P2"], wide(io[:, 0:SLOTS].unsqueeze(1), P, NT, SLOTS),
                                wide(r["row"].unsqueeze(2), P, NT, SLOTS), ALU.is_equal).then_inc(onehots, 1)
                link(v.tensor_tensor(r["one"], wide(io[:, 0:TCOL].unsqueeze(1), P, NT, TCOL),
                                     wide(r["bk"].unsqueeze(2), P, NT, TCOL), ALU.is_equal))
                link(v.tensor_scalar(r["val"], tok[:, :], 2.0, float(k + 1), ALU.mult, ALU.add))
                B = r["B1" if k == 0 else "B2"]
                v.tensor_tensor(B[:, :, 0:TCOL], r["one"], wide(r["val"].unsqueeze(2), P, NT, TCOL),
                                ALU.mult).then_inc(onehots, 1)
                v.tensor_tensor(B[:, :, TCOL:2 * TCOL], r["one"],
                                wide(r["w1" if k == 0 else "w2"].unsqueeze(2), P, NT, TCOL),
                                ALU.mult).then_inc(onehots, 1)
                dve.wait_ge(onehots, 3 * k + 3)
            link(v.tensor_tensor(r["ec"], wide(upto.unsqueeze(1), P, NOVER, NE),
                                 wide(io[:, 0:NOVER].unsqueeze(2), P, NOVER, NE), ALU.is_le))
            link(v.tensor_reduce(r["ev"][:, 0:NOVER], r["ec"], AX, ALU.add))
            link(v.tensor_scalar(r["ev"][:, 0:NOVER], r["ev"][:, 0:NOVER], float(NE - 1), None, ALU.min))
            link(v.tensor_copy(r["ev"][:, NOVER:NOVER + 1], upto[:, NE - 1:NE]))
            link(v.tensor_copy(meta, r["ev"][0:1, :]))
            dve.wait_ge(table_done, 1)
            link(v.tensor_copy(r["fin"][0:SLOTS, :], ps[0:SLOTS, 6, 0:2 * TCOL]))
            V = r["fin"][0:SLOTS, 0:TCOL]
            link(v.tensor_copy(gate[0:SLOTS, :], r["fin"][0:SLOTS, TCOL:2 * TCOL]))
            link(v.tensor_copy(gate[SLOTS:P, 0:TCOL - 1], r["fin"][0:SLOTS, TCOL + 1:2 * TCOL]))
            zero = r["one"][0:SLOTS, 0, :]
            yidx = r["one"][0:SLOTS, 1, :].bitcast(I32)
            link(v.tensor_scalar(zero, V, 0.0, float(EMPTY), ALU.is_equal, ALU.mult))
            link(v.scalar_tensor_tensor(out=V, in0=V, scalar=-1.0, in1=zero, op0=ALU.add, op1=ALU.add))
            link(v.tensor_copy(yidx, V))
            link(v.tensor_scalar(tidx, yidx, 1, None, ALU.logical_shift_right))
            link(v.tensor_copy(tokf[0:SLOTS, :], tidx))
            v.tensor_copy(tokf[SLOTS:P, 0:TCOL - 1], tidx[:, 1:TCOL]).then_inc(table_ready, 1)

            def turn_evac(b, par):
                for q in range(2):
                    dve.wait_ge(xs_turned, b * 2 + (q + 1))
                    v.tensor_tensor(xsT[:, par, 8 * q:8 * q + 8, :],
                                    ps[:, 2 + q, 0:8 * SLOTS].rearrange("p (k n) -> p k n", n=SLOTS),
                                    wide(gT[:, G_FFN + 8 * q:G_FFN + 8 * q + 8].unsqueeze(2), P, 8, SLOTS),
                                    ALU.mult).then_inc(xsT_ready, 1)

            def add_parts(added, half, last=False):
                for i in range(8 * half, 8 * half + 8):
                    t, n = i // 4, i % 4
                    dve.wait_ge(part_done, added + (i + 1))
                    v.tensor_tensor(X[:, t, n * 512:(n + 1) * 512], ps[:, 6 + i % 2, :], X[:, t, n * 512:(n + 1) * 512],
                                    ALU.add).then_inc(sum_ready if last else part_added, 1)

            def block_dve(b, par, pair):
                if par == 0 and pair is not None:
                    turn_evac(b + 1, 1 - par)
                    add_parts(pair * 16 - 16, 0)
                dve.wait_ge(sil_ready, b + 1)
                v.tensor_tensor(act_t.rearrange("p (f n) -> p f n", n=SLOTS), sil.rearrange("p (f n) -> p f n", n=SLOTS),
                                guT[:, :, SLOTS:2 * SLOTS], ALU.mult).then_inc(act_ready, 1)
                if par == 0 and pair is not None:
                    add_parts(pair * 16 - 16, 1)
                else:
                    turn_evac(b + 1, 1 - par)
                if par == 1:
                    v.tensor_scalar(spread, tramp, tokf[:, ds(b - 1, 1)], gate[:, ds(b - 1, 1)],
                                    ALU.is_equal, ALU.mult).then_inc(spread_ready, 1)
                dve.wait_ge(used, b * 12 + (UE + 12))
                v.tensor_copy(y[par * SLOTS:(par + 1) * SLOTS, 1:4:2, :], ps[SLOTS:2 * SLOTS, 4:6, :]).then_inc(y_dve, 1)

            dve.wait_ge(table_ready, 1)
            dve.wait_ge(tramp_ready, 1)
            turn_evac(0, 0)
            block_dve(0, 0, None)
            block_dve(1, 1, None)
            with dve.Fori(1, NE // 2) as it:
                b = it * 2
                block_dve(b, 0, it)
                block_dve(b + 1, 1, it)
            more = dve.value_load(meta[0:1, NOVER:NOVER + 1], min_val=0, max_val=NOVER)
            with dve.If(more > 0):
                with dve.Fori(NE // 2, NBLK // 2) as it:
                    b = it * 2
                    block_dve(b, 0, it)
                    block_dve(b + 1, 1, it)
                for half in range(2):
                    add_parts(8 * NBLK - 16, half, last=True)
            with dve.If(more < 1):
                for half in range(2):
                    add_parts(8 * NE - 16, half, last=True)

        @block.tensor
        def _(pe):
            mm, turn = nc.tensor.matmul, nc.tensor.transpose

            pe.wait_ge(consts, 6)
            pe.wait_ge(gain_in, 16 * 11)
            turn(ps[:, 7, 0:NGR], PB[0:NGR, 8192:8192 + P], ident[0:NGR, 0:NGR]).then_inc(gain_turned, 1)

            def norm_tile(T, src):
                pe.wait_ge(diag_ready, T + 1)
                for b in range(4):
                    if T > 0:
                        pe.wait_ge(hT_ready, T * 4 + (b - 3))
                    for k in range(4 * b, 4 * b + 4):
                        ins = mm(ps[:, b, (k % 4) * P:(k % 4 + 1) * P], src[:, k * P:(k + 1) * P], dg[:, T % 2, :],
                                 start=True, stop=True, skip_group_check=True)
                    ins.then_inc(h_turned, 1)

            norm_tile(0, memx[:, 0, :])
            norm_tile(1, memx[:, 1, :])
            pe.wait_ge(hT_ready, 8)
            for c in range(4):
                n = c
                chunk_landed(pe, n)
                w = chunk(n, XW)
                for kk in range(4):
                    k = 4 * c + kk
                    for f in range(XH):
                        ins = mm(ps[:, 4 + f // 2, (f % 2) * NM:(f % 2 + 1) * NM], w[:, kk, f * P:(f + 1) * P],
                                 memT[:, k, :], start=(k == 0 and f % 2 == 0), stop=(k == KD - 1),
                                 skip_group_check=True)
                ins.then_inc(used, 1)
            for c in range(4):
                n = 4 + c
                chunk_landed(pe, n)
                if c == 0:
                    pe.wait_ge(gains, 1)
                w = chunk(n, XW)
                for kk in range(4):
                    k = 4 * c + kk
                    for m in range(2):
                        ins = mm(ps[:, 6 + m, :], memT[:, k, m * P:(m + 1) * P], w[:, kk, :],
                                 start=(k == 0), stop=(k == KD - 1))
                ins.then_inc(used, 1)
                if c == 0:
                    pe.wait_ge(xk_sq, 2)
                    for b in range(2):
                        mm(ps[:, b, :], ones[:, :], sqm[:, b * 512:(b + 1) * 512], start=True, stop=True
                           ).then_inc(xk_ss, 1)
            pe.wait_ge(xk_root, 2)
            for t in range(NT):
                norm_tile(2 + t, X[:, t, :])
            pe.wait_ge(hT_ready, 24)
            pe.wait_ge(kx_ready, 2)
            pe.wait_ge(vx_ready, 2)

            def col_tile(s, bank):
                w = slot(s).rearrange("p (k n) -> p k n", n=P)
                for k in range(KD):
                    ins = mm(ps[:, bank, :], w[:, k, :], H[:, k, :], start=(k == 0), stop=(k == KD - 1))
                ins.then_inc(used, 1)

            def head_sums(n, bank, b):
                pe.wait_ge(q_sq, n + 1)
                mm(ps[:, bank, :], blk[:, :], sq[:, b, :], start=True, stop=True).then_inc(q_ss, 1)

            chunk_landed(pe, SEQ_K)
            col_tile(2, 7)
            with pe.Fori(0, 2) as it:
                n = it * 4
                for s in range(4):
                    pe.wait_ge(landed[s], n * 4 + 16 * (loads_before[SEQ_Q + s] + 1))
                    if s >= 2:
                        pe.wait_ge(q_ready, n + 1)
                    col_tile(s, 4 + s)
                    head_sums(n + s, (s - 1) % 4, s % 2)
                pe.wait_ge(q_ready, n + 3)
            chunk_landed(pe, SEQ_V)
            w = chunk(SEQ_V, P)
            for k in range(KD):
                ins = mm(ps[:, 5, :], w[:, k, :], H[:, k, :], start=(k == 0), stop=(k == KD - 1))
                if k == 3:
                    head_sums(8, 3, 0)
            ins.then_inc(used, 1)
            pe.wait_ge(q_ready, 9)
            pe.wait_ge(k_padded, 2)
            pe.wait_ge(k_ready, 2)

            for i in range(8):
                t, g = i // 2, i % 2
                for m in (0, 4, 1, 5, 2, 6, 3, 7):
                    hp = slice(m // 4 * HD, (m // 4 + 1) * HD)
                    for at, n, col in WINDOW[m % 2]:
                        ins = mm(ps[:, m // 2, (m % 2) * WIN + at:(m % 2) * WIN + at + n],
                                 proj[hp, 4 * g + m % 4, t * P:(t + 1) * P],
                                 kdup[hp, g, t * P + col:t * P + col + n], start=True, stop=True,
                                 skip_group_check=True)
                    if m % 2 == 1:
                        ins.then_inc(scores_done, 1)
                if i == 0:
                    pe.wait_ge(v_copied, 1)
                    for tt in range(NT):
                        ins = turn(ps[:, 6, tt * P:(tt + 1) * P], vTp[:, tt * P:(tt + 1) * P], ident[:, :])
                    ins.then_inc(v_turned, 1)
                    for tt in range(NT):
                        ins = turn(ps[0:CHUNK, 7, tt * P:(tt + 1) * P], vTp[:, tt * P + P:tt * P + P + CHUNK], ident[:, :])
                    ins.then_inc(v_turned, 1)
                chunk_landed(pe, SEQ_U + i)
                if i > 0:
                    pe.wait_ge(u_ready, i)
                w = chunk(SEQ_U + i, P)
                for k in range(KD):
                    ins = mm(ps[:, 4, :], w[:, k, :], H[:, k, :], start=(k == 0), stop=(k == KD - 1))
                ins.then_inc(used, 1)
                pe.wait_ge(exp_done, 9 * i + 9)
                for j in range(4):
                    for n in range(3):
                        ins = turn(ps[:, j, n * P:(n + 1) * P], Spair[:, j, n * P:(n + 1) * P], ident[:, :])
                    ins.then_inc(pt_turned, 1)
                if i == 0:
                    pe.wait_ge(v_ready, 3)
                for j in range(4):
                    pe.wait_ge(pt_dve if j % 2 == 0 else pt_act, 2 * i + j // 2 + 1)
                    if j == 0 and i > 0:
                        pe.wait_ge(a_ready, i)
                    for e in range(2):
                        o = ps[:, 5, (2 * j + e) * HD:(2 * j + e + 1) * HD]
                        mm(o, PT[:, j, 2 * e * P:(2 * e + 1) * P], vA[:, t, g * HD:(g + 1) * HD],
                           start=True, stop=False, skip_group_check=True)
                        ins = mm(o, PT[:, j, P:2 * P], vB[:, e, t, g * HD:(g + 1) * HD],
                                 start=False, stop=True, skip_group_check=True)
                ins.then_inc(pv_done, 1)
            pe.wait_ge(a_ready, 8)
            for t in range(NT):
                if t >= 2:
                    pe.wait_ge(aT_dve, t - 1)
                    pe.wait_ge(aT_act, t - 1)
                for b in range(2):
                    for k in range(4 * b, 4 * b + 4):
                        ins = turn(ps[:, 2 * (t % 2) + b, (k % 4) * P:(k % 4 + 1) * P],
                                   a_rows[:, t, k * P:(k + 1) * P], ident[:, :])
                    ins.then_inc(a_turned, 1)
            chunk_landed(pe, SEQ_POOL)
            pe.wait_ge(u_ready, 8)
            w = chunk(SEQ_POOL, 256)
            for m in range(8):
                g = m // 2
                if m % 2 == 0:
                    pe.wait_ge(d_ready, 2 * g + 2)
                if m >= 4:
                    pe.wait_ge(pT_ready, m - 3)
                for kk in range(2):
                    ins = mm(ps[:, 4 + m % 4, :], w[:, 2 * g + kk, (m % 2) * P:(m % 2 + 1) * P],
                             proj[:, 10 + 2 * g + kk, :], start=(kk == 0), stop=(kk == 1))
                ins.then_inc(pool_done if m < 7 else used, 1)

            pe.wait_ge(aT_dve, 4)
            pe.wait_ge(aT_act, 4)
            pe.wait_ge(pT_ready, 8)
            with pe.Fori(0, 2) as it:
                n = it * 2
                for par in range(2):
                    if par == 1:
                        pe.wait_ge(x_added, n * 4 + 1)
                    for c in range(4):
                        pe.wait_ge(landed[c], n * 16 + 16 * (loads_before[SEQ_OUT + c] + 1 + par))
                        w = slot(c).rearrange("p (k n) -> p k n", n=512)
                        for t in range(NT):
                            for kk in range(4):
                                k = 4 * c + kk
                                ins = mm(ps[:, 4 * par + t, :], H[:, k, t * P:(t + 1) * P], w[:, kk, :],
                                         start=(k == 0), stop=(k == KD - 1))
                            if c == 3 and t < 3:
                                ins.then_inc(o_done, 1)
                        ins.then_inc(used, 1)
                pe.wait_ge(x_added, n * 4 + 4)
            for t in range(NT):
                norm_tile(6 + t, X[:, t, :])
            for f in range(XH):
                for c in range(4):
                    if f == 0:
                        chunk_landed(pe, SEQ_XQ + c)
                        pe.wait_ge(hT_ready, 36 + c + 1)
                    w = chunk(SEQ_XQ + c, XW)
                    for kk in range(4):
                        k = 4 * c + kk
                        ins = mm(ps[:, 4 + f, :], w[:, kk, f * P:(f + 1) * P], H[:, k, :],
                                 start=(k == 0), stop=(k == KD - 1))
                    if c == 0 and f > 0:
                        pe.wait_ge(xq_sq, f)
                        mm(ps[:, f - 1, :], ones[:, :], sqx[:, (f - 1) % 2, :], start=True, stop=True).then_inc(xq_ss, 1)
                    if f == XH - 1:
                        ins.then_inc(used, 1)
                if f < XH - 1:
                    ins.then_inc(xq_done, 1)
            pe.wait_ge(xq_sq, XH)
            mm(ps[:, XH - 1, :], ones[:, :], sqx[:, (XH - 1) % 2, :], start=True, stop=True).then_inc(xq_ss, 1)

            def xscores(t):
                if t >= 2:
                    pe.wait_ge(xexp_done, 4 * t - 4)
                for h in range(XH):
                    ins = mm(ps[:, 5 * (t % 2) + h // 2, (h % 2) * NM:(h % 2 + 1) * NM], qx[:, h, t * P:(t + 1) * P],
                             kx[:, h, :], start=True, stop=True, skip_group_check=True)
                ins.then_inc(xs_done, 1)

            def xturn(t):
                pe.wait_ge(xp_ready, t + 1)
                for n in range(8):
                    if n == 0 and t > 0:
                        pe.wait_ge(xpt_act, t)
                    if n == 4 and t > 0:
                        pe.wait_ge(xpt_dve, t)
                    ins = turn(ps[:, 2 + n // 4, (n % 4) * P:(n % 4 + 1) * P],
                               SX[:, t % 2, n * P:(n + 1) * P], ident[:, :])
                    if n % 4 == 3:
                        ins.then_inc(xp_turned, 1)

            def xvalues(t):
                pe.wait_ge(xpt_act, t + 1)
                pe.wait_ge(xpt_dve, t + 1)
                if t >= 2:
                    pe.wait_ge(oT_ready, t - 1)
                for h in range(XH):
                    for m in range(2):
                        ins = mm(ps[:, 4 + 3 * (t % 2), h * P:(h + 1) * P], vx[:, m, h * P:(h + 1) * P],
                                 PTX[:, (2 * h + m) * P:(2 * h + m + 1) * P], start=(m == 0), stop=(m == 1),
                                 skip_group_check=True)
                ins.then_inc(xo_part, 1)

            pe.wait_ge(qx_ready, XH)
            xscores(0)
            xscores(1)
            for t in range(NT):
                xturn(t)
                xvalues(t)
                if t + 2 < NT:
                    xscores(t + 2)
            pe.wait_ge(oT_ready, NT)
            for c in range(4):
                chunk_landed(pe, SEQ_XO + c)
            with pe.Fori(0, 2) as it:
                n = it * 2
                for par in range(2):
                    if par == 1:
                        pe.wait_ge(x_added, n * 4 + 16)
                    for t in range(NT):
                        for c in range(4):
                            ins = mm(ps[:, 4 * par + t, :], H[:, c, t * P:(t + 1) * P],
                                     slot(early[SEQ_XO + c][0])[:, ds(n * 512 + par * 512, 512)],
                                     start=(c == 0), stop=(c == 3))
                        ins.then_inc(o_done, 1)
                pe.wait_ge(x_added, n * 4 + 20)
            def logits(t):
                pe.wait_ge(hT_ready, 40 + 4 * t + 4)
                for k in range(KD):
                    ins = mm(ps[:, 4, t * NCOL:(t + 1) * NCOL], H[:, k, t * P:(t + 1) * P], wr[:, k, :],
                             start=(k == 0), stop=(k == KD - 1), skip_group_check=True)
                return ins

            for t in range(NT):
                norm_tile(10 + t, X[:, t, :])
                if t == 0:
                    pe.wait_ge(router_in, 16 * (NG + 1))
                    pe.wait_ge(x_added, 32)
                else:
                    logits(t - 1)
            logits(NT - 1).then_inc(logits_done, 1)
            pe.wait_ge(tri_ready, 1)
            pe.wait_ge(picks, 1)
            for t in range(NT + 1):
                for s in range(min(t + 1, NT)):
                    ins = mm(ps[:, 5, t * NE:(t + 1) * NE], tri if s == t else ones[:, :], rq["M"][:, s, :],
                             start=(s == 0), stop=(s == min(t, NT - 1)), skip_group_check=True)
            ins.then_inc(ranks, 1)
            pe.wait_ge(onehots, 6)
            for n in range(2 * NT):
                k, t = n // NT, n % NT
                ins = mm(ps[0:SLOTS, 6, 0:2 * TCOL], rq["P1" if k == 0 else "P2"][:, t, :],
                         rq["B1" if k == 0 else "B2"][:, t, :], start=(n == 0), stop=(n == 2 * NT - 1))
            ins.then_inc(table_done, 1)

            xs = hs

            def turn_rows(b, par):
                if isinstance(b, int):
                    pe.wait_ge(gathered[par], b * 8 + (16 - 8 * par))
                    wait_past(pe, xsT_ready, b * 2)
                else:
                    rows, copied = pe.to_reg(b * 8 + (16 - 8 * par)), pe.to_reg(b * 2)
                    pe.wait_ge(table_ready, 1)
                    pe.wait_ge(gathered[par], rows)
                    pe.wait_ge(xsT_ready, copied)
                for q in range(2):
                    for k in range(8 * q, 8 * q + 8):
                        ins = turn(ps[:, 2 + q, (k % 8) * SLOTS:(k % 8 + 1) * SLOTS],
                                   xs[0:SLOTS, par, k * P:(k + 1) * P], ident[0:SLOTS, 0:SLOTS])
                    ins.then_inc(xs_turned, 1)

            def expert_landed(b, j):
                s = expert_slot(j)
                pe.wait_ge(landed[s], b * 16 + 16 * (early_loads[s] + 1))

            def spread_parts(before, half, last=False):
                for i in range(8 * half, 8 * half + 8):
                    t, n = i // 4, i % 4
                    if i >= 2:
                        if last:
                            pe.wait_ge(sum_ready, i - 1)
                        else:
                            pe.wait_ge(part_added, before + (i - 1))
                    mm(ps[:, 6 + i % 2, :], spread[:, t * P:(t + 1) * P], y[:, n, :],
                       start=True, stop=True).then_inc(part_done, 1)

            def last_pair(blocks):
                pe.wait_ge(y_act, blocks)
                pe.wait_ge(y_dve, blocks)
                pe.wait_ge(spread_ready, blocks // 2)
                for half in range(2):
                    spread_parts(0, half, last=True)

            def block_pe(b, par, pair):
                pe.wait_ge(xsT_ready, b * 2 + 2)
                wait_past(pe, gu_copied, b)
                for c in range(4):
                    for kk in range(4):
                        k = 4 * c + kk
                        for side in range(2):
                            j = 2 * c + side
                            if kk == 0:
                                expert_landed(b, j)
                            w = slot(expert_slot(j)).rearrange("p (k n) -> p k n", n=FF)
                            ins = mm(ps[side * SLOTS:(side + 1) * SLOTS, 0, :], xsT[:, par, k, :], w[:, kk, :],
                                     start=(k == 0), stop=(k == KD - 1), skip_group_check=True)
                            if kk == 3:
                                ins.then_inc(used, 1)
                turn_rows(b + 1, 1 - par)
                behind = par == 0 and pair is not None
                if behind:
                    pe.wait_ge(y_act, b)
                    pe.wait_ge(y_dve, b)
                    pe.wait_ge(spread_ready, pair)
                    spread_parts(pair * 16 - 16, 0)
                pe.wait_ge(gu_copied, b + 1)
                for f in range(KF):
                    ins = turn(guT[:, f, :], gu[:, f * P:(f + 1) * P], ident[:, :])
                ins.then_inc(gu_turned, 1)
                if behind:
                    spread_parts(pair * 16 - 16, 1)
                if par == 1 and pair is not None:
                    pe.wait_ge(part_added, pair * 16)
                pe.wait_ge(act_ready, b + 1)
                wait_past(pe, y_act, b)
                wait_past(pe, y_dve, b)
                for f in range(KF):
                    expert_landed(b, 8 + f)
                    w = slot(expert_slot(8 + f))
                    for n in range(4):
                        half = slice(n % 2 * SLOTS, (n % 2 + 1) * SLOTS)
                        ins = mm(ps[half, 4 + n // 2, :], act_t[:, f * SLOTS:(f + 1) * SLOTS],
                                 w[:, n * 512:(n + 1) * 512], start=(f == 0), stop=(f == KF - 1), skip_group_check=True)
                    ins.then_inc(used, 1)

            turn_rows(0, 0)
            block_pe(0, 0, None)
            block_pe(1, 1, None)
            with pe.Fori(1, NE // 2) as it:
                b = it * 2
                block_pe(b, 0, it)
                block_pe(b + 1, 1, it)
            more = pe.value_load(meta[0:1, NOVER:NOVER + 1], min_val=0, max_val=NOVER)
            with pe.If(more > 0):
                with pe.Fori(NE // 2, NBLK // 2) as it:
                    b = it * 2
                    block_pe(b, 0, it)
                    block_pe(b + 1, 1, it)
                last_pair(NBLK)
            with pe.If(more < 1):
                last_pair(NE)


_INS = ['x', 'mem', 'mix_norm_g', 'w_in', 'q_norm_g', 'k_norm_g', 'sink_logits', 'pool_w', 'pool_scale', 'w_out',
        'xattn_norm_g', 'mem_norm_g', 'xq_w', 'xkv_w', 'xq_norm_g', 'xk_norm_g', 'xo_w', 'ffn_norm_g',
        'router_group_w', 'router_group_b', 'router_expert_w', 'router_expert_b', 'expert_w_gate',
        'expert_w_up', 'expert_w_down']
_OUTS = [((1, S, D), 'float32')]


def kernel(**inputs):
    import numpy as _np
    import concourse.bacc as _bacc
    from concourse import mybir as _mybir
    from concourse.bass_utils import run_bass_kernel_spmd as _run

    nc = _bacc.Bacc("TRN2", target_bir_lowering=False, num_devices=1)
    arrays, args = {}, []
    for name in _INS:
        a = _np.ascontiguousarray(inputs[name])
        arrays[f"in_{name}_dram"] = a
        args.append(nc.dram_tensor(f"in_{name}_dram", a.shape, _mybir.dt.from_np(a.dtype), kind="ExternalInput").ap())
    for i, (shape, dtype) in enumerate(_OUTS):
        dt = _mybir.dt.from_np(_np.dtype(dtype))
        args.append(nc.dram_tensor(f"out_{i}_dram", shape, dt, kind="ExternalOutput").ap())
    hybrid_block(nc, *args)
    r = _run(nc, [arrays], core_ids=[0])
    got = tuple(r.results[0][f"out_{i}_dram"] for i in range(len(_OUTS)))
    return got[0]
```

```python
from contextlib import ExitStack

import concourse.bass as bass
from concourse import mybir

P = 128
F32 = mybir.dt.float32
I32 = mybir.dt.int32
U32 = mybir.dt.uint32
F32R = mybir.dt.float32r
HIGH = 0xFFFFF000
ALU = mybir.AluOpType
ACT = mybir.ActivationFunctionType
AX = mybir.AxisListType.X
ds = bass.ds

D = 2048
S = 512
NT = S // P
KD = D // P
HD = 64
NH = 16
CHUNK = 64
WIN = 3 * CHUNK
QKV = 1280
NCT = 18
NM = 256
XW = 512
XH = 4
XD = 128
POOLT = 8
NG, EPG = 4, 8
NE = NG * EPG
FF = 512
KF = FF // P
EPS = 1e-6
NEG = -1e30

SLOTS = 64
MORE = -(-S // SLOTS) - 1
NOVER = 2 * ((2 * S // (SLOTS + 1) + 1) // 2)
NBLK = NE + NOVER
TCOL = NBLK + 2
EMPTY = 8192
CHK = 2048
NSLOT = 12
NA = 4
NCOL = NG + NE


def hybrid_block(nc, x, mem, mix_norm_g, w_in, q_norm_g, k_norm_g, sink_logits, pool_w, pool_scale,
                 w_out, xattn_norm_g, mem_norm_g, xq_w, xkv_w, xq_norm_g, xk_norm_g, xo_w, ffn_norm_g,
                 router_group_w, router_group_b, router_expert_w, router_expert_b,
                 expert_w_gate, expert_w_up, expert_w_down, out):
    hn_dram = nc.dram_tensor("normed_rows", (S, D), F32, kind="Internal").ap()

    with ExitStack() as ctx:
        def sb(name, shape, dt=F32):
            return ctx.enter_context(nc.sbuf_tensor(name, shape, dt))

        def sem(name):
            return ctx.enter_context(nc.semaphore(name))

        with ExitStack() as shared:
            shared.enter_context(nc.sbuf_tensor("slots_0_1", [P, 2 * CHK], F32))
            in_hi = shared.enter_context(nc.sbuf_tensor("w_in_high", [P, 2, KD // 2, P], F32R))
            in_lo = shared.enter_context(nc.sbuf_tensor("w_in_low", [P, 2, KD // 2, P], F32R))
            mix_lo = shared.enter_context(nc.sbuf_tensor("mix_low", [P, KD, S], F32R))
            shared.enter_context(nc.sbuf_tensor("slot_8", [P, CHK], F32))
            w_hi = shared.enter_context(nc.sbuf_tensor("weight_high", [P, 2, 2, 512], F32R))
            w_lo = shared.enter_context(nc.sbuf_tensor("weight_low", [P, 2, 2, 512], F32R))
        ring = sb("weight_ring", [P, NSLOT * CHK])
        with nc.sbuf_tensor("normed_low", [P, NT, KD, P], F32R) as h_lo:
            pass
        X = sb("residual", [P, NT, D])
        with nc.sbuf_tensor("mix_high", [P, KD, S], F32R) as mix_hi:
            pass
        H = sb("transposed_acts", [P, KD, S])
        PB = sb("proj_buffer", [P, NCT * S])
        kx = sb("memory_keys_T", [P, XH, NM])
        vx = sb("memory_values", [P, NM // P, XW])
        ident = sb("identity", [P, P])
        ones = sb("ones", [P, P])
        blk = sb("head_blocks", [P, P])
        NGR = 4 * KD + POOLT + 4
        gT = sb("gains_T", [P, NGR])
        stat = sb("norm_stats", [P, 3, 14])
        psq = sb("square_parts", [P, 2, NT, 4])
        eps = sb("eps", [P, 1])
        sink = sb("sink", [P, NH])
        rbias = sb("router_bias", [P, NCOL])
        sm = sb("softmax_stats", [P, 6, 8])
        cols = sb("slot_columns", [SLOTS, 2], I32)
        io = sb("ramp64", [P, 64])
        tok = sb("token_ids", [P, NT])
        ps = ctx.enter_context(nc.psum_tensor("ps", [P, 8, 512], F32))

        def slot(s):
            return ring[:, s * CHK:(s + 1) * CHK]

        hs = PB[:, 0:2 * D].rearrange("p (b d) -> p b d", b=2)
        proj = PB[:, :].rearrange("p (c s) -> p c s", s=S)
        qx = PB[:, 4096:6144].rearrange("p (h s) -> p h s", s=S)
        SX = PB[:, 6144:8192].rearrange("p (b n) -> p b n", b=2)
        sqx = PB[:, 6144:7168].rearrange("p (b n) -> p b n", b=2)
        rtx = PB[:, 7168:8192].rearrange("p (b n) -> p b n", b=2)
        wr = PB[:, 8192:8192 + KD * NCOL].rearrange("p (k c) -> p k c", c=NCOL)
        tri = PB[:, 8768:8896]
        tidx = PB[0:SLOTS, 8896:8896 + TCOL].bitcast(I32)
        tokf = PB[:, 8960:8960 + TCOL]
        gate = PB[:, 9024:9024 + TCOL]
        meta = PB[0:1, 9088:9088 + NOVER + 1].bitcast(I32)
        y = PB[:, 4096:6144].rearrange("p (n c) -> p n c", c=512)
        spread = PB[:, 6144:6656]
        tramp = PB[:, 6656:7168]
        guT = ps[:, 1, :].rearrange("p (f n) -> p f n", n=P)
        whole = PB[:, 0:1024].rearrange("p (b n) -> p b n", b=2)
        high = PB[:, 1024:2048].rearrange("p (b n) -> p b n", b=2)
        whigh = PB[:, 2048:3072].rearrange("p (k n) -> p k n", n=512)
        inhigh = PB[:, 4096:5120].rearrange("p (k n) -> p k n", n=P)
        dg = PB[:, 7936:8192].rearrange("p (b n) -> p b n", b=2)
        Hf = H[:, :, :].rearrange("p k s -> p (k s)")
        PTX = Hf[:, 4 * S:4 * S + 1024]
        xsT = Hf[:, 0:2 * KD * SLOTS].rearrange("p (b k n) -> p b k n", b=2, n=SLOTS)
        act_t = Hf[:, 2048:2048 + KF * SLOTS]
        sil = Hf[:, 2304:2304 + KF * SLOTS]
        gu = Hf[:, 2560:2560 + FF]
        scr = ring[:, NA * CHK:NSLOT * CHK]
        memx = scr[:, 0:4096].rearrange("p (t d) -> p t d", t=2)
        memT = scr[:, 4096:8192].rearrange("p (k m) -> p k m", m=NM)
        sqm = scr[:, 8192:9216]
        rtm = scr[:, 9216:10240]
        bias = scr[:, 0:3072].rearrange("p (h n) -> p h n", n=WIN)
        Ssb = scr[:, 3072:4608].rearrange("p (h n) -> p h n", n=WIN)
        Spair = scr[:, 3072:4608].rearrange("p (j n) -> p j n", n=2 * WIN)
        PT = scr[:, 4608:6144].rearrange("p (j n) -> p j n", n=384)
        a_rows = scr[:, 6144:10240].rearrange("p (t c) -> p t c", t=NT)
        kdup = scr[:, 10240:11392].rearrange("p (g n) -> p g n", g=2)
        vA = scr[:, 11392:11904].rearrange("p (t c) -> p t c", t=NT)
        sq = scr[:, 12416:13440].rearrange("p (b n) -> p b n", b=2)
        rt = scr[:, 13440:14464].rearrange("p (b n) -> p b n", b=2)
        vB = scr[:, 13440:14464].rearrange("p (e t c) -> p e t c", e=2, t=NT)
        wsum = scr[:, 14464:15520].rearrange("p (b n) -> p b n", b=2)
        vTp = scr[:, 15520:16096]
        ramp = scr[:, 16096:16160].rearrange("p (g n) -> p g n", g=4)
        cnt16 = scr[:, 16160:16176]
        dist = PB[:, 5120:5120 + WIN]
        mask = PB[:, 5376:5376 + WIN]

        G_MIX, G_XAT, G_MEM, G_FFN = 0, KD, 2 * KD, 3 * KD
        G_POOL = 4 * KD
        G_Q, G_K, G_XQ, G_XK = (G_POOL + POOLT + j for j in range(4))

        landed = [sem(f"landed{s}") for s in range(NSLOT)]
        used = sem("chunks_used")
        mem_in = [sem("mem_in0"), sem("mem_in1")]
        x_in = [sem(f"x_in{t}") for t in range(NT)]
        gain_in = sem("gain_in")
        small_in = sem("small_in")
        consts = sem("consts")
        eps_set = sem("eps_set")
        gain_turned = sem("gain_turned")
        gains = sem("gains")
        ssq_done = sem("ssq_done")
        root_done = sem("root_done")
        parts_done = sem("square_parts_done")
        rstd_done = sem("rstd_done")
        diag_ready = sem("diag_ready")
        rows_ready = sem("rows_ready")
        h_turned = sem("h_turned")
        h_cut = sem("h_cut")
        h_hi_ready = sem("h_hi_ready")
        h_lo_ready = sem("h_lo_ready")
        x_again = sem("x_again")
        hT_ready = sem("hT_ready")
        hn_stored = [sem("hn_stored0"), sem("hn_stored1")]
        xk_sq = sem("xk_sq")
        xk_ss = sem("xk_ss")
        xk_root = sem("xk_root")
        kx_ready = sem("kx_ready")
        vx_ready = sem("vx_ready")
        q_sq = sem("q_sq")
        q_ss = sem("q_ss")
        q_root = sem("q_root")
        q_ready = sem("q_ready")
        k_padded = sem("k_padded")
        k_ready = sem("k_ready")
        v_copied = sem("v_copied")
        v_turned = sem("v_turned")
        v_ready = sem("v_ready")
        bias_built = sem("bias_built")
        bias_reset = sem("bias_reset")
        ramp_in = sem("ramp_in")
        ramp_ready = sem("ramp_ready")
        scores_done = sem("scores_done")
        scores_read = sem("scores_read")
        max_done = sem("max_done")
        exp_done = sem("exp_done")
        pt_turned = sem("pt_turned")
        pt_dve = sem("pt_dve")
        pt_act = sem("pt_act")
        pv_done = sem("pv_done")
        a_ready = sem("a_ready")
        u_ready = sem("u_ready")
        d_ready = sem("d_ready")
        a_turned = sem("a_turned")
        whole_ready = sem("whole_ready")
        high_cut = sem("high_cut")
        mix_hi_ready = sem("mix_hi_ready")
        mix_lo_ready = sem("mix_lo_ready")
        wcut = sem("weights_cut")
        w_hi_ready = sem("w_hi_ready")
        w_lo_ready = sem("w_lo_ready")
        halves_used = sem("halves_used")
        pool_done = sem("pool_done")
        o_done = sem("out_product_done")
        x_added = sem("x_added")
        router_in = sem("router_in")
        tri_ready = sem("tri_ready")
        xq_done = sem("xq_done")
        xq_sq = sem("xq_sq")
        xq_ss = sem("xq_ss")
        xq_root = sem("xq_root")
        qx_ready = sem("qx_ready")
        xs_done = sem("xscores_done")
        xmax_done = sem("xmax_done")
        xexp_done = sem("xexp_done")
        xp_ready = sem("xprobs_ready")
        xp_turned = sem("xprobs_turned")
        xpt_dve = sem("xpt_dve")
        xpt_act = sem("xpt_act")
        xo_part = sem("xo_part")
        oT_ready = sem("oT_ready")
        logits_done = sem("logits_done")
        gmax_done = sem("gmax_done")
        gexp_done = sem("gexp_done")
        top_done = sem("top_done")
        texp_done = sem("texp_done")
        picks = sem("picks")
        ranks = sem("ranks")
        onehots = sem("onehots")
        table_done = sem("table_done")
        table_ready = sem("table_ready")
        xs_clear = sem("xs_clear")
        idx_copied = sem("idx_copied")
        gathered = [sem("gathered0"), sem("gathered1")]
        xs_turned = sem("xs_turned")
        xsT_ready = sem("xsT_ready")
        gu_copied = sem("gu_copied")
        gu_turned = sem("gu_turned")
        sil_ready = sem("sil_ready")
        act_ready = sem("act_ready")
        y_act = sem("y_act")
        y_dve = sem("y_dve")
        tramp_ready = sem("token_ramp_ready")
        spread_ready = sem("spread_ready")
        part_done = sem("part_done")
        part_added = sem("part_added")
        sum_ready = sem("sum_ready")
        stored = sem("stored")
        act_link = sem("act_link")
        dve_link = sem("dve_link")
        pool_link = sem("pool_link")

        xkv_v = xkv_w[0].rearrange("(k p) n -> p k n", p=P)
        w_in_v = w_in[0].rearrange("(k p) n -> p k n", p=P)
        w_out_v = w_out[0].rearrange("(k p) n -> p k n", p=P)
        xq_v = xq_w[0].rearrange("(k p) n -> p k n", p=P)
        xo_v = xo_w[0].rearrange("(k p) n -> p k n", p=P)
        pool_v = pool_w[0].rearrange("g (k p) n -> p (g k) n", p=P)
        early = []
        for half in range(2):
            for c in range(4):
                early.append((c, xkv_v[:, 4 * c:4 * c + 4, half * XW:(half + 1) * XW], XW))
        SEQ_K = len(early)
        SEQ_Q = SEQ_K + 1
        SEQ_V = SEQ_Q + 8
        for n, ct in enumerate([8] + list(range(8)) + list(range(9, NCT))):
            early.append((n % 2, w_in_v[:, :, ct * P:(ct + 1) * P], P))
        HALVES_IN = 2 * NCT
        SEQ_POOL = len(early)
        early.append((1, pool_v, 256))
        SEQ_OUT = len(early)
        for n in range(4):
            for c in range(4):
                early.append((c, w_out_v[:, 4 * c:4 * c + 4, n * 512:(n + 1) * 512], 512))
        SEQ_XQ = len(early)
        for c in range(4):
            early.append((c, xq_v[:, 4 * c:4 * c + 4, :], XW))
        SEQ_XO = len(early)
        for c in range(4):
            early.append((c, xo_v[:, c:c + 1, :], D))
        UE = SEQ_XO
        loads_before = []
        for n, (s, _, _) in enumerate(early):
            loads_before.append(sum(1 for m in range(n) if early[m][0] == s))
        early_loads = [sum(1 for e in early if e[0] == s) for s in range(NSLOT)]

        def wait_past(eng, semaphore, value):
            if not isinstance(value, int) or value > 0:
                eng.wait_ge(semaphore, value)

        def chunk(n, width):
            return slot(early[n][0]).rearrange("p (k n) -> p k n", n=width)

        def chunk_landed(eng, n):
            eng.wait_ge(landed[early[n][0]], 16 * (loads_before[n] + 1))

        rq = {}

        def carve(spec):
            at = 4096
            for name, shape in spec:
                n = 1
                for v in shape:
                    n *= v
                v = PB[:, at:at + n]
                if len(shape) == 2:
                    v = v.rearrange("p (a b) -> p a b", b=shape[1])
                elif len(shape) == 3:
                    v = v.rearrange("p (a b c) -> p a b c", b=shape[1], c=shape[2])
                rq[name] = v
                at += n
            assert at <= 8192, at

        carve([("L", (NT, NCOL)), ("gm", (NT,)), ("gs", (NT, NG)), ("eg", (NT, NG)), ("gsum", (NT,)), ("gg", (NT,)),
               ("gh", (NT, NG)), ("ti", (NT,)), ("t8", (NT, EPG)), ("es", (NT, EPG)),
               ("m1", (NT,)), ("m2", (NT,)), ("h1", (NT, EPG)), ("h2", (NT, EPG)), ("dt", (NT,)), ("et", (NT,)),
               ("w1", (NT,)), ("w2", (NT,)), ("tg", (NT, NG, EPG)), ("M1", (NT, NE)), ("M2", (NT, NE)),
               ("M", (NT, NE)), ("R", (NT + 1, NE)), ("over", (NE,)), ("cmp", (NE, MORE)), ("ca", (16 + NE,)),
               ("cb", (16 + NE,)), ("base", (NE,)), ("pos", (NT,)), ("ob", (NT,)), ("ek", (NT,)), ("pc", (NT, MORE)),
               ("q", (NT,)), ("z", (NT,)), ("row", (NT,)), ("bk", (NT,)), ("cand", (NT, EPG)),
               ("fin", (2 * TCOL,)), ("tmp", (NT, NE)), ("thr", (MORE,)), ("one", (NT, TCOL)), ("val", (NT,)), ("ec", (NOVER, NE)), ("ev", (NOVER + 1,)),
               ("P1", (NT, SLOTS)), ("P2", (NT, SLOTS)), ("B1", (NT, 2 * TCOL)), ("B2", (NT, 2 * TCOL))])

        def head_at(n):
            return 8 * (n // 8) + 2 * (n % 4) + (n % 8) // 4

        WINDOW = (((0, WIN, 0),), ((0, CHUNK, P), (CHUNK, P, 0)))

        def mix_shape(ap, i):
            return ap.rearrange("p (k n) -> p k n", n=P) if i < 8 else ap

        def mix_part(tensor, i):
            return tensor[:, 4 * (i % 2):4 * (i % 2) + 4, i // 2 * P:(i // 2 + 1) * P] if i < 8 else tensor[:, i, :]

        block = ctx.enter_context(nc.Block())

        gate_v = expert_w_gate[0].rearrange("e (k p) n -> e p k n", p=P)
        up_v = expert_w_up[0].rearrange("e (k p) n -> e p k n", p=P)
        down_v = expert_w_down[0].rearrange("e (k p) n -> e p k n", p=P)

        def expert_chunk(e, j):
            if j < 8:
                return (gate_v, up_v)[j % 2][ds(e, 1), :, 4 * (j // 2):4 * (j // 2) + 4, :].rearrange(
                    "e p k n -> p (e k) n")
            return down_v[ds(e, 1), :, j - 8:j - 7, :].rearrange("e p k n -> p (e k) n")

        def expert_slot(j):
            return (j + 4) % NSLOT

        @block.sync
        def _(sp):
            for t in range(2):
                sp.dma_start(memx[:, t, :], mem[0, t * P:(t + 1) * P, :]).then_inc(mem_in[t], 16)
            sp.wait_ge(gain_in, 16 * 11)
            for n, (s, src, width) in enumerate(early):
                if n == 4:
                    for t in range(NT):
                        sp.dma_start(X[:, t, :], x[0, t * P:(t + 1) * P, :]).then_inc(x_in[t], 16)
                if n == SEQ_OUT + 2:
                    sp.wait_ge(halves_used, HALVES_IN)
                if n == SEQ_OUT + 4:
                    for t in range(NT):
                        sp.dma_start(X[:, t, :], x[0, t * P:(t + 1) * P, :]).then_inc(x_again, 16)
                if n == SEQ_XO:
                    sp.wait_ge(halves_used, HALVES_IN + 32)
                    for j in range(8):
                        sp.dma_start(slot(expert_slot(j)).rearrange("p (k n) -> p k n", n=FF),
                                     expert_chunk(0, j)).then_inc(landed[expert_slot(j)], 16)
                last = [m for m in range(n) if early[m][0] == s]
                if last:
                    sp.wait_ge(used, last[-1] + 1)
                sp.dma_start(slot(s).rearrange("p (k n) -> p k n", n=width), src).then_inc(landed[s], 16)
            for j in range(8, 12):
                s = expert_slot(j)
                sp.wait_ge(o_done, 28)
                sp.dma_start(slot(s).rearrange("p (k n) -> p k n", n=D), expert_chunk(0, j)).then_inc(landed[s], 16)

            def load_expert(e, b):
                for j in range(12):
                    s = expert_slot(j)
                    sp.wait_ge(used, b * 12 + (UE - 12 + j + 1))
                    sp.dma_start(slot(s).rearrange("p (k n) -> p k n", n=FF if j < 8 else D),
                                 expert_chunk(e, j)).then_inc(landed[s], 16)

            with sp.Fori(1, NE) as b:
                load_expert(b, b)
            sp.wait_ge(table_ready, 1)
            more = sp.value_load(meta[0:1, NOVER:NOVER + 1], min_val=0, max_val=NOVER)
            with sp.If(more > 0):
                with sp.Fori(0, NOVER) as j:
                    e = sp.value_load(meta[0:1, ds(j, 1)], min_val=0, max_val=NE - 1)
                    load_expert(e, j + NE)
            for t in range(NT):
                sp.wait_ge(sum_ready, 4 * t + 4)
                sp.dma_start(out[0, t * P:(t + 1) * P, :], X[:, t, :]).then_inc(stored, 16)
            sp.wait_ge(stored, 16 * NT)

        @block.gpsimd
        def _(pool):
            links = [0]

            def link(ins):
                links[0] += 1
                ins.then_inc(pool_link, 1)
                pool.wait_ge(pool_link, links[0])

            g = nc.gpsimd
            g.memset(ones[:, :], 1.0).then_inc(consts, 1)
            g.memset(eps[:, :], EPS).then_inc(eps_set, 1)
            g.iota(io[:, :], pattern=[[1, 64]], base=0, channel_multiplier=0,
                   allow_small_or_imprecise_dtypes=True).then_inc(consts, 1)
            g.iota(tok[:, :], pattern=[[P, NT]], base=0, channel_multiplier=1,
                   allow_small_or_imprecise_dtypes=True).then_inc(consts, 1)
            link(g.memset(ident[:, :], 0.0))
            g.affine_select(out=ident[:, :], in_=ident[:, :], compare_op=ALU.not_equal, fill=1.0, base=0,
                            pattern=[[-1, P]], channel_multiplier=1).then_inc(consts, 1)
            link(g.memset(blk[:, :], 0.0))
            g.memset(blk[0:HD, 0:HD], 1.0).then_inc(consts, 1)
            g.memset(blk[HD:P, HD:P], 1.0).then_inc(consts, 1)

            for i in range(4 * NT):
                t, b = i // 4, i % 4
                pool.wait_ge(h_cut, i + 1)
                g.tensor_tensor(h_lo[:, t, 4 * b:4 * b + 4, :], mix_shape(whole[:, i % 2, :], 0),
                                mix_shape(high[:, i % 2, :], 0), ALU.subtract).then_inc(h_lo_ready, 1)

            pool.wait_ge(kx_ready, 2)
            pool.wait_ge(used, 8)
            g.memset(kdup[:, :, 0:CHUNK], 0.0).then_inc(k_padded, 1)
            g.memset(vTp[:, 0:CHUNK], 0.0).then_inc(k_padded, 1)
            link(g.memset(wsum[:, :, 0:16], 0.0))
            g.iota(cnt16, pattern=[[1, 16]], base=1, channel_multiplier=0,
                   allow_small_or_imprecise_dtypes=True).then_inc(ramp_in, 1)
            link(g.iota(mask, pattern=[[-1, WIN]], base=CHUNK, channel_multiplier=1,
                        allow_small_or_imprecise_dtypes=True))
            link(g.tensor_scalar(dist, mask, -1.0, 0.0, ALU.mult, ALU.max))
            link(g.tensor_scalar(mask, mask, 0.0, None, ALU.max))
            link(g.tensor_tensor(dist, dist, mask, ALU.add))
            link(g.memset(mask, 0.0))
            link(g.memset(mask[0:CHUNK, 2 * CHUNK:3 * CHUNK], NEG))
            link(g.memset(mask[CHUNK:P, 0:CHUNK], NEG))
            for h in range(NH):
                slope = 2.0 ** (-8.0 * (head_at(h) + 1) / NH)
                for at, n, col in WINDOW[h % 2]:
                    part = bias[:, h, at:at + n]
                    link(g.tensor_scalar(part, dist[:, col:col + n], -slope, None, ALU.mult))
                    link(g.tensor_tensor(part, part, mask[:, col:col + n], ALU.add))
            pairs = bias.rearrange("p (j e) n -> p j (e n)", e=2)
            before = [pairs[:, :, 0:CHUNK], pairs[:, :, WIN + CHUNK:WIN + 2 * CHUNK]]
            for part in before:
                g.memset(part, NEG).then_inc(bias_built, 1)
            pool.wait_ge(scores_read, 8)
            for part in before:
                g.memset(part[CHUNK:P], NEG).then_inc(bias_reset, 1)
            for h in range(NH):
                slope = 2.0 ** (-8.0 * (head_at(h) + 1) / NH)
                part = before[h % 2][0:CHUNK, h // 2, :]
                link(g.iota(part, pattern=[[-1, CHUNK]], base=CHUNK, channel_multiplier=1,
                            allow_small_or_imprecise_dtypes=True))
                g.tensor_scalar(part, part, -slope, None, ALU.mult).then_inc(bias_reset, 1)

            pool.wait_ge(ramp_ready, 1)
            for i in range(8):
                lv = i // 2 + 1
                w = 2 ** lv
                u = proj[:, 10 + i, :]
                pool.wait_ge(u_ready, i + 1)
                g.tensor_copy(wsum[:, 0, 16:17], u[:, 0:1])
                link(g.tensor_tensor(wsum[:, 0, 17:528], u[:, 1:512], u[:, 0:511], ALU.add))
                for n in range(1, lv):
                    a, b, sh = (n - 1) % 2, n % 2, 2 ** n
                    link(g.tensor_tensor(wsum[:, b, 16:528], wsum[:, a, 16:528],
                                         wsum[:, a, 16 - sh:528 - sh], ALU.add))
                c = (lv - 1) % 2
                link(g.tensor_tensor(wsum[:, c, 16:32], wsum[:, c, 16:32], ramp[:, lv - 1, :], ALU.mult))
                link(g.tensor_scalar(wsum[:, c, 16:528], wsum[:, c, 16:528], 1.0 / w, None, ALU.mult))
                g.tensor_tensor(u, wsum[:, c, 16:528], u, ALU.subtract).then_inc(d_ready, 1)
                pool.wait_ge(d_ready, i + 1)

            pool.wait_ge(used, SEQ_POOL + 1)
            link(g.memset(tri, 1.0))
            g.affine_select(out=tri, in_=tri, compare_op=ALU.is_gt, fill=0.0, base=0,
                            pattern=[[1, P]], channel_multiplier=-1).then_inc(tri_ready, 1)
            for grp in range(NG):
                pool.dma_start(wr[:, :, NG + grp * EPG:NG + (grp + 1) * EPG],
                               router_expert_w[0, grp].rearrange("(k p) e -> p k e", p=P)).then_inc(router_in, 16)
            pool.dma_start(wr[:, :, 0:NG], router_group_w[0].rearrange("(k p) e -> p k e", p=P)).then_inc(router_in, 16)

            for t in range(NT):
                pool.wait_ge(rows_ready, t + 1)
                pool.dma_start(hn_dram[t * P:(t + 1) * P, :], hs[:, t % 2, :]).then_inc(hn_stored[t % 2], 16)
            for b in range(2):
                pool.wait_ge(hn_stored[b], 32)
            pool.wait_ge(h_turned, 4 * 14)
            g.memset(hs[:, :, :], 0.0).then_inc(xs_clear, 1)
            pool.wait_ge(xs_clear, 1)
            pool.wait_ge(table_ready, 1)
            xs = hs

            def reg(value):
                return value if isinstance(value, int) else pool.to_reg(value)

            g.iota(tramp, pattern=[[1, S]], base=0, channel_multiplier=0,
                   allow_small_or_imprecise_dtypes=True).then_inc(tramp_ready, 1)
            g.tensor_copy(cols[:, 0:1], tidx[:, 0:1]).then_inc(idx_copied, 1)
            pool.wait_ge(idx_copied, 1)
            g.indirect_dma_start(out=xs[0:SLOTS, 0, :], out_offset=None, in_=hn_dram,
                                 in_offset=bass.IndirectOffsetOnAxis(ap=cols[:, 0:1], axis=0),
                                 bounds_check=S - 1, oob_is_err=False).then_inc(gathered[0], 16)

            def step(b, par):
                wait_past(pool, xs_turned, b * 2)
                g.tensor_copy(cols[:, 1 - par:2 - par], tidx[:, ds(b + 1, 1)]).then_inc(idx_copied, 1)
                copied = reg(b + 2)
                pool.wait_ge(table_ready, 1)
                pool.wait_ge(idx_copied, copied)
                g.indirect_dma_start(out=xs[0:SLOTS, 1 - par, :], out_offset=None, in_=hn_dram,
                                     in_offset=bass.IndirectOffsetOnAxis(ap=cols[:, 1 - par:2 - par], axis=0),
                                     bounds_check=S - 1, oob_is_err=False).then_inc(gathered[1 - par], 16)

            step(0, 0)
            step(1, 1)
            with pool.Fori(1, NE // 2) as it:
                b = it * 2
                step(b, 0)
                step(b + 1, 1)
            pool.wait_ge(gathered[0], 16 * (NE // 2 + 1))
            more = pool.value_load(meta[0:1, NOVER:NOVER + 1], min_val=0, max_val=NOVER)
            with pool.If(more > 0):
                with pool.Fori(NE // 2, NBLK // 2) as it:
                    b = it * 2
                    step(b, 0)
                    step(b + 1, 1)
                pool.wait_ge(gathered[0], 16 * (NBLK // 2 + 1))

        @block.scalar
        def _(act):
            a = nc.scalar
            links = [0]

            def link(ins):
                links[0] += 1
                ins.then_inc(act_link, 1)
                act.wait_ge(act_link, links[0])

            grow = PB[0:NGR, 8192:8192 + P]
            for r0, v in ((G_MIX, mix_norm_g), (G_XAT, xattn_norm_g), (G_MEM, mem_norm_g), (G_FFN, ffn_norm_g),
                          (G_POOL, pool_scale)):
                act.dma_start(grow[r0:r0 + v.shape[1] // P, :], v[0].rearrange("(k p) -> k p", p=P)).then_inc(gain_in, 16)
            for r0, v in ((G_Q, q_norm_g), (G_K, k_norm_g)):
                for c in range(2):
                    act.dma_start(grow[r0:r0 + 1, c * HD:(c + 1) * HD], v[0:1, :]).then_inc(gain_in, 16)
            for r0, v in ((G_XQ, xq_norm_g), (G_XK, xk_norm_g)):
                act.dma_start(grow[r0:r0 + 1, :], v[0:1, :]).then_inc(gain_in, 16)
            act.dma_start(sink[:, :], sink_logits[0:1, :].broadcast_to([P, NH])).then_inc(small_in, 16)
            act.dma_start(rbias[:, 0:NG], router_group_b[0:1, :].broadcast_to([P, NG])).then_inc(small_in, 16)
            act.dma_start(rbias[:, NG:NCOL], router_expert_b.rearrange("l g e -> l (g e)").broadcast_to([P, NE])
                          ).then_inc(small_in, 16)
            act.wait_ge(eps_set, 1)

            def root_of(T):
                act.wait_ge(ssq_done, T + 1)
                a.activation(stat[:, 1, T:T + 1], stat[:, 0, T:T + 1], ACT.Sqrt, bias=eps[:, 0:1],
                             scale=1.0 / D).then_inc(root_done, 1)

            def square_sum(T, src):
                a.activation(hs[:, T % 2, :], src, ACT.Square, accum_out=stat[:, 0, T:T + 1]).then_inc(ssq_done, 1)

            def square_parts(stage):
                with act.Fori(0, 4) as n:
                    for t in range(NT):
                        act.wait_ge(x_added, n * 4 + (16 * stage + t + 1))
                        a.activation(hs[:, 0, t * 512:(t + 1) * 512], X[:, t, ds(n * 512, 512)], ACT.Square,
                                     accum_out=psq[:, stage, t, ds(n, 1)]).then_inc(parts_done, 1)
                    act.wait_ge(parts_done, n * 4 + (16 * stage + 4))

            def squares_of(n, stage):
                for t in range(NT):
                    act.wait_ge(x_added, 16 * stage + 4 * n + t + 1)
                    if n > 0 and t == 0:
                        act.wait_ge(parts_done, 16 * stage + 4 * n)
                    a.activation(hs[:, 0, t * 512:(t + 1) * 512], X[:, t, n * 512:(n + 1) * 512], ACT.Square,
                                 accum_out=psq[:, stage, t, n:n + 1]).then_inc(parts_done, 1)

            for t in range(2):
                act.wait_ge(mem_in[t], 16)
                square_sum(t, memx[:, t, :])
                root_of(t)
            for t in range(NT):
                act.wait_ge(x_in[t], 16)
                square_sum(2 + t, X[:, t, :])
                root_of(2 + t)
            act.wait_ge(used, 4)
            for b in range(2):
                a.activation(sqm[:, b * 512:(b + 1) * 512], ps[:, 4 + b, :], ACT.Square).then_inc(xk_sq, 1)
            for b in range(2):
                act.wait_ge(xk_ss, b + 1)
                a.activation(rtm[:, b * 512:(b + 1) * 512], ps[:, b, :], ACT.Sqrt, bias=eps[:, 0:1],
                             scale=1.0 / XD).then_inc(xk_root, 1)
            act.wait_ge(used, 8)
            for m in range(2):
                a.activation(vx[:, m, :], ps[:, 6 + m, :], ACT.Copy).then_inc(vx_ready, 1)

            for i in range(4 * NT):
                t, b = i // 4, i % 4
                act.wait_ge(h_cut, i + 1)
                a.activation(mix_hi[:, 4 * b:4 * b + 4, t * P:(t + 1) * P], mix_shape(high[:, i % 2, :], 0),
                             ACT.Copy).then_inc(h_hi_ready, 1)

            def tile_high(v, half):
                act.wait_ge(wcut, v + 1)
                if v >= 2:
                    act.wait_ge(halves_used, v - 1)
                a.activation(in_hi[:, half], inhigh, ACT.Copy).then_inc(w_hi_ready, 1)

            def squares(n):
                act.wait_ge(halves_used, n * 2 + 2)
                if n >= 2:
                    act.wait_ge(q_ss, n - 1)
                a.activation(sq[:, n % 2, :], ps[:, 4 + (n - 1) % 4, :], ACT.Square).then_inc(q_sq, 1)

            def root(n):
                act.wait_ge(q_ss, n + 1)
                if n >= 2:
                    act.wait_ge(q_ready, n - 1)
                a.activation(rt[:, n % 2, :], ps[:, (n - 1) % 4, :], ACT.Sqrt, bias=eps[:, 0:1],
                             scale=1.0 / HD).then_inc(q_root, 1)

            act.wait_ge(kx_ready, 2)
            for v_ in range(3):
                tile_high(v_, v_ % 2)
            squares(0)
            tile_high(3, 1)
            tile_high(4, 0)
            for n in range(1, 9):
                squares(n)
                tile_high(2 * n + 3, 1)
                root(n - 1)
                tile_high(2 * n + 4, 0)
            root(8)
            act.wait_ge(halves_used, 20)
            a.activation(vTp[:, CHUNK:CHUNK + S], ps[:, 5, :], ACT.Copy).then_inc(v_copied, 1)
            tile_high(21, 1)
            act.wait_ge(v_turned, 2)
            a.activation(vA[:, :, :], ps[:, 6, :].rearrange("p (t c) -> p t c", t=NT), ACT.Copy).then_inc(v_ready, 1)

            for i in range(8):
                act.wait_ge(max_done, 2 * i + 2)
                for h in range(8):
                    a.activation(Ssb[:, h, :], Ssb[:, h, :], ACT.Exp, bias=sm[:, 1, h:h + 1],
                                 accum_out=sm[:, 2, h:h + 1]).then_inc(exp_done, 1)
                a.activation(sm[:, 4, :], sm[:, 3, :], ACT.Exp).then_inc(exp_done, 1)
                if i < 7:
                    tile_high(2 * i + 22, 0)
                act.wait_ge(halves_used, 2 * i + 22)
                a.activation(proj[:, 10 + i, :], ps[:, 4, :], ACT.Copy).then_inc(u_ready, 1)
                for j in (1, 3):
                    act.wait_ge(pt_turned, 4 * i + j + 1)
                    a.activation(PT[:, j, :], ps[:, j, 0:384], ACT.Copy).then_inc(pt_act, 1)
                if i < 7:
                    tile_high(2 * i + 23, 1)
            def mix_high(i):
                act.wait_ge(high_cut, i + 1)
                a.activation(mix_part(mix_hi, i), mix_shape(high[:, i % 2, :], i), ACT.Copy).then_inc(mix_hi_ready, 1)

            def weights_high(u):
                act.wait_ge(wcut, HALVES_IN + u + 1)
                if u >= 2:
                    act.wait_ge(halves_used, HALVES_IN + u - 1)
                a.activation(w_hi[:, u % 2], whigh, ACT.Copy).then_inc(w_hi_ready, 1)

            for i in range(16):
                if i < 8:
                    act.wait_ge(a_turned, i + 1)
                elif i < 15:
                    act.wait_ge(pool_done, i - 7)
                else:
                    act.wait_ge(used, SEQ_POOL + 1)
                if i >= 2:
                    act.wait_ge(mix_lo_ready, i - 1)
                if i < 8:
                    a.activation(whole[:, i % 2, :], ps[:, i % 4, :], ACT.Copy).then_inc(whole_ready, 1)
                else:
                    a.activation(whole[:, i % 2, :], ps[:, 4 + i % 4, :], ACT.Copy,
                                 scale=gT[:, G_POOL + i - 8:G_POOL + i - 7]).then_inc(whole_ready, 1)
                if i > 0:
                    mix_high(i - 1)
                if i == 8:
                    weights_high(0)
                    weights_high(1)
            mix_high(15)
            for u in range(2, 8 * 4):
                weights_high(u)
                if u % 8 == 4 and u > 8:
                    squares_of(u // 8 - 1, 0)
            squares_of(3, 0)

            for t in range(NT):
                root_of(6 + t)
            for f in range(XH):
                act.wait_ge(*((xq_done, f + 1) if f < 3 else (used, SEQ_XQ + 4)))
                if f >= 2:
                    act.wait_ge(xq_ss, f - 1)
                a.activation(sqx[:, f % 2, :], ps[:, 4 + f, :], ACT.Square).then_inc(xq_sq, 1)
                act.wait_ge(xq_ss, f + 1)
                if f >= 2:
                    act.wait_ge(qx_ready, f - 1)
                a.activation(rtx[:, f % 2, :], ps[:, f, :], ACT.Sqrt, bias=eps[:, 0:1], scale=1.0 / XD
                             ).then_inc(xq_root, 1)
            act.wait_ge(qx_ready, XH)

            def xexps(t):
                act.wait_ge(xmax_done, t + 1)
                for h in range(XH):
                    c = (t % 2) * 4 + h
                    a.activation(SX[:, t % 2, h * NM:(h + 1) * NM],
                                 ps[:, 5 * (t % 2) + h // 2, (h % 2) * NM:(h % 2 + 1) * NM], ACT.Exp,
                                 bias=sm[:, 1, c:c + 1], scale=XD ** -0.5,
                                 accum_out=sm[:, 2, c:c + 1]).then_inc(xexp_done, 1)

            xexps(0)
            for t in range(NT):
                if t + 1 < NT:
                    xexps(t + 1)
                act.wait_ge(xp_turned, 2 * t + 1)
                a.activation(PTX[:, 0:512], ps[:, 2, :], ACT.Copy).then_inc(xpt_act, 1)

            square_parts(1)
            for t in range(NT):
                root_of(10 + t)
            for t in range(NT):
                act.wait_ge(rstd_done, 10 + t + 1)
                if t >= 2:
                    act.wait_ge(hn_stored[t % 2], 16)
                a.activation(hs[:, t % 2, :], X[:, t, :], ACT.Copy, scale=stat[:, 2, 10 + t:11 + t]).then_inc(rows_ready, 1)

            act.wait_ge(gmax_done, 1)
            a.activation(rq["eg"], rq["gs"], ACT.Exp).then_inc(gexp_done, 1)
            act.wait_ge(top_done, 1)
            a.activation(rq["et"], rq["dt"], ACT.Exp).then_inc(texp_done, 1)

            def block_act(b, par):
                act.wait_ge(used, b * 12 + (UE + 8))
                a.activation(gu, ps[:, 0, :], ACT.Copy).then_inc(gu_copied, 1)
                act.wait_ge(gu_turned, b + 1)
                wait_past(act, act_ready, b)
                a.activation(sil.rearrange("p (f n) -> p f n", n=SLOTS), guT[:, :, 0:SLOTS],
                             ACT.Silu).then_inc(sil_ready, 1)
                act.wait_ge(used, b * 12 + (UE + 12))
                a.activation(y[par * SLOTS:(par + 1) * SLOTS, 0:4:2, :], ps[0:SLOTS, 4:6, :], ACT.Copy).then_inc(y_act, 1)

            act.wait_ge(table_ready, 1)
            block_act(0, 0)
            block_act(1, 1)
            with act.Fori(1, NE // 2) as it:
                b = it * 2
                block_act(b, 0)
                block_act(b + 1, 1)
            more = act.value_load(meta[0:1, NOVER:NOVER + 1], min_val=0, max_val=NOVER)
            with act.If(more > 0):
                with act.Fori(NE // 2, NBLK // 2) as it:
                    b = it * 2
                    block_act(b, 0)
                    block_act(b + 1, 1)

        @block.vector
        def _(dve):
            v = nc.vector
            links = [0]

            def link(ins):
                links[0] += 1
                ins.then_inc(dve_link, 1)
                dve.wait_ge(dve_link, links[0])

            def wide(ap, *shape):
                return ap.broadcast_to(list(shape))

            def scale_of(T):
                dve.wait_ge(root_done, T + 1)
                v.reciprocal(stat[:, 2, T:T + 1], stat[:, 1, T:T + 1]).then_inc(rstd_done, 1)
                dve.wait_ge(rstd_done, T + 1)
                if T >= 2:
                    dve.wait_ge(h_turned, 4 * T - 4)
                v.tensor_scalar(dg[:, T % 2, :], ident[:, :], stat[:, 2, T:T + 1], None, ALU.mult).then_inc(diag_ready, 1)

            def sum_parts(T, stage):
                dve.wait_ge(parts_done, 16 * stage + 12 + (T - 6) % 4 + 1)
                v.tensor_reduce(stat[:, 0, T:T + 1], psq[:, stage, (T - 6) % 4, :], AX, ALU.add).then_inc(ssq_done, 1)

            def turned(T, dstT, at, gcol):
                for b in range(4):
                    dve.wait_ge(h_turned, T * 4 + b + 1)
                    v.tensor_tensor(dstT[:, 4 * b:4 * b + 4, at:at + P],
                                    ps[:, b, :].rearrange("p (k n) -> p k n", n=P),
                                    wide(gT[:, gcol + 4 * b:gcol + 4 * b + 4].unsqueeze(2), P, 4, P),
                                    ALU.mult).then_inc(hT_ready, 1)

            def norm_tiles(T0, count, dstT, gcol):
                for t in range(min(2, count)):
                    scale_of(T0 + t)
                for t in range(count):
                    turned(T0 + t, dstT, t * P, gcol)
                    if t + 2 < count:
                        scale_of(T0 + t + 2)

            dve.wait_ge(gain_turned, 1)
            v.tensor_copy(gT[:, :], ps[:, 7, 0:NGR]).then_inc(gains, 1)
            dve.wait_ge(gains, 1)
            norm_tiles(0, 2, memT, G_MEM)
            for b in range(2):
                dve.wait_ge(xk_root, b + 1)
                link(v.reciprocal(rtm[:, b * 512:(b + 1) * 512], rtm[:, b * 512:(b + 1) * 512]))
                v.scalar_tensor_tensor(out=kx[:, 2 * b:2 * b + 2, :].rearrange("p h n -> p (h n)"),
                                       in0=ps[:, 4 + b, :], scalar=gT[:, G_XK:G_XK + 1],
                                       in1=rtm[:, b * 512:(b + 1) * 512],
                                       op0=ALU.mult, op1=ALU.mult).then_inc(kx_ready, 1)
            def turned_cut(t):
                for b in range(4):
                    i = 4 * t + b
                    dve.wait_ge(h_turned, (t + 2) * 4 + b + 1)
                    if i >= 2:
                        dve.wait_ge(h_lo_ready, i - 1)
                        dve.wait_ge(h_hi_ready, i - 1)
                    v.tensor_tensor(mix_shape(whole[:, i % 2, :], 0), ps[:, b, :].rearrange("p (k n) -> p k n", n=P),
                                    wide(gT[:, G_MIX + 4 * b:G_MIX + 4 * b + 4].unsqueeze(2), P, 4, P),
                                    ALU.mult).then_inc(hT_ready, 1)
                    dve.wait_ge(hT_ready, 8 + i + 1)
                    v.tensor_scalar(high[:, i % 2, :].bitcast(U32), whole[:, i % 2, :].bitcast(U32), HIGH, None,
                                    ALU.bitwise_and).then_inc(h_cut, 1)

            dve.wait_ge(root_done, 6)
            for t in range(2):
                scale_of(2 + t)
            for t in range(NT):
                turned_cut(t)
                if t + 2 < NT:
                    scale_of(4 + t)

            def cut_tile(v_, s, half):
                raw = slot(s).rearrange("p (k n) -> p k n", n=P)[:, 8 * half:8 * half + 8, :]
                if half == 0:
                    chunk_landed(dve, SEQ_K + v_ // 2)
                if v_ > 0:
                    dve.wait_ge(w_hi_ready, v_)
                    dve.wait_ge(w_lo_ready, v_)
                v.tensor_scalar(inhigh.bitcast(U32), raw.bitcast(U32), HIGH, None, ALU.bitwise_and).then_inc(wcut, 1)
                dve.wait_ge(wcut, v_ + 1)
                if v_ >= 2:
                    dve.wait_ge(halves_used, v_ - 1)
                v.tensor_tensor(in_lo[:, half], raw, inhigh, ALU.subtract).then_inc(w_lo_ready, 1)

            dve.wait_ge(used, 8)
            for v_ in range(3):
                cut_tile(v_, v_ // 2 % 2, v_ % 2)
            dve.wait_ge(ramp_in, 1)
            for lv in range(4):
                w = float(2 ** (lv + 1))
                link(v.tensor_scalar(ramp[:, lv, :], cnt16, w, None, ALU.min))
                link(v.reciprocal(ramp[:, lv, :], ramp[:, lv, :]))
                r = v.tensor_scalar(ramp[:, lv, :], ramp[:, lv, :], w, None, ALU.mult)
                if lv < 3:
                    link(r)
            r.then_inc(ramp_ready, 1)

            def normed_keys():
                dve.wait_ge(q_root, 1)
                link(v.reciprocal(rt[:, 0, :], rt[:, 0, :]))
                dve.wait_ge(k_padded, 2)
                for g in range(2):
                    half = slice(g * HD, (g + 1) * HD)
                    ins = v.scalar_tensor_tensor(out=kdup[half, g, CHUNK:CHUNK + S], in0=ps[half, 7, :],
                                                 scalar=gT[half, G_K:G_K + 1], in1=rt[half, 0, :],
                                                 op0=ALU.mult, op1=ALU.mult)
                    if g == 0:
                        link(ins)
                ins.then_inc(q_ready, 1)
                dve.wait_ge(q_ready, 1)
                for g in range(2):
                    v.tensor_copy(kdup[(1 - g) * HD:(2 - g) * HD, g, CHUNK:CHUNK + S],
                                  kdup[g * HD:(g + 1) * HD, g, CHUNK:CHUNK + S]).then_inc(k_ready, 1)

            def normed_queries(n):
                dve.wait_ge(q_root, n + 1)
                link(v.reciprocal(rt[:, n % 2, :], rt[:, n % 2, :]))
                v.scalar_tensor_tensor(out=proj[:, n - 1, :], in0=ps[:, 4 + (n - 1) % 4, :], scalar=gT[:, G_Q:G_Q + 1],
                                       in1=rt[:, n % 2, :], op0=ALU.mult, op1=ALU.mult).then_inc(q_ready, 1)

            cut_tile(3, 1, 1)
            cut_tile(4, 0, 0)
            for n in range(1, 9):
                cut_tile(2 * n + 3, (n + 1) % 2, 1)
                if n == 1:
                    normed_keys()
                else:
                    normed_queries(n - 1)
                cut_tile(2 * n + 4, n % 2, 0)
            normed_queries(8)
            dve.wait_ge(q_ready, 9)
            link(v.memset(vB[:, :, :, :], 0.0))
            cut_tile(21, 0, 1)

            for i in range(8):
                t, g = i // 2, i % 2
                if i == 0:
                    dve.wait_ge(bias_built, 2)
                    dve.wait_ge(small_in, 48)
                if i == 2:
                    dve.wait_ge(bias_reset, 2 + NH)
                for n, j in enumerate((0, 2, 1, 3)):
                    dve.wait_ge(scores_done, 4 * i + n + 1)
                    v.scalar_tensor_tensor(out=Ssb[:, 2 * j:2 * j + 2, :],
                                           in0=ps[:, j, 0:2 * WIN].rearrange("p (h n) -> p h n", n=WIN),
                                           scalar=HD ** -0.5, in1=bias[:, 8 * g + 2 * j:8 * g + 2 * j + 2, :],
                                           op0=ALU.mult, op1=ALU.add).then_inc(scores_read, 1)
                dve.wait_ge(scores_read, 4 * i + 4)
                link(v.tensor_reduce(sm[:, 0, :], Ssb[:, :, :], AX, ALU.max))
                sinks = sink[:, 8 * g:8 * g + 8].rearrange("p (a b) -> p b a", b=2)
                smv = sm[:, :, :].rearrange("p r (b a) -> p r b a", b=2)
                link(v.tensor_tensor(smv[:, 0], smv[:, 0], sinks, ALU.max))
                v.tensor_scalar(sm[:, 1, :], sm[:, 0, :], -1.0, None, ALU.mult).then_inc(max_done, 1)
                v.tensor_tensor(smv[:, 3], sinks, smv[:, 0], ALU.subtract).then_inc(max_done, 1)
                if i == 0:
                    dve.wait_ge(v_turned, 2)
                    for g_ in range(2):
                        v.tensor_copy(vB[g_ * HD:(g_ + 1) * HD, g_, :, :],
                                      ps[0:HD, 7, :].rearrange("p (t c) -> p t c", t=NT)).then_inc(v_ready, 1)
                if i < 7:
                    cut_tile(2 * i + 22, (i + 1) % 2, 0)
                dve.wait_ge(exp_done, 9 * i + 9)
                link(v.tensor_tensor(sm[:, 5, :], sm[:, 2, :], sm[:, 4, :], ALU.add))
                link(v.reciprocal(sm[:, 5, :], sm[:, 5, :]))
                for j in (0, 2):
                    dve.wait_ge(pt_turned, 4 * i + j + 1)
                    v.tensor_copy(PT[:, j, :], ps[:, j, 0:384]).then_inc(pt_dve, 1)
                if i < 7:
                    cut_tile(2 * i + 23, (i + 1) % 2, 1)
                dve.wait_ge(pv_done, i + 1)
                v.tensor_tensor(a_rows[:, t, g * 512:(g + 1) * 512].rearrange("p (a b d) -> p b a d", b=2, d=HD),
                                ps[:, 5, :].rearrange("p (b a d) -> p b a d", b=2, d=HD),
                                wide(smv[:, 5].unsqueeze(3), P, 2, 4, HD), ALU.mult).then_inc(a_ready, 1)
            def cut_mix(i):
                dve.wait_ge(whole_ready, i + 1)
                if i >= 2:
                    dve.wait_ge(mix_hi_ready, i - 1)
                    dve.wait_ge(mix_lo_ready, i - 1)
                v.tensor_scalar(high[:, i % 2, :].bitcast(U32), whole[:, i % 2, :].bitcast(U32), HIGH, None,
                                ALU.bitwise_and).then_inc(high_cut, 1)
                dve.wait_ge(high_cut, i + 1)
                v.tensor_tensor(mix_part(mix_lo, i), mix_shape(whole[:, i % 2, :], i), mix_shape(high[:, i % 2, :], i),
                                ALU.subtract).then_inc(mix_lo_ready, 1)

            def cut_weights(u):
                n = SEQ_OUT + u // 2
                raw = chunk(n, 512)[:, 2 * (u % 2):2 * (u % 2) + 2, :]
                if u % 2 == 0:
                    chunk_landed(dve, n)
                dve.wait_ge(w_hi_ready, HALVES_IN + u)
                dve.wait_ge(w_lo_ready, HALVES_IN + u)
                v.tensor_scalar(whigh.bitcast(U32), raw.bitcast(U32), HIGH, None, ALU.bitwise_and).then_inc(wcut, 1)
                dve.wait_ge(wcut, HALVES_IN + u + 1)
                if u >= 2:
                    dve.wait_ge(halves_used, HALVES_IN + u - 1)
                v.tensor_tensor(w_lo[:, u % 2], raw, whigh, ALU.subtract).then_inc(w_lo_ready, 1)

            def add_out(n, par, cross):
                for t in range(NT):
                    if cross:
                        dve.wait_ge(o_done, n * 4 + (12 + t + 1))
                    elif t < 3:
                        dve.wait_ge(o_done, n * 3 + (t + 1))
                    else:
                        dve.wait_ge(halves_used, HALVES_IN + n * 8 + 8)
                    xs_ = X[:, t, ds(n * 512, 512)]
                    v.tensor_tensor(xs_, ps[:, 4 * par + t, :], xs_, ALU.add).then_inc(x_added, 1)

            for i in range(16):
                cut_mix(i)
                if i == 7:
                    cut_weights(0)
                    cut_weights(1)
            for u in range(2, 8 * 4):
                cut_weights(u)
                if u == 8:
                    dve.wait_ge(x_again, 16 * NT)
                if u % 8 == 0:
                    add_out(u // 8 - 1, (u // 8 - 1) % 2, False)
            add_out(3, 1, False)

            for t in range(NT):
                sum_parts(6 + t, 0)
            norm_tiles(6, NT, H, G_XAT)
            for f in range(XH):
                dve.wait_ge(xq_root, f + 1)
                link(v.reciprocal(rtx[:, f % 2, :], rtx[:, f % 2, :]))
                v.scalar_tensor_tensor(out=qx[:, f, :], in0=ps[:, 4 + f, :], scalar=gT[:, G_XQ:G_XQ + 1],
                                       in1=rtx[:, f % 2, :], op0=ALU.mult, op1=ALU.mult).then_inc(qx_ready, 1)

            def xmax(t):
                c = slice(4 * (t % 2), 4 * (t % 2) + 4)
                dve.wait_ge(xs_done, t + 1)
                b0 = 5 * (t % 2)
                link(v.tensor_reduce(sm[:, 0, c], ps[:, b0:b0 + 2, :].rearrange("p b (h n) -> p (b h) n", n=NM),
                                     AX, ALU.max))
                v.tensor_scalar(sm[:, 1, c], sm[:, 0, c], -(XD ** -0.5), None, ALU.mult).then_inc(xmax_done, 1)

            def xnorm(t):
                c = slice(4 * (t % 2), 4 * (t % 2) + 4)
                dve.wait_ge(xexp_done, 4 * t + 4)
                link(v.reciprocal(sm[:, 5, c], sm[:, 2, c]))
                sx = SX[:, t % 2, :].rearrange("p (h n) -> p h n", n=NM)
                v.tensor_tensor(sx, sx, wide(sm[:, 5, c].unsqueeze(2), P, XH, NM), ALU.mult).then_inc(xp_ready, 1)

            xmax(0)
            xnorm(0)
            xmax(1)
            for t in range(NT):
                dve.wait_ge(xp_turned, 2 * t + 2)
                v.tensor_copy(PTX[:, 512:1024], ps[:, 3, :]).then_inc(xpt_dve, 1)
                dve.wait_ge(xo_part, t + 1)
                v.tensor_copy(H[:, 0:XH, t * P:(t + 1) * P],
                              ps[:, 4 + 3 * (t % 2), :].rearrange("p (h n) -> p h n", n=P)).then_inc(oT_ready, 1)
                if t + 1 < NT:
                    xnorm(t + 1)
                if t + 2 < NT:
                    xmax(t + 2)
            with dve.Fori(0, 2) as it:
                n = it * 2
                for par in range(2):
                    add_out(n + par, par, True)
            for t in range(NT):
                sum_parts(10 + t, 1)
            norm_tiles(10, NT, H, G_FFN)

            r = rq
            dve.wait_ge(logits_done, 1)
            link(v.tensor_tensor(r["L"], ps[:, 4, 0:NT * NCOL].rearrange("p (t c) -> p t c", c=NCOL),
                                 wide(rbias[:, :].unsqueeze(1), P, NT, NCOL), ALU.add))
            LG = r["L"][:, :, 0:NG]
            LE = r["L"][:, :, NG:NCOL].rearrange("p t (g e) -> p t g e", e=EPG)

            def top(vals, width, best, pick, cand):
                link(v.tensor_reduce(best, vals, AX, ALU.max))
                link(v.tensor_tensor(pick, vals, wide(best.unsqueeze(2), P, NT, width), ALU.is_equal))
                link(v.scalar_tensor_tensor(out=cand, in0=pick, scalar=-64.0,
                                            in1=wide(io[:, 0:width].unsqueeze(1), P, NT, width),
                                            op0=ALU.mult, op1=ALU.add))
                link(v.tensor_reduce(r["ti"], cand, AX, ALU.min))
                link(v.tensor_tensor(pick, cand, wide(r["ti"].unsqueeze(2), P, NT, width), ALU.is_equal))

            top(LG, NG, r["gm"], r["gh"], r["cand"][:, :, 0:NG])
            v.tensor_tensor(r["gs"], LG, wide(r["gm"].unsqueeze(2), P, NT, NG), ALU.subtract).then_inc(gmax_done, 1)
            link(v.tensor_tensor(r["tg"], LE, wide(r["gh"].unsqueeze(3), P, NT, NG, EPG), ALU.mult))
            link(v.tensor_reduce(r["es"], r["tg"].rearrange("p t g e -> p t e g"), AX, ALU.add))
            top(r["es"], EPG, r["m1"], r["h1"], r["cand"])
            link(v.scalar_tensor_tensor(out=r["t8"], in0=r["h1"], scalar=NEG, in1=r["es"], op0=ALU.mult, op1=ALU.add))
            top(r["t8"], EPG, r["m2"], r["h2"], r["cand"])
            v.tensor_tensor(r["dt"], r["m2"], r["m1"], ALU.subtract).then_inc(top_done, 1)
            for k, name in enumerate(("M1", "M2")):
                link(v.tensor_tensor(r[name].rearrange("p t (g e) -> p t g e", e=EPG),
                                     wide(r["gh"].unsqueeze(3), P, NT, NG, EPG),
                                     wide(r["h1" if k == 0 else "h2"].unsqueeze(2), P, NT, NG, EPG), ALU.mult))
            v.tensor_tensor(r["M"], r["M1"], r["M2"], ALU.add).then_inc(picks, 1)
            dve.wait_ge(gexp_done, 1)
            link(v.tensor_reduce(r["gsum"], r["eg"], AX, ALU.add))
            link(v.reciprocal(r["gg"], r["gsum"]))
            dve.wait_ge(texp_done, 1)
            link(v.tensor_scalar(r["w2"], r["et"], 1.0, None, ALU.add))
            link(v.reciprocal(r["w2"], r["w2"]))
            link(v.tensor_tensor(r["w1"], r["gg"], r["w2"], ALU.mult))
            link(v.tensor_tensor(r["w2"], r["w1"], r["et"], ALU.mult))
            dve.wait_ge(ranks, 1)
            link(v.tensor_copy(r["R"], ps[:, 5, 0:(NT + 1) * NE].rearrange("p (t e) -> p t e", e=NE)))
            link(v.tensor_scalar(r["thr"], io[:, 1:1 + MORE], float(SLOTS), None, ALU.mult))
            link(v.tensor_tensor(r["cmp"], wide(r["R"][:, NT, :].unsqueeze(2), P, NE, MORE),
                                 wide(r["thr"].unsqueeze(1), P, NE, MORE), ALU.is_gt))
            link(v.tensor_reduce(r["over"], r["cmp"], AX, ALU.add))
            link(v.memset(r["ca"], 0.0))
            link(v.memset(r["cb"], 0.0))
            link(v.tensor_copy(r["ca"][:, 16:16 + NE], r["over"]))
            src, dst = r["ca"], r["cb"]
            for sh in (1, 2, 4, 8, 16):
                link(v.tensor_tensor(dst[:, 16:16 + NE], src[:, 16:16 + NE], src[:, 16 - sh:16 + NE - sh], ALU.add))
                src, dst = dst, src
            upto = src[:, 16:16 + NE]
            link(v.tensor_tensor(r["base"], upto, r["over"], ALU.subtract))
            for k in range(2):
                M = r["M1" if k == 0 else "M2"]

                def of_pick(dst_, table):
                    link(v.tensor_tensor(r["tmp"], table, M, ALU.mult))
                    link(v.tensor_reduce(dst_, r["tmp"], AX, ALU.add))

                of_pick(r["pos"], r["R"][:, 0:NT, :])
                of_pick(r["ob"], wide(r["base"].unsqueeze(1), P, NT, NE))
                of_pick(r["ek"], wide(io[:, 0:NE].unsqueeze(1), P, NT, NE))
                link(v.tensor_tensor(r["pc"], wide(r["pos"].unsqueeze(2), P, NT, MORE),
                                     wide(r["thr"].unsqueeze(1), P, NT, MORE), ALU.is_ge))
                link(v.tensor_reduce(r["q"], r["pc"], AX, ALU.add))
                link(v.scalar_tensor_tensor(out=r["row"], in0=r["q"], scalar=-float(SLOTS), in1=r["pos"],
                                            op0=ALU.mult, op1=ALU.add))
                link(v.tensor_scalar(r["z"], r["q"], 0.0, None, ALU.is_equal))
                link(v.scalar_tensor_tensor(out=r["bk"], in0=r["ob"], scalar=float(NE - 1), in1=r["q"],
                                            op0=ALU.add, op1=ALU.add))
                link(v.tensor_tensor(r["ek"], r["ek"], r["bk"], ALU.subtract))
                link(v.tensor_tensor(r["ek"], r["ek"], r["z"], ALU.mult))
                link(v.tensor_tensor(r["bk"], r["bk"], r["ek"], ALU.add))
                v.tensor_tensor(r["P1" if k == 0 else "P2"], wide(io[:, 0:SLOTS].unsqueeze(1), P, NT, SLOTS),
                                wide(r["row"].unsqueeze(2), P, NT, SLOTS), ALU.is_equal).then_inc(onehots, 1)
                link(v.tensor_tensor(r["one"], wide(io[:, 0:TCOL].unsqueeze(1), P, NT, TCOL),
                                     wide(r["bk"].unsqueeze(2), P, NT, TCOL), ALU.is_equal))
                link(v.tensor_scalar(r["val"], tok[:, :], 2.0, float(k + 1), ALU.mult, ALU.add))
                B = r["B1" if k == 0 else "B2"]
                v.tensor_tensor(B[:, :, 0:TCOL], r["one"], wide(r["val"].unsqueeze(2), P, NT, TCOL),
                                ALU.mult).then_inc(onehots, 1)
                v.tensor_tensor(B[:, :, TCOL:2 * TCOL], r["one"],
                                wide(r["w1" if k == 0 else "w2"].unsqueeze(2), P, NT, TCOL),
                                ALU.mult).then_inc(onehots, 1)
                dve.wait_ge(onehots, 3 * k + 3)
            link(v.tensor_tensor(r["ec"], wide(upto.unsqueeze(1), P, NOVER, NE),
                                 wide(io[:, 0:NOVER].unsqueeze(2), P, NOVER, NE), ALU.is_le))
            link(v.tensor_reduce(r["ev"][:, 0:NOVER], r["ec"], AX, ALU.add))
            link(v.tensor_scalar(r["ev"][:, 0:NOVER], r["ev"][:, 0:NOVER], float(NE - 1), None, ALU.min))
            link(v.tensor_copy(r["ev"][:, NOVER:NOVER + 1], upto[:, NE - 1:NE]))
            link(v.tensor_copy(meta, r["ev"][0:1, :]))
            dve.wait_ge(table_done, 1)
            link(v.tensor_copy(r["fin"][0:SLOTS, :], ps[0:SLOTS, 6, 0:2 * TCOL]))
            V = r["fin"][0:SLOTS, 0:TCOL]
            link(v.tensor_copy(gate[0:SLOTS, :], r["fin"][0:SLOTS, TCOL:2 * TCOL]))
            link(v.tensor_copy(gate[SLOTS:P, 0:TCOL - 1], r["fin"][0:SLOTS, TCOL + 1:2 * TCOL]))
            zero = r["one"][0:SLOTS, 0, :]
            yidx = r["one"][0:SLOTS, 1, :].bitcast(I32)
            link(v.tensor_scalar(zero, V, 0.0, float(EMPTY), ALU.is_equal, ALU.mult))
            link(v.scalar_tensor_tensor(out=V, in0=V, scalar=-1.0, in1=zero, op0=ALU.add, op1=ALU.add))
            link(v.tensor_copy(yidx, V))
            link(v.tensor_scalar(tidx, yidx, 1, None, ALU.logical_shift_right))
            link(v.tensor_copy(tokf[0:SLOTS, :], tidx))
            v.tensor_copy(tokf[SLOTS:P, 0:TCOL - 1], tidx[:, 1:TCOL]).then_inc(table_ready, 1)

            def turn_evac(b, par):
                for q in range(2):
                    dve.wait_ge(xs_turned, b * 2 + (q + 1))
                    v.tensor_tensor(xsT[:, par, 8 * q:8 * q + 8, :],
                                    ps[:, 2 + q, 0:8 * SLOTS].rearrange("p (k n) -> p k n", n=SLOTS),
                                    wide(gT[:, G_FFN + 8 * q:G_FFN + 8 * q + 8].unsqueeze(2), P, 8, SLOTS),
                                    ALU.mult).then_inc(xsT_ready, 1)

            def add_parts(added, half, last=False):
                for i in range(8 * half, 8 * half + 8):
                    t, n = i // 4, i % 4
                    dve.wait_ge(part_done, added + (i + 1))
                    v.tensor_tensor(X[:, t, n * 512:(n + 1) * 512], ps[:, 6 + i % 2, :], X[:, t, n * 512:(n + 1) * 512],
                                    ALU.add).then_inc(sum_ready if last else part_added, 1)

            def block_dve(b, par, pair):
                if par == 0 and pair is not None:
                    turn_evac(b + 1, 1 - par)
                    add_parts(pair * 16 - 16, 0)
                dve.wait_ge(sil_ready, b + 1)
                v.tensor_tensor(act_t.rearrange("p (f n) -> p f n", n=SLOTS), sil.rearrange("p (f n) -> p f n", n=SLOTS),
                                guT[:, :, SLOTS:2 * SLOTS], ALU.mult).then_inc(act_ready, 1)
                if par == 0 and pair is not None:
                    add_parts(pair * 16 - 16, 1)
                else:
                    turn_evac(b + 1, 1 - par)
                if par == 1:
                    v.tensor_scalar(spread, tramp, tokf[:, ds(b - 1, 1)], gate[:, ds(b - 1, 1)],
                                    ALU.is_equal, ALU.mult).then_inc(spread_ready, 1)
                dve.wait_ge(used, b * 12 + (UE + 12))
                v.tensor_copy(y[par * SLOTS:(par + 1) * SLOTS, 1:4:2, :], ps[SLOTS:2 * SLOTS, 4:6, :]).then_inc(y_dve, 1)

            dve.wait_ge(table_ready, 1)
            dve.wait_ge(tramp_ready, 1)
            turn_evac(0, 0)
            block_dve(0, 0, None)
            block_dve(1, 1, None)
            with dve.Fori(1, NE // 2) as it:
                b = it * 2
                block_dve(b, 0, it)
                block_dve(b + 1, 1, it)
            more = dve.value_load(meta[0:1, NOVER:NOVER + 1], min_val=0, max_val=NOVER)
            with dve.If(more > 0):
                with dve.Fori(NE // 2, NBLK // 2) as it:
                    b = it * 2
                    block_dve(b, 0, it)
                    block_dve(b + 1, 1, it)
                for half in range(2):
                    add_parts(8 * NBLK - 16, half, last=True)
            with dve.If(more < 1):
                for half in range(2):
                    add_parts(8 * NE - 16, half, last=True)

        @block.tensor
        def _(pe):
            mm, turn = nc.tensor.matmul, nc.tensor.transpose

            pe.wait_ge(consts, 6)
            pe.wait_ge(gain_in, 16 * 11)
            turn(ps[:, 7, 0:NGR], PB[0:NGR, 8192:8192 + P], ident[0:NGR, 0:NGR]).then_inc(gain_turned, 1)

            def norm_tile(T, src):
                pe.wait_ge(diag_ready, T + 1)
                for b in range(4):
                    if T > 0:
                        pe.wait_ge(hT_ready, T * 4 + (b - 3))
                    for k in range(4 * b, 4 * b + 4):
                        ins = mm(ps[:, b, (k % 4) * P:(k % 4 + 1) * P], src[:, k * P:(k + 1) * P], dg[:, T % 2, :],
                                 start=True, stop=True, skip_group_check=True)
                    ins.then_inc(h_turned, 1)

            norm_tile(0, memx[:, 0, :])
            norm_tile(1, memx[:, 1, :])
            pe.wait_ge(hT_ready, 8)
            for c in range(4):
                n = c
                chunk_landed(pe, n)
                w = chunk(n, XW)
                for kk in range(4):
                    k = 4 * c + kk
                    for f in range(XH):
                        ins = mm(ps[:, 4 + f // 2, (f % 2) * NM:(f % 2 + 1) * NM], w[:, kk, f * P:(f + 1) * P],
                                 memT[:, k, :], start=(k == 0 and f % 2 == 0), stop=(k == KD - 1),
                                 skip_group_check=True)
                ins.then_inc(used, 1)
            for c in range(4):
                n = 4 + c
                chunk_landed(pe, n)
                if c == 0:
                    pe.wait_ge(gains, 1)
                w = chunk(n, XW)
                for kk in range(4):
                    k = 4 * c + kk
                    for m in range(2):
                        ins = mm(ps[:, 6 + m, :], memT[:, k, m * P:(m + 1) * P], w[:, kk, :],
                                 start=(k == 0), stop=(k == KD - 1))
                ins.then_inc(used, 1)
                if c == 0:
                    pe.wait_ge(xk_sq, 2)
                    for b in range(2):
                        mm(ps[:, b, :], ones[:, :], sqm[:, b * 512:(b + 1) * 512], start=True, stop=True
                           ).then_inc(xk_ss, 1)
            pe.wait_ge(xk_root, 2)
            for t in range(NT):
                norm_tile(2 + t, X[:, t, :])
            pe.wait_ge(h_hi_ready, 16)
            pe.wait_ge(h_lo_ready, 16)
            pe.wait_ge(kx_ready, 2)
            pe.wait_ge(vx_ready, 2)

            def col_tile(n, bank, between=None):
                for half in range(2):
                    pe.wait_ge(w_hi_ready, n * 2 + (half + 1))
                    pe.wait_ge(w_lo_ready, n * 2 + (half + 1))
                    for kk in range(KD // 2):
                        k = half * (KD // 2) + kk
                        high_k = mix_hi[:, k, :].rearrange("p (t n) -> p t n", n=P)
                        for part, (w_, h_) in enumerate(((in_hi, high_k), (in_hi, h_lo[:, :, k, :]), (in_lo, high_k))):
                            ins = mm(ps[:, bank, :].rearrange("p (t n) -> p t n", n=P), w_[:, half, kk, :], h_, start=(k == 0 and part == 0),
                                     stop=(k == KD - 1 and part == 2))
                            if half == 1 and kk == 0 and part == 0:
                                ins.then_inc(used, 1)
                        if k == 3 and between is not None:
                            between()
                    ins.then_inc(halves_used, 1)

            def head_sums(n, bank, b):
                pe.wait_ge(q_sq, n + 1)
                mm(ps[:, bank, :], blk[:, :], sq[:, b, :], start=True, stop=True).then_inc(q_ss, 1)

            col_tile(0, 7)
            with pe.Fori(0, 2) as it:
                n = it * 4
                for s in range(4):
                    if s >= 2:
                        pe.wait_ge(q_ready, n + 1)
                    col_tile(n + (s + 1), 4 + s)
                    head_sums(n + s, (s - 1) % 4, s % 2)
                pe.wait_ge(q_ready, n + 3)
            col_tile(9, 5, lambda: head_sums(8, 3, 0))
            pe.wait_ge(q_ready, 9)
            pe.wait_ge(k_padded, 2)
            pe.wait_ge(k_ready, 2)

            for i in range(8):
                t, g = i // 2, i % 2
                for m in (0, 4, 1, 5, 2, 6, 3, 7):
                    hp = slice(m // 4 * HD, (m // 4 + 1) * HD)
                    for at, n, col in WINDOW[m % 2]:
                        ins = mm(ps[:, m // 2, (m % 2) * WIN + at:(m % 2) * WIN + at + n],
                                 proj[hp, 4 * g + m % 4, t * P:(t + 1) * P],
                                 kdup[hp, g, t * P + col:t * P + col + n], start=True, stop=True,
                                 skip_group_check=True)
                    if m % 2 == 1:
                        ins.then_inc(scores_done, 1)
                if i == 0:
                    pe.wait_ge(v_copied, 1)
                    for tt in range(NT):
                        ins = turn(ps[:, 6, tt * P:(tt + 1) * P], vTp[:, tt * P:(tt + 1) * P], ident[:, :])
                    ins.then_inc(v_turned, 1)
                    for tt in range(NT):
                        ins = turn(ps[0:CHUNK, 7, tt * P:(tt + 1) * P], vTp[:, tt * P + P:tt * P + P + CHUNK], ident[:, :])
                    ins.then_inc(v_turned, 1)
                if i > 0:
                    pe.wait_ge(u_ready, i)
                col_tile(10 + i, 4)
                pe.wait_ge(exp_done, 9 * i + 9)
                for j in range(4):
                    for n in range(3):
                        ins = turn(ps[:, j, n * P:(n + 1) * P], Spair[:, j, n * P:(n + 1) * P], ident[:, :])
                    ins.then_inc(pt_turned, 1)
                if i == 0:
                    pe.wait_ge(v_ready, 3)
                for j in range(4):
                    pe.wait_ge(pt_dve if j % 2 == 0 else pt_act, 2 * i + j // 2 + 1)
                    if j == 0 and i > 0:
                        pe.wait_ge(a_ready, i)
                    for e in range(2):
                        o = ps[:, 5, (2 * j + e) * HD:(2 * j + e + 1) * HD]
                        mm(o, PT[:, j, 2 * e * P:(2 * e + 1) * P], vA[:, t, g * HD:(g + 1) * HD],
                           start=True, stop=False, skip_group_check=True)
                        ins = mm(o, PT[:, j, P:2 * P], vB[:, e, t, g * HD:(g + 1) * HD],
                                 start=False, stop=True, skip_group_check=True)
                ins.then_inc(pv_done, 1)
            pe.wait_ge(a_ready, 8)
            for t in range(NT):
                if t >= 2:
                    pe.wait_ge(whole_ready, 2 * t - 2)
                for b in range(2):
                    for k in range(4 * b, 4 * b + 4):
                        ins = turn(ps[:, 2 * (t % 2) + b, (k % 4) * P:(k % 4 + 1) * P],
                                   a_rows[:, t, k * P:(k + 1) * P], ident[:, :])
                    ins.then_inc(a_turned, 1)
            chunk_landed(pe, SEQ_POOL)
            pe.wait_ge(u_ready, 8)
            w = chunk(SEQ_POOL, 256)
            for m in range(8):
                g = m // 2
                if m % 2 == 0:
                    pe.wait_ge(d_ready, 2 * g + 2)
                if m >= 4:
                    pe.wait_ge(whole_ready, 8 + m - 3)
                for kk in range(2):
                    ins = mm(ps[:, 4 + m % 4, :], w[:, 2 * g + kk, (m % 2) * P:(m % 2 + 1) * P],
                             proj[:, 10 + 2 * g + kk, :], start=(kk == 0), stop=(kk == 1))
                ins.then_inc(pool_done if m < 7 else used, 1)

            pe.wait_ge(mix_hi_ready, 16)
            pe.wait_ge(mix_lo_ready, 16)
            with pe.Fori(0, 2) as it:
                n = it * 2
                for par in range(2):
                    if par == 1:
                        pe.wait_ge(x_added, n * 4 + 1)
                    for c in range(4):
                        for half in range(2):
                            done = 8 * par + 2 * c + half + 1
                            pe.wait_ge(w_hi_ready, n * 8 + (HALVES_IN + done))
                            pe.wait_ge(w_lo_ready, n * 8 + (HALVES_IN + done))
                            for t in range(NT):
                                for kk in range(2):
                                    k = 4 * c + 2 * half + kk
                                    for part, (m_, w_) in enumerate(((mix_hi, w_hi), (mix_hi, w_lo), (mix_lo, w_hi))):
                                        ins = mm(ps[:, 4 * par + t, :], m_[:, k, t * P:(t + 1) * P], w_[:, half, kk, :],
                                                 start=(k == 0 and part == 0), stop=(k == KD - 1 and part == 2))
                                        if half == 1 and t == 3 and kk == 0 and part == 0:
                                            ins.then_inc(used, 1)
                                if c == 3 and half == 1 and t < 3:
                                    ins.then_inc(o_done, 1)
                            ins.then_inc(halves_used, 1)
                pe.wait_ge(x_added, n * 4 + 4)
            for t in range(NT):
                norm_tile(6 + t, X[:, t, :])
            for f in range(XH):
                for c in range(4):
                    if f == 0:
                        chunk_landed(pe, SEQ_XQ + c)
                        pe.wait_ge(hT_ready, 36 + c + 1)
                    w = chunk(SEQ_XQ + c, XW)
                    for kk in range(4):
                        k = 4 * c + kk
                        ins = mm(ps[:, 4 + f, :], w[:, kk, f * P:(f + 1) * P], H[:, k, :],
                                 start=(k == 0), stop=(k == KD - 1))
                    if c == 0 and f > 0:
                        pe.wait_ge(xq_sq, f)
                        mm(ps[:, f - 1, :], ones[:, :], sqx[:, (f - 1) % 2, :], start=True, stop=True).then_inc(xq_ss, 1)
                    if f == XH - 1:
                        ins.then_inc(used, 1)
                if f < XH - 1:
                    ins.then_inc(xq_done, 1)
            pe.wait_ge(xq_sq, XH)
            mm(ps[:, XH - 1, :], ones[:, :], sqx[:, (XH - 1) % 2, :], start=True, stop=True).then_inc(xq_ss, 1)

            def xscores(t):
                if t >= 2:
                    pe.wait_ge(xexp_done, 4 * t - 4)
                for h in range(XH):
                    ins = mm(ps[:, 5 * (t % 2) + h // 2, (h % 2) * NM:(h % 2 + 1) * NM], qx[:, h, t * P:(t + 1) * P],
                             kx[:, h, :], start=True, stop=True, skip_group_check=True)
                ins.then_inc(xs_done, 1)

            def xturn(t):
                pe.wait_ge(xp_ready, t + 1)
                for n in range(8):
                    if n == 0 and t > 0:
                        pe.wait_ge(xpt_act, t)
                    if n == 4 and t > 0:
                        pe.wait_ge(xpt_dve, t)
                    ins = turn(ps[:, 2 + n // 4, (n % 4) * P:(n % 4 + 1) * P],
                               SX[:, t % 2, n * P:(n + 1) * P], ident[:, :])
                    if n % 4 == 3:
                        ins.then_inc(xp_turned, 1)

            def xvalues(t):
                pe.wait_ge(xpt_act, t + 1)
                pe.wait_ge(xpt_dve, t + 1)
                if t >= 2:
                    pe.wait_ge(oT_ready, t - 1)
                for h in range(XH):
                    for m in range(2):
                        ins = mm(ps[:, 4 + 3 * (t % 2), h * P:(h + 1) * P], vx[:, m, h * P:(h + 1) * P],
                                 PTX[:, (2 * h + m) * P:(2 * h + m + 1) * P], start=(m == 0), stop=(m == 1),
                                 skip_group_check=True)
                ins.then_inc(xo_part, 1)

            pe.wait_ge(qx_ready, XH)
            xscores(0)
            xscores(1)
            for t in range(NT):
                xturn(t)
                xvalues(t)
                if t + 2 < NT:
                    xscores(t + 2)
            pe.wait_ge(oT_ready, NT)
            for c in range(4):
                chunk_landed(pe, SEQ_XO + c)
            with pe.Fori(0, 2) as it:
                n = it * 2
                for par in range(2):
                    if par == 1:
                        pe.wait_ge(x_added, n * 4 + 16)
                    for t in range(NT):
                        for c in range(4):
                            ins = mm(ps[:, 4 * par + t, :], H[:, c, t * P:(t + 1) * P],
                                     slot(early[SEQ_XO + c][0])[:, ds(n * 512 + par * 512, 512)],
                                     start=(c == 0), stop=(c == 3))
                        ins.then_inc(o_done, 1)
                pe.wait_ge(x_added, n * 4 + 20)
            def logits(t):
                pe.wait_ge(hT_ready, 40 + 4 * t + 4)
                for k in range(KD):
                    ins = mm(ps[:, 4, t * NCOL:(t + 1) * NCOL], H[:, k, t * P:(t + 1) * P], wr[:, k, :],
                             start=(k == 0), stop=(k == KD - 1), skip_group_check=True)
                return ins

            for t in range(NT):
                norm_tile(10 + t, X[:, t, :])
                if t == 0:
                    pe.wait_ge(router_in, 16 * (NG + 1))
                    pe.wait_ge(x_added, 32)
                else:
                    logits(t - 1)
            logits(NT - 1).then_inc(logits_done, 1)
            pe.wait_ge(tri_ready, 1)
            pe.wait_ge(picks, 1)
            for t in range(NT + 1):
                for s in range(min(t + 1, NT)):
                    ins = mm(ps[:, 5, t * NE:(t + 1) * NE], tri if s == t else ones[:, :], rq["M"][:, s, :],
                             start=(s == 0), stop=(s == min(t, NT - 1)), skip_group_check=True)
            ins.then_inc(ranks, 1)
            pe.wait_ge(onehots, 6)
            for n in range(2 * NT):
                k, t = n // NT, n % NT
                ins = mm(ps[0:SLOTS, 6, 0:2 * TCOL], rq["P1" if k == 0 else "P2"][:, t, :],
                         rq["B1" if k == 0 else "B2"][:, t, :], start=(n == 0), stop=(n == 2 * NT - 1))
            ins.then_inc(table_done, 1)

            xs = hs

            def turn_rows(b, par):
                if isinstance(b, int):
                    pe.wait_ge(gathered[par], b * 8 + (16 - 8 * par))
                    wait_past(pe, xsT_ready, b * 2)
                else:
                    rows, copied = pe.to_reg(b * 8 + (16 - 8 * par)), pe.to_reg(b * 2)
                    pe.wait_ge(table_ready, 1)
                    pe.wait_ge(gathered[par], rows)
                    pe.wait_ge(xsT_ready, copied)
                for q in range(2):
                    for k in range(8 * q, 8 * q + 8):
                        ins = turn(ps[:, 2 + q, (k % 8) * SLOTS:(k % 8 + 1) * SLOTS],
                                   xs[0:SLOTS, par, k * P:(k + 1) * P], ident[0:SLOTS, 0:SLOTS])
                    ins.then_inc(xs_turned, 1)

            def expert_landed(b, j):
                s = expert_slot(j)
                pe.wait_ge(landed[s], b * 16 + 16 * (early_loads[s] + 1))

            def spread_parts(before, half, last=False):
                for i in range(8 * half, 8 * half + 8):
                    t, n = i // 4, i % 4
                    if i >= 2:
                        if last:
                            pe.wait_ge(sum_ready, i - 1)
                        else:
                            pe.wait_ge(part_added, before + (i - 1))
                    mm(ps[:, 6 + i % 2, :], spread[:, t * P:(t + 1) * P], y[:, n, :],
                       start=True, stop=True).then_inc(part_done, 1)

            def last_pair(blocks):
                pe.wait_ge(y_act, blocks)
                pe.wait_ge(y_dve, blocks)
                pe.wait_ge(spread_ready, blocks // 2)
                for half in range(2):
                    spread_parts(0, half, last=True)

            def block_pe(b, par, pair):
                pe.wait_ge(xsT_ready, b * 2 + 2)
                wait_past(pe, gu_copied, b)
                for c in range(4):
                    for kk in range(4):
                        k = 4 * c + kk
                        for side in range(2):
                            j = 2 * c + side
                            if kk == 0:
                                expert_landed(b, j)
                            w = slot(expert_slot(j)).rearrange("p (k n) -> p k n", n=FF)
                            ins = mm(ps[side * SLOTS:(side + 1) * SLOTS, 0, :], xsT[:, par, k, :], w[:, kk, :],
                                     start=(k == 0), stop=(k == KD - 1), skip_group_check=True)
                            if kk == 3:
                                ins.then_inc(used, 1)
                turn_rows(b + 1, 1 - par)
                behind = par == 0 and pair is not None
                if behind:
                    pe.wait_ge(y_act, b)
                    pe.wait_ge(y_dve, b)
                    pe.wait_ge(spread_ready, pair)
                    spread_parts(pair * 16 - 16, 0)
                pe.wait_ge(gu_copied, b + 1)
                for f in range(KF):
                    ins = turn(guT[:, f, :], gu[:, f * P:(f + 1) * P], ident[:, :])
                ins.then_inc(gu_turned, 1)
                if behind:
                    spread_parts(pair * 16 - 16, 1)
                if par == 1 and pair is not None:
                    pe.wait_ge(part_added, pair * 16)
                pe.wait_ge(act_ready, b + 1)
                wait_past(pe, y_act, b)
                wait_past(pe, y_dve, b)
                for f in range(KF):
                    expert_landed(b, 8 + f)
                    w = slot(expert_slot(8 + f))
                    for n in range(4):
                        half = slice(n % 2 * SLOTS, (n % 2 + 1) * SLOTS)
                        ins = mm(ps[half, 4 + n // 2, :], act_t[:, f * SLOTS:(f + 1) * SLOTS],
                                 w[:, n * 512:(n + 1) * 512], start=(f == 0), stop=(f == KF - 1), skip_group_check=True)
                    ins.then_inc(used, 1)

            turn_rows(0, 0)
            block_pe(0, 0, None)
            block_pe(1, 1, None)
            with pe.Fori(1, NE // 2) as it:
                b = it * 2
                block_pe(b, 0, it)
                block_pe(b + 1, 1, it)
            more = pe.value_load(meta[0:1, NOVER:NOVER + 1], min_val=0, max_val=NOVER)
            with pe.If(more > 0):
                with pe.Fori(NE // 2, NBLK // 2) as it:
                    b = it * 2
                    block_pe(b, 0, it)
                    block_pe(b + 1, 1, it)
                last_pair(NBLK)
            with pe.If(more < 1):
                last_pair(NE)


_INS = ['x', 'mem', 'mix_norm_g', 'w_in', 'q_norm_g', 'k_norm_g', 'sink_logits', 'pool_w', 'pool_scale', 'w_out',
        'xattn_norm_g', 'mem_norm_g', 'xq_w', 'xkv_w', 'xq_norm_g', 'xk_norm_g', 'xo_w', 'ffn_norm_g',
        'router_group_w', 'router_group_b', 'router_expert_w', 'router_expert_b', 'expert_w_gate',
        'expert_w_up', 'expert_w_down']
_OUTS = [((1, S, D), 'float32')]


def kernel(**inputs):
    import numpy as _np
    import concourse.bacc as _bacc
    from concourse import mybir as _mybir
    from concourse.bass_utils import run_bass_kernel_spmd as _run

    nc = _bacc.Bacc("TRN2", target_bir_lowering=False, num_devices=1)
    arrays, args = {}, []
    for name in _INS:
        a = _np.ascontiguousarray(inputs[name])
        arrays[f"in_{name}_dram"] = a
        args.append(nc.dram_tensor(f"in_{name}_dram", a.shape, _mybir.dt.from_np(a.dtype), kind="ExternalInput").ap())
    for i, (shape, dtype) in enumerate(_OUTS):
        dt = _mybir.dt.from_np(_np.dtype(dtype))
        args.append(nc.dram_tensor(f"out_{i}_dram", shape, dt, kind="ExternalOutput").ap())
    hybrid_block(nc, *args)
    r = _run(nc, [arrays], core_ids=[0])
    got = tuple(r.results[0][f"out_{i}_dram"] for i in range(len(_OUTS)))
    return got[0]
```
